# Optimizing a Trainium2 kernel written in Bass

```python
import jax, jax.numpy as jnp
from jax import lax
import numpy as np

D_MODEL = 1024
BATCH = 1
SEQ = 512
DEPTH = 1

MEM_LEN = 256
EPS = 1e-6

NSA_HEADS = 8
NSA_KV_GROUPS = 2
NSA_HEAD_DIM = 128
CMP_BLOCK = 32
CMP_STRIDE = 16
CMP_HIDDEN = 256
SEL_BLOCK = 64
N_SELECT = 16
WINDOW = 512
Q_BLOCK = 128
ROPE_THETA = 500000.0
ROT_DIM = NSA_HEAD_DIM // 4

RET_HEADS = 4
RET_QK_DIM = 64
RET_V_DIM = 128
RET_CHUNK = 128
RET_THETA = 10000.0

MEM_HEADS = 4
MEM_HEAD_DIM = 128

NSA_WIDTH = NSA_HEADS * NSA_HEAD_DIM
RET_WIDTH = RET_HEADS * RET_V_DIM
MEM_WIDTH = MEM_HEADS * MEM_HEAD_DIM
MIX_WIDTH = NSA_WIDTH + RET_WIDTH + MEM_WIDTH
NSA_KV_WIDTH = NSA_KV_GROUPS * NSA_HEAD_DIM
IN_SPLITS = (NSA_WIDTH, 3 * 2 * NSA_KV_WIDTH, 3 * NSA_HEADS, RET_HEADS * RET_QK_DIM,
             RET_HEADS * RET_QK_DIM, RET_WIDTH, MEM_WIDTH, MIX_WIDTH)
IN_WIDTH = 6168

kernel_name = "hymba_nsa_retention_memory_layer"

def rms_norm(x, g):
    xf = x.astype(jnp.float32)
    y = xf * lax.rsqrt(jnp.mean(xf * xf, axis=-1, keepdims=True) + EPS)
    return (y * g.astype(jnp.float32)).astype(x.dtype)

def rotary(x, pos, rot_dim, theta):
    half = rot_dim // 2
    inv_freq = theta ** (-jnp.arange(half, dtype=jnp.float32) / half)
    ang = pos.astype(jnp.float32)[..., None] * inv_freq
    cos, sin = jnp.cos(ang), jnp.sin(ang)
    x1 = x[..., :half].astype(jnp.float32)
    x2 = x[..., half:rot_dim].astype(jnp.float32)
    out = jnp.concatenate([x1 * cos - x2 * sin, x1 * sin + x2 * cos,
                           x[..., rot_dim:].astype(jnp.float32)], axis=-1)
    return out.astype(x.dtype)

def masked_softmax(s, mask):
    s = jnp.where(mask, s.astype(jnp.float32), -jnp.inf)
    m = jnp.max(s, axis=-1, keepdims=True)
    m = jnp.where(jnp.isfinite(m), m, 0.0)
    p = jnp.exp(s - m)
    return p / jnp.maximum(jnp.sum(p, axis=-1, keepdims=True), 1e-30)

def compress_blocks(k, pos_emb, w1, w2):
    B, G, T, dh = k.shape
    n_cmp = (T - CMP_BLOCK) // CMP_STRIDE + 1
    idx = np.arange(n_cmp)[:, None] * CMP_STRIDE + np.arange(CMP_BLOCK)[None, :]
    blocks = k[:, :, idx] + pos_emb.astype(k.dtype)
    h = jax.nn.gelu(blocks.reshape(B, G, n_cmp, CMP_BLOCK * dh) @ w1)
    return h @ w2

def nsa_heads(q, k_cmp, v_cmp, k_slc, v_slc, k_win, v_win, gates,
              cmp_pos_k, cmp_w1_k, cmp_w2_k, cmp_pos_v, cmp_w1_v, cmp_w2_v):
    B, G, R, T, dh = q.shape
    scale = dh ** -0.5
    t = np.arange(T)

    n_cmp = (T - CMP_BLOCK) // CMP_STRIDE + 1
    cmp_start = np.arange(n_cmp) * CMP_STRIDE
    kc = compress_blocks(k_cmp, cmp_pos_k, cmp_w1_k, cmp_w2_k)
    vc = compress_blocks(v_cmp, cmp_pos_v, cmp_w1_v, cmp_w2_v)
    s = jnp.einsum('bgrtd,bgnd->bgrtn', q, kc) * scale
    p_cmp = masked_softmax(s, (cmp_start + CMP_BLOCK - 1)[None, :] <= t[:, None])
    o_cmp = jnp.einsum('bgrtn,bgnd->bgrtd', p_cmp.astype(vc.dtype), vc)

    n_sb = T // SEL_BLOCK
    sel_start = np.arange(n_sb) * SEL_BLOCK
    overlap = np.clip(np.minimum(cmp_start[:, None] + CMP_BLOCK, sel_start[None, :] + SEL_BLOCK)
                      - np.maximum(cmp_start[:, None], sel_start[None, :]), 0, None)
    overlap = jnp.asarray(overlap.astype(np.float32) / CMP_BLOCK)
    imp = jnp.einsum('bgrtn,nj->bgtj', p_cmp, overlap)
    blk = np.arange(n_sb)[None, :]
    cur = (t // SEL_BLOCK)[:, None]
    forced = (blk == 0) | (blk == cur) | (blk == cur - 1)
    valid = blk * SEL_BLOCK <= t[:, None]
    imp = jnp.where(forced, jnp.inf, jnp.where(valid, imp, -jnp.inf))
    n_sel = min(N_SELECT, n_sb)
    _, sel_idx = lax.top_k(imp, n_sel)

    kb_slc = k_slc.reshape(B, G, n_sb, SEL_BLOCK, dh)
    vb_slc = v_slc.reshape(B, G, n_sb, SEL_BLOCK, dh)
    k_win_pad = jnp.pad(k_win, ((0, 0), (0, 0), (WINDOW, 0), (0, 0)))
    v_win_pad = jnp.pad(v_win, ((0, 0), (0, 0), (WINDOW, 0), (0, 0)))
    nqb = T // Q_BLOCK
    gather = jax.vmap(lambda kg, ig: kg[ig])

    def one_block(item):
        b = item // nqb
        t0 = (item % nqb) * Q_BLOCK
        qb = lax.dynamic_slice_in_dim(q[b], t0, Q_BLOCK, axis=2)
        tq = t0 + jnp.arange(Q_BLOCK)
        idx = lax.dynamic_slice_in_dim(sel_idx[b], t0, Q_BLOCK, axis=1)
        ks = gather(kb_slc[b], idx).reshape(G, Q_BLOCK, n_sel * SEL_BLOCK, dh)
        vs = gather(vb_slc[b], idx).reshape(G, Q_BLOCK, n_sel * SEL_BLOCK, dh)
        kpos = (idx[..., None] * SEL_BLOCK + jnp.arange(SEL_BLOCK)).reshape(G, Q_BLOCK, -1)
        s_sl = jnp.einsum('grqd,gqkd->grqk', qb, ks) * scale
        p_sl = masked_softmax(s_sl, (kpos <= tq[None, :, None])[:, None])
        o_sl = jnp.einsum('grqk,gqkd->grqd', p_sl.astype(vs.dtype), vs)
        kw = lax.dynamic_slice_in_dim(k_win_pad[b], t0, Q_BLOCK + WINDOW, axis=1)
        vw = lax.dynamic_slice_in_dim(v_win_pad[b], t0, Q_BLOCK + WINDOW, axis=1)
        kwpos = t0 - WINDOW + jnp.arange(Q_BLOCK + WINDOW)
        rel = tq[:, None] - kwpos[None, :]
        mask_w = (rel >= 0) & (rel < WINDOW) & (kwpos[None, :] >= 0)
        s_w = jnp.einsum('grqd,gkd->grqk', qb, kw) * scale
        p_w = masked_softmax(s_w, mask_w)
        o_w = jnp.einsum('grqk,gkd->grqd', p_w.astype(vw.dtype), vw)
        return o_sl, o_w

    o_slc, o_win = lax.map(one_block, jnp.arange(B * nqb))

    def unblock(o):
        return o.reshape(B, nqb, G, R, Q_BLOCK, dh).transpose(0, 2, 3, 1, 4, 5).reshape(B, G, R, T, dh)

    o_slc, o_win = unblock(o_slc), unblock(o_win)
    g = gates.reshape(B, T, 3, G, R).transpose(2, 0, 3, 4, 1)[..., None]
    o = g[0] * o_cmp + g[1] * o_slc + g[2] * o_win
    return o.transpose(0, 3, 1, 2, 4).reshape(B, T, G * R * dh)

def retention_heads(q, k, v, pos, gn_gain):
    B, H, T, dk = q.shape
    dv = v.shape[-1]
    q = rotary(q, pos, dk, RET_THETA)
    k = rotary(k, pos, dk, RET_THETA) * (dk ** -0.5)
    log_gamma = jnp.log1p(-(2.0 ** (-5.0 - jnp.arange(H, dtype=jnp.float32))))
    C = RET_CHUNK
    n = jnp.arange(C, dtype=jnp.float32)
    diff = n[:, None] - n[None, :]
    decay = jnp.where(diff >= 0, jnp.exp(log_gamma[:, None, None] * jnp.maximum(diff, 0.0)), 0.0)
    xi = jnp.exp(log_gamma[:, None] * (n + 1.0))[..., None]
    zeta = jnp.exp(log_gamma[:, None] * (C - 1.0 - n))[..., None]
    gamma_c = jnp.exp(log_gamma * C)[:, None, None]
    nc = T // C

    def to_chunks(a):
        return a.reshape(B, H, nc, C, a.shape[-1]).transpose(2, 0, 1, 3, 4)

    def step(state, inp):
        qc, kc, vc = inp
        inner = jnp.einsum('bhnd,bhmd->bhnm', qc, kc) * decay
        out = (jnp.einsum('bhnm,bhme->bhne', inner, vc)
               + jnp.einsum('bhnd,bhde->bhne', qc, state) * xi)
        state = state * gamma_c + jnp.einsum('bhmd,bhme->bhde', kc * zeta, vc)
        return state, out

    state0 = jnp.zeros((B, H, dk, dv), jnp.float32)
    _, o = lax.scan(step, state0, (to_chunks(q), to_chunks(k), to_chunks(v)))
    o = o.transpose(1, 0, 3, 2, 4).reshape(B, T, H, dv).astype(jnp.float32)
    mu = jnp.mean(o, axis=-1, keepdims=True)
    var = jnp.mean(jnp.square(o - mu), axis=-1, keepdims=True)
    o = ((o - mu) * lax.rsqrt(var + EPS)).reshape(B, T, H * dv) * gn_gain.astype(jnp.float32)
    return o.astype(v.dtype)

def memory_heads(qm, mem_n, w_mem_kv):
    B, M, _ = mem_n.shape
    kv = (mem_n @ w_mem_kv).reshape(B, M, 2, MEM_HEADS, MEM_HEAD_DIM)
    km, vm = kv[:, :, 0], kv[:, :, 1]
    s = jnp.einsum('bthd,bmhd->bhtm', qm, km) * (MEM_HEAD_DIM ** -0.5)
    p = jax.nn.softmax(s.astype(jnp.float32), axis=-1)
    o = jnp.einsum('bhtm,bmhd->bthd', p.astype(vm.dtype), vm)
    return o.reshape(B, qm.shape[1], MEM_WIDTH)

def hybrid_layer(x, mem, positions, norm_pre, w_in, cmp_pos_k, cmp_w1_k, cmp_w2_k,
                 cmp_pos_v, cmp_w1_v, cmp_w2_v, ret_gn, mem_norm, w_mem_kv, w_out, norm_post):
    B, T, _ = x.shape
    h = rms_norm(x, norm_pre)
    z = h @ w_in
    q_nsa, kv_nsa, g_nsa, q_ret, k_ret, v_ret, q_mem, gate = jnp.split(
        z, list(np.cumsum(IN_SPLITS)[:-1]), axis=-1)

    R = NSA_HEADS // NSA_KV_GROUPS
    q_nsa = q_nsa.reshape(B, T, NSA_KV_GROUPS, R, NSA_HEAD_DIM).transpose(0, 2, 3, 1, 4)
    q_nsa = rotary(q_nsa, positions[:, None, None, :], ROT_DIM, ROPE_THETA)
    kvn = kv_nsa.reshape(B, T, 3, 2, NSA_KV_GROUPS, NSA_HEAD_DIM).transpose(2, 3, 0, 4, 1, 5)
    kpos = positions[:, None, :]
    k_cmp = rotary(kvn[0, 0], kpos, ROT_DIM, ROPE_THETA)
    k_slc = rotary(kvn[1, 0], kpos, ROT_DIM, ROPE_THETA)
    k_win = rotary(kvn[2, 0], kpos, ROT_DIM, ROPE_THETA)
    gates = jax.nn.sigmoid(g_nsa).reshape(B, T, 3, NSA_HEADS)
    o_nsa = nsa_heads(q_nsa, k_cmp, kvn[0, 1], k_slc, kvn[1, 1], k_win, kvn[2, 1], gates,
                      cmp_pos_k, cmp_w1_k, cmp_w2_k, cmp_pos_v, cmp_w1_v, cmp_w2_v)

    q_ret = q_ret.reshape(B, T, RET_HEADS, RET_QK_DIM).transpose(0, 2, 1, 3)
    k_ret = k_ret.reshape(B, T, RET_HEADS, RET_QK_DIM).transpose(0, 2, 1, 3)
    v_ret = v_ret.reshape(B, T, RET_HEADS, RET_V_DIM).transpose(0, 2, 1, 3)
    o_ret = retention_heads(q_ret, k_ret, v_ret, positions[:, None, :], ret_gn)

    o_mem = memory_heads(q_mem.reshape(B, T, MEM_HEADS, MEM_HEAD_DIM), rms_norm(mem, mem_norm), w_mem_kv)

    mixed = jnp.concatenate([o_nsa, o_ret, o_mem], axis=-1) * jax.nn.silu(gate)
    y = mixed @ w_out
    return x + rms_norm(y, norm_post)

def setup_inputs(seed: int = 0) -> dict:
    key = jax.random.key(seed)
    ks = jax.random.split(key, 20)
    f32 = jnp.float32

    def w(k, shape, fan_in):
        return jax.random.normal(k, shape, f32) * (fan_in ** -0.5)

    def gain(k, shape):
        return 1.0 + 0.05 * jax.random.normal(k, shape, f32)

    x = jax.random.normal(ks[0], (BATCH, SEQ, D_MODEL), f32)
    mem = jax.random.normal(ks[1], (BATCH, MEM_LEN, D_MODEL), f32)
    offsets = jax.random.randint(ks[2], (BATCH, 1), 0, 1024, dtype=jnp.int32)
    positions = (offsets + jnp.arange(SEQ, dtype=jnp.int32)[None, :]).astype(jnp.int32)
    L = DEPTH
    return {
        "x": x,
        "mem": mem,
        "positions": positions,
        "norm_pre": gain(ks[3], (L, D_MODEL)),
        "w_in": w(ks[4], (L, D_MODEL, IN_WIDTH), D_MODEL),
        "cmp_pos_k": 0.1 * jax.random.normal(ks[5], (L, CMP_BLOCK, NSA_HEAD_DIM), f32),
        "cmp_w1_k": w(ks[6], (L, CMP_BLOCK * NSA_HEAD_DIM, CMP_HIDDEN), CMP_BLOCK * NSA_HEAD_DIM),
        "cmp_w2_k": w(ks[7], (L, CMP_HIDDEN, NSA_HEAD_DIM), CMP_HIDDEN),
        "cmp_pos_v": 0.1 * jax.random.normal(ks[8], (L, CMP_BLOCK, NSA_HEAD_DIM), f32),
        "cmp_w1_v": w(ks[9], (L, CMP_BLOCK * NSA_HEAD_DIM, CMP_HIDDEN), CMP_BLOCK * NSA_HEAD_DIM),
        "cmp_w2_v": w(ks[10], (L, CMP_HIDDEN, NSA_HEAD_DIM), CMP_HIDDEN),
        "ret_gn": gain(ks[11], (L, RET_WIDTH)),
        "mem_norm": gain(ks[12], (L, D_MODEL)),
        "w_mem_kv": w(ks[13], (L, D_MODEL, 2 * MEM_WIDTH), D_MODEL),
        "w_out": w(ks[14], (L, MIX_WIDTH, D_MODEL), MIX_WIDTH),
        "norm_post": gain(ks[15], (L, D_MODEL)),
    }

def reference(x, mem, positions, norm_pre, w_in, cmp_pos_k, cmp_w1_k, cmp_w2_k,
              cmp_pos_v, cmp_w1_v, cmp_w2_v, ret_gn, mem_norm, w_mem_kv, w_out, norm_post):
    for layer in range(DEPTH):
        x = hybrid_layer(x, mem, positions, norm_pre[layer], w_in[layer],
                         cmp_pos_k[layer], cmp_w1_k[layer], cmp_w2_k[layer],
                         cmp_pos_v[layer], cmp_w1_v[layer], cmp_w2_v[layer],
                         ret_gn[layer], mem_norm[layer], w_mem_kv[layer],
                         w_out[layer], norm_post[layer])
    return x


_drawn_inputs = setup_inputs


def setup_inputs(seed=0):
    import zlib

    import numpy as np

    out = dict(_drawn_inputs(seed))
    spreads = {}
    factors = {'cmp_pos_k': 64.0,
     'mem_norm': 8.0,
     'cmp_w1_k': 6.692,
     'cmp_w2_k': 6.772,
     'cmp_pos_v': 8.0,
     'cmp_w1_v': 2.682,
     'ret_gn': 8.0}
    for name, (base, spread) in spreads.items():
        noise = np.random.default_rng([zlib.crc32(name.encode()), seed]).standard_normal(out[name].shape)
        drawn = base * np.exp(spread * noise) if base else spread * noise
        out[name] = __import__('jax').numpy.asarray(drawn.astype(out[name].dtype))
    for name, factor in factors.items():
        out[name] = (out[name] * factor).astype(out[name].dtype)
    return out
```

```python
import math
from contextlib import ExitStack

import numpy as np
import concourse.bass as bass
from concourse import mybir

F32 = mybir.dt.float32
F32R = mybir.dt.float32r
I32 = mybir.dt.int32
ACT = mybir.ActivationFunctionType
ALU = mybir.AluOpType
AX = mybir.AxisListType

P = 128
D = 1024
T = 512
MEM = 256
EPS = 1e-6
DH = 128
GROUPS, PER_GROUP = 2, 4
HEADS = GROUPS * PER_GROUP
RET_HEADS, RET_QK, RET_V = 4, 64, 128
MEM_HEADS = 4
CMP_BLOCK, CMP_STRIDE, CMP_HIDDEN = 32, 16, 256
N_CMP = (T - CMP_BLOCK) // CMP_STRIDE + 1
CMP_COLS = 32
ROT_DIM = DH // 4
NSA_THETA, RET_THETA = 500000.0, 10000.0
SCALE = DH ** -0.5
NEG = -1e30
KT = D // P
TT = T // P
MT = MEM // P
MIX_TILES = HEADS + RET_HEADS + MEM_HEADS
NSA0, RET0, MEM0 = 0, HEADS, HEADS + RET_HEADS
VP = 4
VC = 256
GC = 3 * HEADS // VP
VW = VC + GC
SLAB = 4 * VW
RING = 3
LEAD = 2
KEYS = CMP_COLS + 2 * T
W1_C = 4
BLK_N = GROUPS * N_CMP
BLK_W = CMP_BLOCK * BLK_N + (P - BLK_N)
OUT_ORDER = [*range(RET0, MIX_TILES), *range(NSA0, RET0)]

C_Q, C_KV, C_G = 0, HEADS * DH, HEADS * DH + 6 * GROUPS * DH
C_RQ = C_G + 3 * HEADS
C_RK = C_RQ + RET_HEADS * RET_QK
C_RV = C_RK + RET_HEADS * RET_QK
C_MQ = C_RV + RET_HEADS * RET_V
C_GATE = C_MQ + MEM_HEADS * DH


def kv_col(branch, kv, group):
    return C_KV + ((branch * 2 + kv) * GROUPS + group) * DH


S_GPRE, S_GMEM, S_GN = 0, KT, 2 * KT
S_FREQ = S_GN + RET_HEADS
S_POS = S_FREQ + 4
S_W2 = S_POS + 2 * CMP_BLOCK
S_COLS = S_W2 + 2 * 2 * DH


def schedule():
    s = [("norm", "mem", 0)]
    s += [("slab", "memk", h) for h in range(MEM_HEADS)]
    s += [("slab", "memv", v) for v in range(4)]
    s += [("norm", "x", 0)]
    s += [("tables", "rot", 0)]
    s += [("slab", "v", v) for v in range(2 * VP)]
    s += [("slab", "memq", h) for h in range(MEM_HEADS)]
    proj = [("retq", 0), ("retq", 1), ("retk", 0), ("retk", 1), ("kc", 0), ("kc", 1), ("vc", 0), ("vc", 1)]
    for u, (kind, n) in enumerate(proj):
        s += [("mem", "att", u), ("slab", kind, n)]
    s += [("mem", "flush", 0), ("rot", "flush", 0)]
    for h, (kind, n) in enumerate([("ks", 0), ("ks", 1), ("kw", 0), ("kw", 1)]):
        s += [("ret", "scores", h), ("slab", kind, n), ("ret", "values", h)]
        if h:
            s += [("ret", "turn", h - 1)]
    s += [("blocks", "k", 0), ("slab", "gate", MEM0), ("ret", "turn", RET_HEADS - 1)]
    s += [("slab", "w1k", n) for n in range(4)] + [("slab", "gate", MEM0 + 1)] + [("slab", "w1k", n) for n in range(4, 8)]
    s += [("blocks", "v", 0), ("slab", "gate", MEM0 + 2), ("mlp", "k", 0)]
    s += [("slab", "w1v", n) for n in range(4)] + [("slab", "gate", MEM0 + 3)] + [("slab", "w1v", n) for n in range(4, 8)]
    s += [("slab", "q", 0), ("mlp", "v", 0)] + [("slab", "q", h) for h in range(1, PER_GROUP)] + [("rot", "flush", 0)]
    fill = [("q", h) for h in range(PER_GROUP, HEADS)] + [("gate", RET0 + h) for h in range(RET_HEADS)]
    fill += [("gate", NSA0 + h) for h in range(PER_GROUP)]
    for p in range(GROUPS * TT * 2):
        s += [("pair", "att", p)]
        if fill:
            s += [("slab", *fill.pop(0))]
        if p == PER_GROUP:
            s += [("rot", "flush", 0)]
    s += [("pair", "flush", 0)]
    s += [("slab", "gate", NSA0 + h) for h in range(PER_GROUP, HEADS)]
    s += [("slab", "out", n) for n in range(MIX_TILES)]
    return s


SCHEDULE = schedule()
SLABS = [(kind, n) for what, kind, n in SCHEDULE if what == "slab"]
PAIRS = GROUPS * TT * 2


def pair_of(p):
    return p // (2 * TT), p // 2 % TT, 2 * (p % 2)


def count_uses():
    t = o = 0
    t_used, o_used = {}, {}
    for what, kind, n in SCHEDULE:
        if what == "norm":
            t += KT
        elif what == "mem":
            if kind == "flush" or n:
                t, o = t + 1, o + 1
        elif what == "ret":
            t += {"scores": TT, "values": 0, "turn": 1}[kind]
            o += kind == "values"
        elif what == "mlp":
            t += 2
        elif what == "slab" and kind in ("w1k", "w1v") and n == 0:
            o += 1
        elif what == "pair" and (kind == "flush" or n):
            p = PAIRS - 1 if kind == "flush" else n - 1
            t, o = t + pair_of(p)[1] + 2, o + 1
        t_used[what, kind, n], o_used[what, kind, n] = t, o
    return t_used, o_used


T_USED, O_USED = count_uses()
PJ_KINDS = ("memk", "memq", "retq", "retk", "kc", "vc", "ks", "kw", "q", "gate")


def slab_words(kind):
    return SLAB if kind == "v" else D


def build(nc, x, mem, positions, small, gpost, w_proj, w_val, w_mem, w_cmp, w_out, out):
    ctx = ExitStack()
    with ctx:
        at = [16512]

        def sb(name, shape, dt=F32, offset=None):
            size = 4 * int(np.prod(shape[1:]))
            if offset is None:
                offset = at[0]
                at[0] += (size + 31) // 32 * 32
            return nc.alloc_sbuf_tensor_at(name, shape, dt, offset=offset)

        def sem(name):
            return ctx.enter_context(nc.semaphore(name))

        h_hi, h_lo = (sb(f"h_{p}", [P, KT, T], F32R) for p in ("hi", "lo"))
        slab_raw = [sb(f"slab_raw{i}", [P, SLAB]) for i in range(RING)]
        slab_hi = [sb(f"slab_hi{i}", [P, SLAB], F32R) for i in range(RING)]
        slab_lo = [sb(f"slab_lo{i}", [P, SLAB], F32R) for i in range(RING)]
        mixed_at = at[0]
        mixed = sb("mixed", [P, MIX_TILES, T])
        keys_at = at[0]
        keys_hi, keys_lo = (sb(f"keys_{p}", [P, GROUPS, KEYS], F32R) for p in ("hi", "lo"))
        v_hi, v_lo = (sb(f"v_{p}", [P, TT, 2 * VC], F32R) for p in ("hi", "lo"))
        vc_hi, vc_lo = (sb(f"vc_{p}", [P, GROUPS, DH], F32R) for p in ("hi", "lo"))
        par = sb("par", [P, S_COLS])
        ident = sb("ident", [P, P])
        masks = sb("masks", [P, TT * CMP_COLS + 2 * P])
        gates = sb("gates", [P, TT, 3 * HEADS])
        gate_t = sb("gate_t", [P, TT, GC])
        nsa_rot = sb("nsa_rot", [P, 2, T])
        sumsq = sb("sumsq", [P, 16])
        meansq = sb("meansq", [P, 16])
        rstd = sb("rstd", [P, 16])
        power = sb("power", [P, 4])
        smax = sb("smax", [P, 2, 4])
        nbias = sb("nbias", [P, 2, 4])
        ssum = sb("ssum", [P, 2, 4])
        coef = sb("coef", [P, 2, 4])
        bn = sb("bn", [P, TT, 6])
        mv = sb("mv", [P, TT, 2])
        swp = sb("swp", [32, T])
        region = at[0]

        q_at = region
        p_at = q_at + 2 * HEADS * T * 4
        pt_at = p_at + 2 * 2 * KEYS * 4
        z_at = pt_at + 4 * T * 4
        assert z_at + 2 * T * 4 <= 229344, z_at + 2 * T * 4
        q_hi = sb("q_hi", [P, HEADS, T], F32R, q_at)
        q_lo = sb("q_lo", [P, HEADS, T], F32R, q_at + HEADS * T * 4)
        prob = [sb(f"prob{i}", [P, 2, KEYS], F32, p_at + i * 2 * KEYS * 4) for i in range(2)]
        pt_hi = [sb(f"pt_hi{i}", [P, T], F32R, pt_at + i * T * 4) for i in range(2)]
        pt_lo = [sb(f"pt_lo{i}", [P, T], F32R, pt_at + (2 + i) * T * 4) for i in range(2)]
        z = [sb(f"z{i}", [P, T], F32, z_at + i * T * 4) for i in range(2)]
        x_nat = sb("x_nat", [P, TT, D], F32, mixed_at)
        mem_nat = sb("mem_nat", [P, MT, D], F32, mixed_at + TT * D * 4)
        square = sb("square", [P, D], F32, mixed_at + (TT + MT) * D * 4)
        posi = sb("posi", [P, T], I32, mixed_at + (TT + MT + 1) * D * 4)
        posf = sb("posf", [P, T], F32, mixed_at + (TT + MT + 1) * D * 4 + T * 4)
        ang = sb("ang", [P, 4, T], F32, mixed_at)
        turns = sb("turns", [P, 4, T], F32, mixed_at + 4 * T * 4)
        m_hi = sb("m_hi", [P, KT, MEM], F32R, q_at)
        m_lo = sb("m_lo", [P, KT, MEM], F32R, q_at + KT * MEM * 4)
        mq_hi = sb("mq_hi", [P, MEM_HEADS, T], F32R, q_at + 16384)
        mq_lo = sb("mq_lo", [P, MEM_HEADS, T], F32R, q_at + 24576)
        mk_hi = sb("mk_hi", [P, MEM_HEADS, MEM], F32R, keys_at)
        mk_lo = sb("mk_lo", [P, MEM_HEADS, MEM], F32R, keys_at + 4096)
        mv_hi = sb("mv_hi", [P, MT, T], F32R, keys_at + 8192)
        mv_lo = sb("mv_lo", [P, MT, T], F32R, keys_at + 12288)
        mprob = [sb(f"mprob{i}", [P, 2, MEM], F32, p_at + i * 2048) for i in range(2)]
        decay = sb("decay", [P, RET_HEADS, T], F32, mixed_at)
        decay_i = sb("decay_i", [P, T], I32, mixed_at + 16384)
        ret_v = sb("ret_v", [P, TT, RET_HEADS * RET_V], F32, mixed_at + 8192)
        ret_q = sb("ret_q", [P, RET_HEADS, T], F32, q_at)
        ret_k = sb("ret_k", [P, 2, T], F32, q_at + 8192)
        ret_rot = sb("ret_rot", [P, 2, T], F32, q_at + 12288)
        ret_z = sb("ret_z", [P, T], F32, p_at + 12288)
        inner = [sb(f"inner{i}", [P, 1280], F32, q_at + 16384 + i * 5120) for i in range(2)]
        ret_n = [sb(f"ret_n{i}", [P, TT, RET_V], F32, q_at + 26624 + i * 2048) for i in range(2)]
        z_cmp = sb("z_cmp", [P, 4, T], F32, p_at + 4096)
        blk = sb("blk", [P, BLK_W], F32, q_at)
        blk_hi = sb("blk_hi", [P, BLK_W], F32R, q_at + 8224)
        blk_lo = sb("blk_lo", [P, BLK_W], F32R, q_at + 16448)
        hid = sb("hid", [P, 4, CMP_HIDDEN], F32, p_at + 12288)
        hid_t = sb("hid_t", [P, 2, BLK_N], F32, q_at + 30720)
        mix_hi = [sb(f"mix_hi{i}", [P, T], F32R, q_at + i * 2048) for i in range(RING)]
        mix_lo = [sb(f"mix_lo{i}", [P, T], F32R, q_at + (RING + i) * 2048) for i in range(RING)]
        gpost_b = sb("gpost_b", [P, D], F32, q_at + 12288)
        x_res = sb("x_res", [P, TT, D], F32, q_at + 16384)
        y_sb = [sb(f"y_sb{i}", [P, D], F32, pt_at + i * D * 4) for i in range(2)]
        y_sq = sb("y_sq", [P, D], F32, z_at)

        ps = ctx.enter_context(nc.psum_tensor("ps", [P, 8, 512], F32))
        S_, O_, PJ_, T_ = 0, 3, 4, 6

        ld_mem, ld_x, ld_par, ld_pos = sem("ld_mem"), sem("ld_x"), sem("ld_par"), sem("ld_pos")
        ld_res, ld_post = sem("ld_res"), sem("ld_post")
        slab_loaded = [sem(f"slab_loaded{i}") for i in range(RING)]
        slab_hi_ready, slab_lo_ready, slab_used = sem("slab_hi_ready"), sem("slab_lo_ready"), sem("slab_used")
        pool_step, act_step, dve_step = sem("pool_step"), sem("act_step"), sem("dve_step")
        consts_ready = sem("consts_ready")
        squares_done = sem("squares_done")
        meansq_ready, rstd_ready = sem("meansq_ready"), sem("rstd_ready")
        normed = sem("normed")
        t_full, t_hi = sem("t_full"), sem("t_hi")
        t_drained = [sem("t_drained0"), sem("t_drained1")]
        pj_hi = sem("pj_hi")
        pj_drained = [sem("pj_drained0"), sem("pj_drained1")]
        memv_hi, memv_drained = sem("memv_hi"), sem("memv_drained")
        val_copied, val_tanh, val_drained = sem("val_copied"), sem("val_tanh"), sem("val_drained")
        angles_ready, rot_ready = sem("angles_ready"), sem("rot_ready")
        decay_iota, decay_exp, decay_ready = sem("decay_iota"), sem("decay_exp"), sem("decay_ready")
        s_full, s_drained, bias_ready, prob_ready = sem("s_full"), sem("s_drained"), sem("bias_ready"), sem("prob_ready")
        pv_done = sem("pv_done")
        ret_full, o_drained = sem("ret_full"), sem("o_drained")
        ret_swapped, ret_sin, ret_ready = sem("ret_swapped"), sem("ret_sin"), sem("ret_ready")
        rot_swapped, rot_turned, rot_hi = sem("rot_swapped"), sem("rot_turned"), sem("rot_hi")
        z_done = sem("z_done")
        ret_var, ret_rstd, ret_normed = sem("ret_var"), sem("ret_rstd"), sem("ret_normed")
        blk_sum, blk_hi_ready, blk_ready = sem("blk_sum"), sem("blk_hi_ready"), sem("blk_ready")
        hid_sq, hid_poly, hid_tanh, hid_ready = sem("hid_sq"), sem("hid_poly"), sem("hid_tanh"), sem("hid_ready")
        gate_tanh = sem("gate_tanh")
        mix_hi_ready, mix_ready = sem("mix_hi_ready"), sem("mix_ready")
        y_full, y_squared, y_meansq, y_rstd, y_ready, y_stored = (
            sem("y_full"), sem("y_squared"), sem("y_meansq"), sem("y_rstd"), sem("y_ready"),
            [sem(f"y_stored{t}") for t in range(TT)])

        block = ctx.enter_context(nc.Block())

        def wait_slab_used(e, kind, n):
            e.wait_ge(slab_used, SLABS.index((kind, n)) + 1)

        def wait_t_drained(e, uses):
            e.wait_ge(t_drained[0], (uses + 1) // 2)
            if uses >= 2:
                e.wait_ge(t_drained[1], uses // 2)

        def wait_pj_all_drained(e, uses):
            e.wait_ge(pj_drained[0], (uses + 1) // 2)
            e.wait_ge(pj_drained[1], uses // 2)

        def gated_by(t):
            return [s for s in SLABS if s[0] == "gate"].index(("gate", t)) + 1

        def wait_head_out(e, t):
            if t >= MEM0:
                step = ("mem", "flush", 0) if t == MIX_TILES - 1 else ("mem", "att", 2 * (t - MEM0) + 2)
                e.wait_ge(o_drained, O_USED[step])
            elif t >= RET0:
                k = T_USED["ret", "turn", t - RET0] - 1
                e.wait_ge(t_drained[k % 2], k // 2 + 1)
            else:
                p = (t // PER_GROUP * TT + TT - 1) * 2 + t % PER_GROUP // 2
                e.wait_ge(o_drained, O_USED[("pair", "att", p + 1) if p + 1 < PAIRS else ("pair", "flush", 0)])

        RET_PROJ = [("retq", 0), ("retq", 1), ("retk", 0), ("retk", 1)]
        Z_ORDER = [s for s in SLABS if s[0] in ("retq", "retk", "ks", "kw", "q", "gate")]
        ROT_ORDER = [s for s in SLABS if s[0] in ("kc", "ks", "kw", "q")]
        HI_ORDER = [s for s in SLABS if s[0] in ("ks", "kw", "q")]
        PJ_ORDER = [s for s in SLABS if s[0] in PJ_KINDS]
        Z_INDEX = {s: i for i, s in enumerate(Z_ORDER)}
        ROT_INDEX = {s: i for i, s in enumerate(ROT_ORDER)}
        HI_INDEX = {s: i for i, s in enumerate(HI_ORDER)}
        SPLIT_ORDER = [s for s in PJ_ORDER if s[0] in ("memk", "memq")]

        def wait_pj_drained(e, kind, n):
            j = PJ_ORDER.index((kind, n))
            e.wait_ge(pj_drained[j % 2], j // 2 + 1)

        def pj_bank(kind, n):
            return PJ_ + PJ_ORDER.index((kind, n)) % 2

        def z_key_dst(t_hi_or_lo, kind, n):
            if kind == "q":
                return (q_hi if t_hi_or_lo == "hi" else q_lo)[:, n, :]
            keys = keys_hi if t_hi_or_lo == "hi" else keys_lo
            v = keys[:, n, CMP_COLS:].rearrange("p (j b k) -> p b j k", b=2, k=P)
            return v[:, 0 if kind == "ks" else 1, :, :]

        def blocks_of(t):
            return t.rearrange("p (j k) -> p j k", k=P)

        @block.sync
        def _(sp):
            src = {}
            for i, s in enumerate([s for s in SLABS if s[0] in ("memq", "retq", "retk", "kc", "vc", "ks", "kw", "q", "gate")]):
                src[s] = w_proj[i]
            for v in range(2 * VP):
                src["v", v] = w_val[v]
            for h in range(MEM_HEADS):
                src["memk", h] = w_mem[h]
                src["memv", h] = w_mem[MEM_HEADS + h]
            for n in range(8):
                src["w1k", n] = w_cmp[n]
                src["w1v", n] = w_cmp[8 + n]
            for n in range(MIX_TILES):
                src["out", n] = w_out[n]
            for n, s in enumerate(SLABS):
                if s == ("out", 0):
                    sp.wait_ge(s_full, 2 * MEM_HEADS + 2 * PAIRS)
                    sp.dma_start(x_res[:, :, :], x.rearrange("(t p) d -> p t d", p=P)).then_inc(ld_res, 16)
                    sp.dma_start(gpost_b[:, :], gpost.partition_broadcast(P)).then_inc(ld_post, 16)
                if n >= RING:
                    sp.wait_ge(slab_lo_ready, n - RING + 1)
                w = slab_words(s[0])
                sp.dma_start(slab_raw[n % RING][:, 0:w], src[s]).then_inc(slab_loaded[n % RING], 16)
            for t in range(TT):
                sp.wait_ge(y_ready, t + 1)
                sp.dma_start(out[t * P:(t + 1) * P, :], y_sb[t % 2][:, :]).then_inc(y_stored[t], 16)
            for t in range(TT):
                sp.wait_ge(y_stored[t], 16)

        @block.gpsimd
        def _(pool):
            count = [0]

            def link(ins):
                count[0] += 1
                ins.then_inc(pool_step, 1)
                pool.wait_ge(pool_step, count[0])

            link(pool.memset(ident[:, :], 0.0))
            pool.affine_select(out=ident[:, :], in_=ident[:, :], compare_op=ALU.not_equal, fill=1.0, base=0,
                               pattern=[[-1, P]], channel_multiplier=1).then_inc(consts_ready, 1)
            pool.memset(power[:, :], -0.5).then_inc(consts_ready, 1)
            
            def power_of(dst, src, ready, n, signal):
                pool.wait_ge(ready, n)
                pool.wait_ge(consts_ready, 2)
                w = src.shape[-1]
                pool.tensor_tensor(dst, src, power[:, 0:w], ALU.pow).then_inc(signal, 1)

            power_of(rstd[:, 0:MT], meansq[:, 0:MT], meansq_ready, 1, rstd_ready)
            power_of(rstd[:, 2:2 + TT], meansq[:, 2:2 + TT], meansq_ready, 2, rstd_ready)
            link(pool.memset(masks[:, :], 0.0))
            cw = TT * CMP_COLS
            for i in range(TT):
                m = masks[:, (TT - 1 - i) * CMP_COLS:(TT - i) * CMP_COLS]
                pool.affine_select(out=m, in_=m, compare_op=ALU.is_ge, fill=NEG, base=i * P - (CMP_BLOCK - 1),
                                   pattern=[[-CMP_STRIDE, CMP_COLS]], channel_multiplier=1).then_inc(consts_ready, 1)
            m = masks[:, cw:]
            pool.affine_select(out=m, in_=m, compare_op=ALU.is_ge, fill=NEG, base=0,
                               pattern=[[0, 2], [-1, P]], channel_multiplier=1).then_inc(consts_ready, 1)
            pool.memset(vc_hi[:, :, :].bitcast(F32), 0.0).then_inc(consts_ready, 1)
            pool.memset(vc_lo[:, :, :].bitcast(F32), 0.0).then_inc(consts_ready, 1)
            pool.wait_ge(rot_ready, 2)
            pool.iota(decay_i[:, :], [[1, T]], base=0, channel_multiplier=-1).then_inc(decay_iota, 1)
            wait_slab_used(pool, "memv", 3)
            pool.memset(ret_q[:, :, :], 0.0).then_inc(decay_ready, 1)
            pool.wait_ge(decay_exp, RET_HEADS)
            for h in range(RET_HEADS):
                pool.affine_select(out=decay[:, h, :], in_=decay[:, h, :], compare_op=ALU.is_ge, fill=0.0, base=0,
                                   pattern=[[1, T]], channel_multiplier=-1).then_inc(decay_ready, 1)
            for what, kind, n in SCHEDULE:
                if what == "slab" and kind in ("retq", "retk"):
                    i = RET_PROJ.index((kind, n))
                    t = z[Z_INDEX[kind, n] % 2]
                    pool.wait_ge(ret_swapped, 4 * (i + 1))
                    pool.wait_ge(rot_ready, 1)
                    pool.tensor_tensor(t[:, :], t[:, :], ret_rot[:, 1, :], ALU.mult).then_inc(ret_sin, 1)
                elif what == "slab" and kind in ("kc", "ks", "kw", "q"):
                    r = ROT_INDEX[kind, n]
                    t = z_cmp[0:32, n, :] if kind == "kc" else z[Z_INDEX[kind, n] % 2][0:32, :]
                    w = swp[:, :]
                    pool.wait_ge(rot_swapped, r + 1)
                    link(pool.tensor_tensor(w, w, nsa_rot[0:32, 1, :], ALU.mult))
                    link(pool.tensor_tensor(t, t, nsa_rot[0:32, 0, :], ALU.mult))
                    pool.tensor_tensor(t, t, w, ALU.add).then_inc(rot_turned, 1)
                elif (what, kind) == ("ret", "values"):
                    power_of(rstd[:, 6:6 + TT], meansq[:, 6:6 + TT], ret_var, n + 1, ret_rstd)
            for t in range(TT):
                power_of(rstd[:, 10 + t:11 + t], meansq[:, 10 + t:11 + t], y_meansq, t + 1, y_rstd)

        @block.scalar
        def _(act):
            count = [0]

            def link(ins):
                count[0] += 1
                ins.then_inc(act_step, 1)
                act.wait_ge(act_step, count[0])

            act.dma_start(mem_nat[:, :, :], mem.rearrange("(t p) d -> p t d", p=P)).then_inc(ld_mem, 16)
            act.dma_start(par[:, :], small).then_inc(ld_par, 16)
            act.dma_start(x_nat[:, :, :], x.rearrange("(t p) d -> p t d", p=P)).then_inc(ld_x, 16)
            act.dma_start(posi[:, :], positions.partition_broadcast(P)).then_inc(ld_pos, 16)
            n_split = [0]

            def split():
                n = n_split[0]
                if n == len(SLABS):
                    return
                n_split[0] += 1
                act.wait_ge(slab_loaded[n % RING], 16 * (n // RING + 1))
                if n >= RING:
                    act.wait_ge(slab_used, n - RING + 1)
                w = slab_words(SLABS[n][0])
                act.activation(slab_hi[n % RING][:, 0:w], slab_raw[n % RING][:, 0:w], ACT.Copy).then_inc(slab_hi_ready, 1)

            t_uses, s_uses, o_uses, z_uses, pvs = [0], [0], [0], [0], [0]
            t_marks = []

            def take_t():
                k = t_uses[0]
                t_uses[0] += 1
                act.wait_ge(t_full, k + 1)
                return k

            def turned_block(w):
                k = take_t()
                if pvs[0] >= 2:
                    act.wait_ge(pv_done, pvs[0] - 1)
                pvs[0] += 1
                act.activation(pt_hi[k % 2][:, 0:w], ps[:, T_ + k % 2, 0:w], ACT.Copy).then_inc(t_hi, 1)

            def head_out(dst, src):
                o_uses[0] += 1
                act.wait_ge(pv_done, pvs[0])
                act.activation(dst, src, ACT.Copy).then_inc(o_drained, 1)

            def mem_exps(u):
                s_uses[0] += 1
                act.wait_ge(bias_ready, s_uses[0])
                if u >= 2:
                    act.wait_ge(t_full, t_marks[u - 2])
                for qt in range(2):
                    ins = act.activation(mprob[u % 2][:, qt, :], ps[:, S_, qt * MEM:(qt + 1) * MEM], ACT.Exp,
                                         bias=nbias[:, u % 2, qt:qt + 1], scale=SCALE, accum_out=ssum[:, u % 2, qt:qt + 1])
                ins.then_inc(s_drained, 1)

            def mem_values(u):
                turned_block(T)
                t_marks.append(t_uses[0])
                h, half = u // 2, u % 2
                head_out(mixed[:, MEM0 + h, half * 2 * P:(half + 1) * 2 * P], ps[:, O_, 0:2 * P])

            def head_exps(p, hh):
                _, i, _ = pair_of(p)
                u = s_uses[0]
                s_uses[0] += 1
                act.wait_ge(bias_ready, u + 1)
                if p == 0 and hh == 0:
                    act.wait_ge(t_full, t_uses[0])
                    act.wait_ge(pv_done, pvs[0])
                if hh == 0 and p >= 2:
                    act.wait_ge(t_full, t_marks[p - 2])
                o = prob[p % 2][:, hh, :]
                ob = o[:, CMP_COLS:CMP_COLS + 2 * P * (i + 1)].rearrange("p (j b k) -> p b j k", b=2, k=P)
                flat = ps[:, 0:3, :].rearrange("p s c -> p (s c)")
                sbk = flat[:, 256:256 + 2 * P * (i + 1)].rearrange("p (j b k) -> p b j k", b=2, k=P)
                act.activation(o[:, 0:CMP_COLS], flat[:, 224:256], ACT.Exp, bias=nbias[:, u % 2, 0:1], scale=SCALE,
                               accum_out=ssum[:, u % 2, 0:1])
                for b in range(2):
                    ins = act.activation(ob[:, b, :, :], sbk[:, b, :, :], ACT.Exp, bias=nbias[:, u % 2, 1 + b:2 + b],
                                         scale=SCALE, accum_out=ssum[:, u % 2, 1 + b:2 + b])
                ins.then_inc(s_drained, 1)

            def pair_values(p, part):
                g, i, h0 = pair_of(p)
                if part == 0:
                    turned_block(2 * P)
                js = range(0, (i + 1) // 2) if part == 0 else range((i + 1) // 2, i + 1)
                for _ in js:
                    turned_block(T)
                if part == 1:
                    t_marks.append(t_uses[0])
                    m0 = NSA0 + PER_GROUP * g + h0
                    head_out(mixed[:, m0:m0 + 2, i * P:(i + 1) * P],
                             ps[:, O_, 0:2 * P].rearrange("p (h q) -> p h q", h=2))

            pending = []

            def finish_rot():
                if not pending:
                    return
                kind, n = pending.pop()
                if kind == "kc":
                    return
                act.wait_ge(rot_turned, ROT_INDEX[kind, n] + 1)
                src = z[Z_INDEX[kind, n] % 2][:, :]
                dst = z_key_dst("hi", kind, n)
                act.activation(dst, src if kind == "q" else blocks_of(src), ACT.Copy).then_inc(rot_hi, 1)

            def take_z():
                k = z_uses[0]
                z_uses[0] += 1
                if k >= 2:
                    act.wait_ge(z_done, k - 1)
                return z[k % 2]

            def project(kind, n):
                if kind in ("memk", "memq"):
                    wait_slab_used(act, kind, n)
                    src, dst = ps[:, pj_bank(kind, n), :], mq_hi[:, n, :]
                    if kind == "memk":
                        src, dst = src[:, 0:MEM], mk_hi[:, n, :]
                    act.activation(dst, src, ACT.Copy).then_inc(pj_hi, 1)
                elif kind == "memv" and n == 3:
                    wait_slab_used(act, "memv", 3)
                    act.activation(mv_hi[:, :, :], ps[:, S_:S_ + 2, :], ACT.Copy).then_inc(memv_hi, 1)
                elif kind == "v" and n % 2:
                    piece = n // 2
                    bank = 4 * (piece % 2)
                    wait_slab_used(act, "v", n)
                    src = ps[:, bank:bank + 4, :]
                    if piece < 2:
                        act.activation(v_hi[:, :, piece * VC:(piece + 1) * VC], src[:, :, 0:VC], ACT.Copy).then_inc(val_copied, 1)
                    else:
                        act.activation(ret_v[:, :, (piece - 2) * VC:(piece - 1) * VC], src[:, :, 0:VC], ACT.Copy).then_inc(val_copied, 1)
                    if piece:
                        act.wait_ge(val_drained, piece)
                    act.activation(gate_t[:, :, :], src[:, :, VC:VW], ACT.Tanh, scale=0.5).then_inc(val_tanh, 1)
                elif kind in ("retq", "retk"):
                    wait_slab_used(act, kind, n)
                    t = take_z()
                    for b in range(4):
                        act.activation(t[32 * b:32 * b + 32, :], ps[32 * (b ^ 1):32 * (b ^ 1) + 32, pj_bank(kind, n), :],
                                       ACT.Copy).then_inc(ret_swapped, 1)
                elif kind in ("kc", "vc", "ks", "kw", "q"):
                    wait_slab_used(act, kind, n)
                    if kind in ("kc", "vc"):
                        dst = z_cmp[:, (2 if kind == "vc" else 0) + n, :]
                    else:
                        dst = take_z()[:, :]
                    j = PJ_ORDER.index((kind, n))
                    act.activation(dst, ps[:, PJ_ + j % 2, :], ACT.Copy).then_inc(pj_drained[j % 2], 1)
                    finish_rot()
                    if kind != "vc":
                        pending.append((kind, n))
                elif kind == "gate":
                    finish_rot()
                    wait_slab_used(act, kind, n)
                    t = take_z()
                    act.activation(t[:, :], ps[:, pj_bank(kind, n), :], ACT.Tanh, scale=0.5).then_inc(gate_tanh, 1)

            def mixed_hi(n):
                if n >= RING:
                    act.wait_ge(slab_used, SLABS.index(("out", 0)) + n - RING + 1)
                t = OUT_ORDER[n]
                act.wait_ge(z_done, Z_INDEX["gate", t] + 1)
                act.activation(mix_hi[n % RING][:, :], mixed[:, t, :], ACT.Copy).then_inc(mix_hi_ready, 1)

            for _ in range(LEAD):
                split()
            for what, kind, n in SCHEDULE:
                if what == "norm":
                    rows = MT if kind == "mem" else TT
                    src, col = (mem_nat, 0) if kind == "mem" else (x_nat, 2)
                    gain = S_GMEM if kind == "mem" else S_GPRE
                    hi = m_hi if kind == "mem" else h_hi
                    if kind == "mem":
                        act.wait_ge(ld_mem, 16)
                        for r in range(MT):
                            if r:
                                act.wait_ge(squares_done, r)
                            act.activation(square[:, :], mem_nat[:, r, :], ACT.Square,
                                           accum_out=sumsq[:, r:r + 1]).then_inc(squares_done, 1)
                        act.wait_ge(ld_par, 16)
                    for k in range(KT):
                        b = take_t()
                        act.activation(hi[:, k, :], ps[:, T_ + b % 2, 0:rows * P], ACT.Copy,
                                       scale=par[:, gain + k:gain + k + 1]).then_inc(t_hi, 1)
                    if kind == "mem":
                        act.wait_ge(ld_x, 16)
                        for r in range(TT):
                            act.wait_ge(squares_done, MT + r)
                            act.activation(square[:, :], x_nat[:, r, :], ACT.Square,
                                           accum_out=sumsq[:, 2 + r:3 + r]).then_inc(squares_done, 1)
                elif what == "tables":
                    act.wait_ge(angles_ready, 1)
                    act.activation(ret_rot[:, :, :], ang[:, 0:2, :], ACT.Sin).then_inc(rot_ready, 1)
                    act.activation(nsa_rot[:, :, :], ang[:, 2:4, :], ACT.Sin).then_inc(rot_ready, 1)
                    act.wait_ge(decay_iota, 1)
                    act.wait_ge(rot_ready, 2)
                    for h in range(RET_HEADS):
                        act.activation(decay[:, h, :], decay_i[:, :], ACT.Exp,
                                       scale=math.log1p(-(2.0 ** (-5 - h)))).then_inc(decay_exp, 1)
                elif what == "slab":
                    split()
                    if kind == "out":
                        mixed_hi(n)
                    else:
                        project(kind, n)
                elif what == "mem" and kind == "att":
                    mem_exps(n)
                    if n:
                        mem_values(n - 1)
                elif what == "mem":
                    mem_values(2 * MEM_HEADS - 1)
                    t_marks.clear()
                elif what == "rot":
                    finish_rot()
                elif (what, kind) == ("ret", "scores"):
                    t_uses[0] += TT
                elif (what, kind) == ("ret", "values"):
                    o_uses[0] += 1
                elif (what, kind) == ("ret", "turn"):
                    k = take_t()
                    act.activation(mixed[:, RET0 + n, :], ps[:, T_ + k % 2, :], ACT.Copy,
                                   scale=par[:, S_GN + n:S_GN + n + 1]).then_inc(t_drained[k % 2], 1)
                elif what == "blocks":
                    i = 0 if kind == "k" else 1
                    act.wait_ge(blk_sum, i + 1)
                    if i:
                        wait_slab_used(act, "w1k", 7)
                    act.activation(blk_hi[:, :], blk[:, :], ACT.Copy).then_inc(blk_hi_ready, 1)
                elif what == "mlp":
                    i = 0 if kind == "k" else 1
                    o_uses[0] += 1
                    wait_slab_used(act, "w1" + kind, 7)
                    if i:
                        act.wait_ge(t_full, t_uses[0])
                    act.activation(hid[0:BLK_N, 0, :], ps[0:BLK_N, O_, 0:CMP_HIDDEN], ACT.Copy).then_inc(o_drained, 1)
                    act.wait_ge(o_drained, o_uses[0])
                    act.activation(hid[0:BLK_N, 1, :], hid[0:BLK_N, 0, :], ACT.Square).then_inc(hid_sq, 1)
                    act.wait_ge(hid_poly, i + 1)
                    act.activation(hid[0:BLK_N, 3, :], hid[0:BLK_N, 2, :], ACT.Tanh,
                                   scale=math.sqrt(2.0 / math.pi)).then_inc(hid_tanh, 1)
                    k = take_t()
                    act.activation(hid_t[:, :, :], ps[:, T_ + k % 2, 0:2 * P].rearrange("p (c r) -> p c r", c=2)[:, :, 0:BLK_N],
                                   ACT.Copy, scale=0.5).then_inc(t_drained[k % 2], 1)
                    k = take_t()
                    if kind == "k":
                        act.activation(keys_hi[:, :, 0:N_CMP], ps[:, T_ + k % 2, 0:BLK_N].rearrange("p (g n) -> p g n", g=2),
                                       ACT.Copy).then_inc(t_hi, 1)
                    else:
                        act.activation(vc_hi[0:N_CMP, :, :], ps[0:N_CMP, T_ + k % 2, 0:2 * P].rearrange("p (g n) -> p g n", g=2),
                                       ACT.Copy).then_inc(t_hi, 1)
                elif what == "pair" and kind == "att":
                    for hh in range(2):
                        head_exps(n, hh)
                        if n:
                            pair_values(n - 1, hh)
                elif what == "pair":
                    for hh in range(2):
                        pair_values(PAIRS - 1, hh)
            for t in range(TT):
                act.wait_ge(y_full, t + 1)
                if t:
                    act.wait_ge(y_squared, t)
                act.activation(y_sq[:, :], ps[:, 2 * t:2 * t + 2, :].rearrange("p h c -> p (h c)"), ACT.Square,
                               accum_out=sumsq[:, 10 + t:11 + t]).then_inc(y_squared, 1)

        @block.vector
        def _(dve):
            count = [0]

            def link(ins):
                count[0] += 1
                ins.then_inc(dve_step, 1)
                dve.wait_ge(dve_step, count[0])

            n_split = [0]

            def split():
                n = n_split[0]
                if n == len(SLABS):
                    return
                n_split[0] += 1
                dve.wait_ge(slab_hi_ready, n + 1)
                w = slab_words(SLABS[n][0])
                dve.tensor_tensor(slab_lo[n % RING][:, 0:w], slab_raw[n % RING][:, 0:w],
                                  slab_hi[n % RING][:, 0:w].bitcast(F32), ALU.subtract).then_inc(slab_lo_ready, 1)

            t_uses, t_his, s_uses, z_uses = [0], [0], [0], [0]

            def take_t_hi():
                k = t_uses[0]
                t_uses[0] += 1
                t_his[0] += 1
                dve.wait_ge(t_hi, t_his[0])
                return k

            def turned_block(w):
                k = take_t_hi()
                dve.tensor_tensor(pt_lo[k % 2][:, 0:w], ps[:, T_ + k % 2, 0:w], pt_hi[k % 2][:, 0:w].bitcast(F32),
                                  ALU.subtract).then_inc(t_drained[k % 2], 1)

            def norm_rows(nat, r0, nr, part):
                dve.wait_ge(squares_done, r0 + nr)
                dve.tensor_scalar(meansq[:, r0:r0 + nr], sumsq[:, r0:r0 + nr], 1.0 / D, EPS, ALU.mult,
                                  ALU.add).then_inc(meansq_ready, 1)
                dve.wait_ge(rstd_ready, part)
                for r in range(nr):
                    dve.tensor_scalar(nat[:, r, :], nat[:, r, :], rstd[:, r0 + r:r0 + r + 1], None,
                                      ALU.mult).then_inc(normed, 1)

            def mem_front(u):
                s_uses[0] += 1
                dve.wait_ge(s_full, s_uses[0])
                link(dve.tensor_reduce(smax[:, u % 2, 0:2], ps[:, S_, :].rearrange("p (q k) -> p q k", q=2), AX.X, ALU.max))
                dve.tensor_scalar(nbias[:, u % 2, 0:2], smax[:, u % 2, 0:2], -SCALE, None, ALU.mult).then_inc(bias_ready, 1)

            def mem_back(u):
                dve.wait_ge(s_drained, s_uses[0])
                link(dve.reciprocal(coef[:, u % 2, 0:2], ssum[:, u % 2, 0:2]))
                for qt in range(2):
                    ins = dve.tensor_scalar(mprob[u % 2][:, qt, :], mprob[u % 2][:, qt, :], coef[:, u % 2, qt:qt + 1],
                                            None, ALU.mult)
                ins.then_inc(prob_ready, 1)

            def mem_values(u):
                turned_block(T)

            def head_front(p, hh):
                g, i, h0 = pair_of(p)
                u = s_uses[0]
                s_uses[0] += 1
                if p == 0 and hh == 0:
                    dve.wait_ge(consts_ready, 2 + TT + 1)
                dve.wait_ge(s_full, u + 1)
                flat = ps[:, 0:3, :].rearrange("p s c -> p (s c)")
                cw = TT * CMP_COLS
                if i == 0:
                    link(dve.tensor_tensor(flat[:, 224:512], flat[:, 224:512], masks[:, cw - CMP_COLS:cw + 2 * P], ALU.add))
                else:
                    m = masks[:, (TT - 1 - i) * CMP_COLS:(TT - i) * CMP_COLS]
                    dve.tensor_tensor(flat[:, 224:256], flat[:, 224:256], m, ALU.add)
                    d = flat[:, 256 + 2 * P * i:256 + 2 * P * (i + 1)]
                    link(dve.tensor_tensor(d, d, masks[:, cw:], ALU.add))
                dve.tensor_reduce(smax[:, u % 2, 0:1], flat[:, 224:256], AX.X, ALU.max)
                view = flat[:, 256:256 + 2 * P * (i + 1)].rearrange("p (j b k) -> p b j k", b=2, k=P)
                link(dve.tensor_reduce(smax[:, u % 2, 1:3], view, AX.XY, ALU.max))
                dve.tensor_scalar(nbias[:, u % 2, 0:3], smax[:, u % 2, 0:3], 0.1 * NEG, -SCALE, ALU.max,
                                  ALU.mult).then_inc(bias_ready, 1)

            def head_back(p, hh):
                g, i, h0 = pair_of(p)
                u = s_uses[0] - 1
                dve.wait_ge(s_drained, u + 1)
                head = PER_GROUP * g + h0 + hh
                c = coef[:, u % 2, 0:3]
                link(dve.tensor_scalar(c, ssum[:, u % 2, 0:3], 1e-30, None, ALU.max))
                link(dve.reciprocal(c, c))
                link(dve.tensor_tensor(c, c, gates[:, i, head:3 * HEADS:HEADS], ALU.mult))
                o = prob[p % 2][:, hh, :]
                ob = o[:, CMP_COLS:CMP_COLS + 2 * P * (i + 1)].rearrange("p (j b k) -> p b j k", b=2, k=P)
                dve.tensor_scalar(o[:, 0:CMP_COLS], o[:, 0:CMP_COLS], coef[:, u % 2, 0:1], None, ALU.mult)
                for b in range(2):
                    ins = dve.tensor_scalar(ob[:, b, :, :], ob[:, b, :, :], coef[:, u % 2, 1 + b:2 + b], None, ALU.mult)
                ins.then_inc(prob_ready, 1)

            def pair_values(p, part):
                g, i, h0 = pair_of(p)
                if part == 0:
                    turned_block(2 * P)
                js = range(0, (i + 1) // 2) if part == 0 else range((i + 1) // 2, i + 1)
                for _ in js:
                    turned_block(T)

            pending = []

            def finish_rot():
                if not pending:
                    return
                kind, n = pending.pop()
                if kind == "kc":
                    return
                dve.wait_ge(rot_hi, HI_INDEX[kind, n] + 1)
                src = z[Z_INDEX[kind, n] % 2][:, :]
                hi, lo = z_key_dst("hi", kind, n), z_key_dst("lo", kind, n)
                dve.tensor_tensor(lo, src if kind == "q" else blocks_of(src), hi.bitcast(F32),
                                  ALU.subtract).then_inc(z_done, 1)

            def project(kind, n):
                if kind in ("memk", "memq"):
                    j = PJ_ORDER.index((kind, n))
                    dve.wait_ge(pj_hi, SPLIT_ORDER.index((kind, n)) + 1)
                    src, hi, lo = ps[:, PJ_ + j % 2, :], mq_hi[:, n, :], mq_lo[:, n, :]
                    if kind == "memk":
                        src, hi, lo = src[:, 0:MEM], mk_hi[:, n, :], mk_lo[:, n, :]
                    dve.tensor_tensor(lo, src, hi.bitcast(F32), ALU.subtract).then_inc(pj_drained[j % 2], 1)
                elif kind == "memv" and n == 3:
                    dve.wait_ge(memv_hi, 1)
                    dve.tensor_tensor(mv_lo[:, :, :], ps[:, S_:S_ + 2, :], mv_hi[:, :, :].bitcast(F32),
                                      ALU.subtract).then_inc(memv_drained, 1)
                elif kind == "v" and n % 2:
                    piece = n // 2
                    bank = 4 * (piece % 2)
                    if piece < 2:
                        c = slice(piece * VC, (piece + 1) * VC)
                        dve.wait_ge(val_tanh, piece + 1)
                        dve.tensor_tensor(v_lo[:, :, c], ps[:, bank:bank + 4, 0:VC], v_hi[:, :, c].bitcast(F32), ALU.subtract)
                    dve.wait_ge(val_tanh, piece + 1)
                    dve.tensor_scalar(gates[:, :, piece * GC:(piece + 1) * GC], gate_t[:, :, :], 1.0, 0.5, ALU.add,
                                      ALU.mult).then_inc(val_drained, 1)
                elif kind in ("retq", "retk"):
                    i = RET_PROJ.index((kind, n))
                    j = PJ_ORDER.index((kind, n))
                    dve.wait_ge(ret_swapped, 4 * (i + 1))
                    dve.wait_ge(rot_ready, 1)
                    if i == 0:
                        dve.wait_ge(decay_ready, 1)
                    else:
                        dve.wait_ge(z_done, z_uses[0])
                    dve.tensor_tensor(ret_z[:, :], ps[:, PJ_ + j % 2, :], ret_rot[:, 0, :], ALU.mult).then_inc(pj_drained[j % 2], 1)
                    dve.wait_ge(pj_drained[j % 2], j // 2 + 1)
                    dve.wait_ge(ret_sin, i + 1)
                    t = z[z_uses[0] % 2]
                    z_uses[0] += 1
                    if kind == "retk":
                        dve.tensor_tensor(ret_k[:, n, :], ret_z[:, :], t[:, :], ALU.add).then_inc(z_done, 1)
                    else:
                        for hh in range(2):
                            r = slice(64 * hh, 64 * hh + 64)
                            ins = dve.tensor_tensor(ret_q[r, 2 * n + hh, :], ret_z[r, :], t[r, :], ALU.add)
                        ins.then_inc(z_done, 1)
                elif kind in ("kc", "vc", "ks", "kw", "q"):
                    if kind != "vc":
                        wait_pj_drained(dve, kind, n)
                        r = ROT_INDEX[kind, n]
                        if r:
                            dve.wait_ge(rot_turned, r)
                        if kind == "kc":
                            src = z_cmp[0:32, n, :]
                        else:
                            src = z[z_uses[0] % 2][0:32, :]
                            z_uses[0] += 1
                        dve.stream_shuffle(swp[:, :], src, [(i + 16) % 32 for i in range(32)]).then_inc(rot_swapped, 1)
                    finish_rot()
                    if kind != "vc":
                        pending.append((kind, n))
                elif kind == "gate":
                    finish_rot()
                    t = z[z_uses[0] % 2]
                    z_uses[0] += 1
                    j = PJ_ORDER.index((kind, n))
                    dve.wait_ge(gate_tanh, gated_by(n))
                    dve.scalar_tensor_tensor(t[:, :], t[:, :], 1.0, ps[:, PJ_ + j % 2, :], ALU.add, ALU.mult).then_inc(pj_drained[j % 2], 1)
                    dve.wait_ge(pj_drained[j % 2], j // 2 + 1)
                    wait_head_out(dve, n)
                    dve.scalar_tensor_tensor(mixed[:, n, :], t[:, :], 0.5, mixed[:, n, :], ALU.mult, ALU.mult).then_inc(z_done, 1)

            def mixed_lo(n):
                t = OUT_ORDER[n]
                dve.wait_ge(mix_hi_ready, n + 1)
                dve.tensor_tensor(mix_lo[n % RING][:, :], mixed[:, t, :], mix_hi[n % RING][:, :].bitcast(F32),
                                  ALU.subtract).then_inc(mix_ready, 1)

            for _ in range(LEAD):
                split()
            for what, kind, n in SCHEDULE:
                if what == "norm":
                    gain = S_GMEM if kind == "mem" else S_GPRE
                    hi, lo = (m_hi, m_lo) if kind == "mem" else (h_hi, h_lo)
                    rows = MT if kind == "mem" else TT
                    if kind == "mem":
                        norm_rows(mem_nat, 0, MT, 1)
                        dve.wait_ge(ld_par, 16)
                    for k in range(KT):
                        b = take_t_hi()
                        dve.scalar_tensor_tensor(lo[:, k, :], ps[:, T_ + b % 2, 0:rows * P], par[:, gain + k:gain + k + 1],
                                                 hi[:, k, :].bitcast(F32), ALU.mult, ALU.subtract).then_inc(t_drained[b % 2], 1)
                    if kind == "mem":
                        norm_rows(x_nat, 2, TT, 2)
                elif what == "tables":
                    dve.wait_ge(ld_pos, 16)
                    link(dve.tensor_copy(posf[:, :], posi[:, :]))
                    dve.wait_ge(t_full, KT + KT)
                    for v in range(4):
                        ins = dve.tensor_scalar(ang[:, v, :], posf[:, :], par[:, S_FREQ + v:S_FREQ + v + 1], None, ALU.mult)
                    link(ins)
                    magic = 12582912.0
                    for v in range(4):
                        ins = dve.tensor_scalar(turns[:, v, :], ang[:, v, :], 1.0 / (2 * math.pi), 0.25 * (v % 2 == 0),
                                                ALU.mult, ALU.add)
                    link(ins)
                    link(dve.tensor_scalar(turns[:, :, :], turns[:, :, :], magic, None, ALU.add))
                    link(dve.tensor_scalar(turns[:, :, :], turns[:, :, :], magic, None, ALU.subtract))
                    c1 = 6.28125
                    c2 = float(np.float32(round((2 * math.pi - c1) * 2 ** 19) / 2 ** 19))
                    c3 = 2 * math.pi - c1 - c2
                    for c in (c1, c2, c3):
                        link(dve.scalar_tensor_tensor(ang[:, :, :], turns[:, :, :], -c, ang[:, :, :], ALU.mult, ALU.add))
                    for v in (0, 2):
                        ins = dve.tensor_scalar(ang[:, v, :], ang[:, v, :], math.pi / 2, None, ALU.add)
                    link(ins)
                    dve.tensor_scalar(ang[:, :, :], ang[:, :, :], 3.1415925, -3.1415925, ALU.min, ALU.max).then_inc(angles_ready, 1)
                elif what == "slab":
                    split()
                    if kind == "out":
                        mixed_lo(n)
                    else:
                        project(kind, n)
                elif what == "mem" and kind == "att":
                    mem_front(n)
                    if n:
                        mem_values(n - 1)
                    mem_back(n)
                elif what == "mem":
                    mem_values(2 * MEM_HEADS - 1)
                elif what == "rot":
                    finish_rot()
                elif (what, kind) == ("ret", "scores"):
                    if n == 0:
                        dve.wait_ge(decay_ready, 1 + RET_HEADS)
                    off = 0
                    if n >= 2:
                        dve.wait_ge(ret_full, n - 1)
                    for j in range(TT):
                        k = t_uses[0]
                        t_uses[0] += 1
                        w = T - P * j
                        dve.wait_ge(t_full, k + 1)
                        dve.scalar_tensor_tensor(inner[n % 2][:, off:off + w], ps[:, T_ + k % 2, 0:w], RET_QK ** -0.5,
                                                 decay[:, n, 0:w], ALU.mult, ALU.mult).then_inc(t_drained[k % 2], 1)
                        off += w
                elif (what, kind) == ("ret", "values"):
                    dve.wait_ge(ret_full, n + 1)
                    for i in range(TT):
                        ins = dve.bn_stats(bn[:, i, :], ps[:, O_, i * P:(i + 1) * P])
                    link(ins)
                    for i in range(TT):
                        ins = dve.bn_aggr(mv[:, i, :], bn[:, i, :])
                    link(ins)
                    dve.tensor_scalar(meansq[:, 6:6 + TT], mv[:, :, 1], EPS, None, ALU.add).then_inc(ret_var, 1)
                    dve.wait_ge(ret_rstd, n + 1)
                    if n >= 2:
                        dve.wait_ge(t_full, T_USED["ret", "turn", n - 2])
                    for i in range(TT):
                        ins = dve.tensor_scalar(ret_n[n % 2][:, i, :], ps[:, O_, i * P:(i + 1) * P], mv[:, i, 0:1],
                                                rstd[:, 6 + i:7 + i], ALU.subtract, ALU.mult)
                    ins.then_inc(o_drained, 1)
                elif (what, kind) == ("ret", "turn"):
                    t_uses[0] += 1
                elif what == "blocks":
                    i = 0 if kind == "k" else 1
                    if i == 0:
                        dve.wait_ge(rot_turned, 2)
                        for g in range(GROUPS):
                            wait_pj_drained(dve, "vc", g)
                        dve.wait_ge(ret_full, RET_HEADS)
                        link(dve.memset(blk[:, CMP_BLOCK * BLK_N:], 0.0))
                    else:
                        dve.wait_ge(blk_ready, 1)
                    pos = par[:, S_POS + CMP_BLOCK * i:S_POS + CMP_BLOCK * (i + 1)]
                    bv = blk[:, 0:CMP_BLOCK * BLK_N].rearrange("p (c g n) -> p c g n", g=GROUPS, n=N_CMP)
                    for g in range(GROUPS):
                        zc = z_cmp[:, 2 * i + g, :].rearrange("p (n s) -> p s n", s=CMP_STRIDE)
                        for half in range(2):
                            c = slice(half * CMP_STRIDE, (half + 1) * CMP_STRIDE)
                            ins = dve.tensor_tensor(bv[:, c, g, :], zc[:, :, half:half + N_CMP],
                                                    pos[:, c].unsqueeze(2).to_broadcast([P, CMP_STRIDE, N_CMP]), ALU.add)
                    ins.then_inc(blk_sum, 1)
                    dve.wait_ge(blk_hi_ready, i + 1)
                    dve.tensor_tensor(blk_lo[:, :], blk[:, :], blk_hi[:, :].bitcast(F32), ALU.subtract).then_inc(blk_ready, 1)
                elif what == "mlp":
                    i = 0 if kind == "k" else 1
                    dve.wait_ge(hid_sq, i + 1)
                    a = hid[0:BLK_N, 2, :]
                    link(dve.tensor_scalar(a, hid[0:BLK_N, 1, :], 0.044715, 1.0, ALU.mult, ALU.add))
                    dve.tensor_tensor(a, a, hid[0:BLK_N, 0, :], ALU.mult).then_inc(hid_poly, 1)
                    dve.wait_ge(hid_tanh, i + 1)
                    dve.scalar_tensor_tensor(hid[0:BLK_N, 3, :], hid[0:BLK_N, 3, :], 1.0, hid[0:BLK_N, 0, :], ALU.add,
                                             ALU.mult).then_inc(hid_ready, 1)
                    t_uses[0] += 1
                    k = take_t_hi()
                    if kind == "k":
                        dve.memset(keys_hi[:, :, N_CMP:CMP_COLS].bitcast(F32), 0.0)
                        dve.memset(keys_lo[:, :, N_CMP:CMP_COLS].bitcast(F32), 0.0)
                        dve.tensor_tensor(keys_lo[:, :, 0:N_CMP], ps[:, T_ + k % 2, 0:BLK_N].rearrange("p (g n) -> p g n", g=2),
                                          keys_hi[:, :, 0:N_CMP].bitcast(F32), ALU.subtract).then_inc(t_drained[k % 2], 1)
                    else:
                        dve.tensor_tensor(vc_lo[0:N_CMP, :, :], ps[0:N_CMP, T_ + k % 2, 0:2 * P].rearrange("p (g n) -> p g n", g=2),
                                          vc_hi[0:N_CMP, :, :].bitcast(F32), ALU.subtract).then_inc(t_drained[k % 2], 1)
                elif what == "pair" and kind == "att":
                    for hh in range(2):
                        head_front(n, hh)
                        if n:
                            pair_values(n - 1, hh)
                        head_back(n, hh)
                elif what == "pair":
                    for hh in range(2):
                        pair_values(PAIRS - 1, hh)
            dve.wait_ge(ld_res, 16)
            dve.wait_ge(ld_post, 16)
            for t in range(TT):
                y = ps[:, 2 * t:2 * t + 2, :].rearrange("p h c -> p (h c)")
                dve.wait_ge(y_squared, t + 1)
                dve.tensor_scalar(meansq[:, 10 + t:11 + t], sumsq[:, 10 + t:11 + t], 1.0 / D, EPS, ALU.mult,
                                  ALU.add).then_inc(y_meansq, 1)
                dve.wait_ge(y_rstd, t + 1)
                if t >= 2:
                    dve.wait_ge(y_stored[t - 2], 16)
                link(dve.scalar_tensor_tensor(y_sb[t % 2][:, :], y, rstd[:, 10 + t:11 + t], gpost_b[:, :], ALU.mult, ALU.mult))
                dve.tensor_tensor(y_sb[t % 2][:, :], y_sb[t % 2][:, :], x_res[:, t, :], ALU.add).then_inc(y_ready, 1)

        @block.tensor
        def _(pe):
            t_uses, s_uses, o_uses, slabs, pts = [0], [0], [0], [0], [0]

            def take_t():
                k = t_uses[0]
                t_uses[0] += 1
                if k >= 2:
                    pe.wait_ge(t_drained[k % 2], k // 2)
                return k

            def product(dst, w, m, first=True, last=True):
                pe.matmul(dst, w[0], m[0], start=first, stop=False)
                pe.matmul(dst, w[0], m[1], start=False, stop=False)
                return pe.matmul(dst, w[1], m[0], start=False, stop=last)

            def turn_blocks(blocks):
                k = take_t()
                for c, src in enumerate(blocks):
                    ins = pe.transpose(ps[:, T_ + k % 2, c * P:(c + 1) * P], src, ident[:, :])
                ins.then_inc(t_full, 1)
                return k

            def o_bank():
                if o_uses[0]:
                    pe.wait_ge(o_drained, o_uses[0])
                o_uses[0] += 1

            def wait_turned(k):
                pe.wait_ge(t_drained[k % 2], k // 2 + 1)

            def mem_scores(u):
                h, half = u // 2, u % 2
                if s_uses[0]:
                    pe.wait_ge(s_drained, s_uses[0])
                s_uses[0] += 1
                for qt in range(2):
                    c = slice((2 * half + qt) * P, (2 * half + qt + 1) * P)
                    ins = product(ps[:, S_, qt * MEM:(qt + 1) * MEM], (mq_hi[:, h, c], mq_lo[:, h, c]),
                                  (mk_hi[:, h, :], mk_lo[:, h, :]))
                ins.then_inc(s_full, 1)

            def mem_values(u):
                h = u // 2
                pe.wait_ge(prob_ready, u + 1)
                k = turn_blocks([mprob[u % 2][:, qt, kt * P:(kt + 1) * P] for kt in range(MT) for qt in range(2)])
                o_bank()
                wait_turned(k)
                c = slice(h * DH, (h + 1) * DH)
                for kt in range(MT):
                    m = slice(kt * 2 * P, (kt + 1) * 2 * P)
                    ins = product(ps[:, O_, 0:2 * P], (mv_hi[:, kt, c], mv_lo[:, kt, c]),
                                  (pt_hi[k % 2][:, m], pt_lo[k % 2][:, m]), kt == 0, kt == MT - 1)
                ins.then_inc(pv_done, 1)

            def head_scores(p, hh):
                g, i, h0 = pair_of(p)
                h = PER_GROUP * g + h0 + hh
                if s_uses[0]:
                    pe.wait_ge(s_drained, s_uses[0])
                s_uses[0] += 1
                c = slice(i * P, (i + 1) * P)
                q = (q_hi[:, h, c], q_lo[:, h, c])
                cuts = [(0, CMP_COLS + 2 * P, S_, 224)]
                if i:
                    cuts.append((CMP_COLS + 2 * P, 2 * P * min(i, 2), S_ + 1, 0))
                if i == 3:
                    cuts.append((CMP_COLS + 6 * P, 2 * P, S_ + 2, 0))
                for k0, w, bank, col in cuts:
                    ins = product(ps[:, bank, col:col + w], q, (keys_hi[:, g, k0:k0 + w], keys_lo[:, g, k0:k0 + w]))
                ins.then_inc(s_full, 1)

            def pair_values(p, part):
                g, i, h0 = pair_of(p)
                js = range(0, (i + 1) // 2) if part == 0 else range((i + 1) // 2, i + 1)
                if part == 0:
                    pe.wait_ge(prob_ready, 2 * MEM_HEADS + 2 * (p + 1))
                todo = [-1, *js] if part == 0 else list(js)
                used = []
                pr = prob[p % 2]

                def turn(j):
                    if j < 0:
                        return turn_blocks([pr[:, hh, 0:P] for hh in range(2)])
                    c = CMP_COLS + 2 * P * j
                    return turn_blocks([pr[:, hh, c + b * P:c + (b + 1) * P] for b in range(2) for hh in range(2)])

                def values(j, k):
                    wait_turned(k)
                    if j < 0:
                        o_bank()
                        product(ps[:, O_, 0:2 * P], (vc_hi[:, g, :], vc_lo[:, g, :]),
                                (pt_hi[k % 2][:, 0:2 * P], pt_lo[k % 2][:, 0:2 * P]), True, False).then_inc(pv_done, 1)
                        return
                    for b in range(2):
                        c = slice(b * VC + g * DH, b * VC + (g + 1) * DH)
                        m = slice(b * 2 * P, (b + 1) * 2 * P)
                        ins = product(ps[:, O_, 0:2 * P], (v_hi[:, j, c], v_lo[:, j, c]),
                                      (pt_hi[k % 2][:, m], pt_lo[k % 2][:, m]), False, j == i and b == 1)
                    ins.then_inc(pv_done, 1)

                last = None
                for j in todo:
                    k = turn(j)
                    if last:
                        values(*last)
                    last = (j, k)
                values(*last)

            def project(kind, n):
                s = slabs[0]
                slabs[0] += 1
                pe.wait_ge(slab_lo_ready, s + 1)
                hi, lo = slab_hi[s % RING], slab_lo[s % RING]
                if kind in PJ_KINDS:
                    j = PJ_ORDER.index((kind, n))
                    if j >= 2:
                        pe.wait_ge(pj_drained[j % 2], j // 2)
                    if j in (4, 5):
                        pe.wait_ge(val_drained, VP)
                    mh, ml, w = (m_hi, m_lo, MEM) if kind == "memk" else (h_hi, h_lo, T)
                    for k in range(KT):
                        c = slice(k * P, (k + 1) * P)
                        ins = product(ps[:, PJ_ + j % 2, 0:w], (hi[:, c], lo[:, c]), (mh[:, k, :], ml[:, k, :]),
                                      k == 0, k == KT - 1)
                elif kind == "memv":
                    for kk in range(2):
                        c = slice(kk * T, (kk + 1) * T)
                        for t in range(MT):
                            r = slice(t * P, (t + 1) * P)
                            k = 2 * n + kk
                            ins = product(ps[:, S_ + t, :], (m_hi[:, k, r], m_lo[:, k, r]), (hi[:, c], lo[:, c]),
                                          k == 0, k == KT - 1)
                elif kind == "v":
                    piece, half = n // 2, n % 2
                    if half == 0:
                        if piece == 0:
                            pe.wait_ge(memv_drained, 1)
                        elif piece == 1:
                            wait_pj_all_drained(pe, MEM_HEADS)
                            wait_t_drained(pe, t_uses[0])
                        else:
                            pe.wait_ge(val_drained, piece - 1)
                    bank = 4 * (piece % 2)
                    for t in range(TT):
                        r = slice(t * P, (t + 1) * P)
                        for kk in range(4):
                            k = 4 * half + kk
                            c = slice(kk * VW, (kk + 1) * VW)
                            ins = product(ps[:, bank + t, 0:VW], (h_hi[:, k, r], h_lo[:, k, r]), (hi[:, c], lo[:, c]),
                                          k == 0, k == KT - 1)
                elif kind in ("w1k", "w1v"):
                    if n == 0:
                        o_bank()
                        pe.wait_ge(blk_ready, 1 if kind == "w1k" else 2)
                    for cc in range(W1_C):
                        c = W1_C * n + cc
                        b = slice(c * BLK_N, c * BLK_N + P)
                        m = slice(cc * CMP_HIDDEN, (cc + 1) * CMP_HIDDEN)
                        ins = product(ps[:, O_, 0:CMP_HIDDEN], (blk_hi[:, b], blk_lo[:, b]), (hi[:, m], lo[:, m]),
                                      c == 0, c == CMP_BLOCK - 1)
                ins.then_inc(slab_used, 1)

            def out_products(n, t, s):
                hi, lo = slab_hi[s % RING], slab_lo[s % RING]
                r = slice(t * P, (t + 1) * P)
                for half in range(2):
                    c = slice(half * T, (half + 1) * T)
                    ins = product(ps[:, 2 * t + half, :], (mix_hi[n % RING][:, r], mix_lo[n % RING][:, r]),
                                  (hi[:, c], lo[:, c]), n == 0, n == MIX_TILES - 1)
                return ins

            for what, kind, n in SCHEDULE:
                if what == "norm":
                    if kind == "mem":
                        pe.wait_ge(consts_ready, 1)
                    pe.wait_ge(normed, MT if kind == "mem" else MT + TT)
                    nat, rows = (mem_nat, MT) if kind == "mem" else (x_nat, TT)
                    for k in range(KT):
                        turn_blocks([nat[:, r, k * P:(k + 1) * P] for r in range(rows)])
                    wait_t_drained(pe, t_uses[0])
                elif what == "slab" and kind != "out":
                    project(kind, n)
                elif what == "mem" and kind == "att":
                    if n == 0:
                        pe.wait_ge(val_drained, VP)
                        pe.wait_ge(pj_drained[0], 4)
                        pe.wait_ge(pj_drained[1], 4)
                    mem_scores(n)
                    if n:
                        mem_values(n - 1)
                elif what == "mem":
                    mem_values(2 * MEM_HEADS - 1)
                elif (what, kind) == ("ret", "scores"):
                    if n == 0:
                        pe.wait_ge(z_done, len(RET_PROJ))
                    for j in range(TT):
                        k = take_t()
                        pe.matmul(ps[:, T_ + k % 2, 0:T - P * j], ret_k[:, n // 2, j * P:(j + 1) * P],
                                  ret_q[:, n, j * P:], start=True, stop=True).then_inc(t_full, 1)
                elif (what, kind) == ("ret", "values"):
                    o_bank()
                    wait_t_drained(pe, T_USED["ret", "scores", n])
                    offs = [0, 512, 896, 1152]
                    for i in range(TT):
                        for j in range(i + 1):
                            c = offs[j] + (i - j) * P
                            ins = pe.matmul(ps[:, O_, i * P:(i + 1) * P], inner[n % 2][:, c:c + P],
                                            ret_v[:, j, n * RET_V:(n + 1) * RET_V], start=j == 0, stop=j == i)
                    ins.then_inc(ret_full, 1)
                elif (what, kind) == ("ret", "turn"):
                    pe.wait_ge(o_drained, O_USED["ret", "values", n])
                    turn_blocks([ret_n[n % 2][:, i, :] for i in range(TT)])
                elif what == "mlp":
                    pe.wait_ge(hid_ready, 1 if kind == "k" else 2)
                    k = take_t()
                    for c in range(2):
                        ins = pe.transpose(ps[:, T_ + k % 2, c * P:c * P + BLK_N], hid[0:BLK_N, 3, c * P:(c + 1) * P],
                                           ident[0:BLK_N, 0:BLK_N])
                    ins.then_inc(t_full, 1)
                    wait_turned(k)
                    k = take_t()
                    w2 = par[:, S_W2:].rearrange("p (a c d) -> p a c d", a=2, c=2)
                    if kind == "k":
                        for c in range(2):
                            ins = pe.matmul(ps[:, T_ + k % 2, 0:BLK_N], w2[:, 0, c, :], hid_t[:, c, :], start=c == 0, stop=c == 1)
                    else:
                        for g in range(GROUPS):
                            for c in range(2):
                                ins = pe.matmul(ps[0:N_CMP, T_ + k % 2, g * P:(g + 1) * P], hid_t[:, c, g * N_CMP:(g + 1) * N_CMP],
                                                w2[:, 1, c, :], start=c == 0, stop=c == 1)
                    ins.then_inc(t_full, 1)
                elif what == "pair" and kind == "att":
                    if n == 0:
                        wait_t_drained(pe, t_uses[0])
                        pe.wait_ge(consts_ready, 2 + TT + 1 + 2)
                        pe.wait_ge(z_done, Z_INDEX["q", PER_GROUP - 1] + 1)
                    if n == 2 * TT:
                        pe.wait_ge(z_done, Z_INDEX["q", HEADS - 1] + 1)
                    for hh in range(2):
                        head_scores(n, hh)
                        if n:
                            pair_values(n - 1, hh)
                elif what == "pair":
                    for hh in range(2):
                        pair_values(PAIRS - 1, hh)
            s0 = slabs[0]
            last3 = MIX_TILES - RING
            pe.wait_ge(s_drained, s_uses[0])
            pe.wait_ge(o_drained, o_uses[0])
            for n in range(last3):
                pe.wait_ge(slab_lo_ready, s0 + n + 1)
                pe.wait_ge(mix_ready, n + 1)
                for t in range(TT):
                    if n == 0 and t == 2:
                        wait_pj_all_drained(pe, len(PJ_ORDER))
                    if n == 0 and t == 3:
                        wait_t_drained(pe, t_uses[0])
                    ins = out_products(n, t, s0 + n)
                ins.then_inc(slab_used, 1)
            pe.wait_ge(slab_lo_ready, s0 + MIX_TILES)
            pe.wait_ge(mix_ready, MIX_TILES)
            for t in range(TT):
                for n in range(last3, MIX_TILES):
                    ins = out_products(n, t, s0 + n)
                ins.then_inc(y_full, 1)


INV = [THETA ** (-np.arange(half, dtype=np.float64) / half)
       for THETA, half in ((RET_THETA, RET_QK // 2), (NSA_THETA, ROT_DIM // 2))]


def frequencies():
    f = np.zeros((P, 4), np.float32)
    for v, (inv, half) in enumerate(zip(INV, (RET_QK // 2, ROT_DIM // 2))):
        row = np.arange(P)
        f[:, 2 * v] = inv[row % half]
        f[:, 2 * v + 1] = inv[row % half] * np.where(row // half % 2 == 0, -1.0, 1.0)
    return f


def column_slabs(w, starts):
    v = w.reshape(KT, P, -1)
    return np.stack([v[:, :, c:c + P].transpose(1, 0, 2).reshape(P, D) for c in starts])


def kernel(x, mem, positions, norm_pre, w_in, cmp_pos_k, cmp_w1_k, cmp_w2_k, cmp_pos_v, cmp_w1_v, cmp_w2_v,
           ret_gn, mem_norm, w_mem_kv, w_out, norm_post):
    import concourse.bacc as bacc
    from concourse.bass_utils import run_bass_kernel_spmd

    w_in, w_mem_kv, w_out = (np.asarray(a)[0] for a in (w_in, w_mem_kv, w_out))
    start = {"memq": lambda n: C_MQ + n * P, "retq": lambda n: C_RQ + n * P, "retk": lambda n: C_RK + n * P,
             "kc": lambda n: kv_col(0, 0, n), "vc": lambda n: kv_col(0, 1, n), "ks": lambda n: kv_col(1, 0, n),
             "kw": lambda n: kv_col(2, 0, n), "q": lambda n: C_Q + n * P, "gate": lambda n: C_GATE + n * P}
    w_proj = column_slabs(w_in, [start[k](n) for k, n in SLABS if k in start])
    pieces = []
    for v, c0 in enumerate((kv_col(1, 1, 0), kv_col(2, 1, 0), C_RV, C_RV + VC)):
        cols = np.r_[c0:c0 + VC, C_G + v * GC:C_G + (v + 1) * GC]
        w = w_in[:, cols].reshape(2, 4, P, VW)
        pieces += [w[f].transpose(1, 0, 2).reshape(P, SLAB) for f in range(2)]
    w_val = np.stack(pieces)
    half = MEM_HEADS * DH
    w_mem = np.concatenate([
        column_slabs(w_mem_kv, [h * DH for h in range(MEM_HEADS)]),
        w_mem_kv[:, half:].reshape(4, 2, P, half).transpose(0, 2, 1, 3).reshape(4, P, D)])
    w_cmp = np.concatenate([np.asarray(w)[0].reshape(8, W1_C, P, CMP_HIDDEN).transpose(0, 2, 1, 3).reshape(8, P, D)
                            for w in (cmp_w1_k, cmp_w1_v)])
    w_o = np.stack([w_out[t * P:(t + 1) * P] for t in OUT_ORDER])
    small = np.concatenate(
        [np.asarray(a)[0].reshape(-1, P).T for a in (norm_pre, mem_norm, ret_gn)] + [frequencies()]
        + [np.asarray(a)[0].T for a in (cmp_pos_k, cmp_pos_v)]
        + [np.asarray(a)[0].reshape(2, P, DH).transpose(1, 0, 2).reshape(P, 2 * DH) for a in (cmp_w2_k, cmp_w2_v)], axis=1)
    arrays = {"x_in": np.asarray(x)[0], "mem_in": np.asarray(mem)[0], "positions_in": np.asarray(positions)[0],
              "small_in": small, "gpost_in": np.asarray(norm_post)[0], "w_proj_in": w_proj, "w_val_in": w_val,
              "w_mem_in": w_mem, "w_cmp_in": w_cmp, "w_out_in": w_o}
    arrays = {k: np.ascontiguousarray(a) for k, a in arrays.items()}
    nc = bacc.Bacc("TRN2", target_bir_lowering=False, num_devices=1)
    args = [nc.dram_tensor(k, a.shape, mybir.dt.from_np(a.dtype), kind="ExternalInput").ap() for k, a in arrays.items()]
    out = nc.dram_tensor("y_out", (T, D), F32, kind="ExternalOutput").ap()
    build(nc, *args, out)
    r = run_bass_kernel_spmd(nc, [arrays], core_ids=[0])
    return r.results[0]["y_out"].reshape(1, T, D)
```

```python
import math
from contextlib import ExitStack

import numpy as np
import concourse.bass as bass
from concourse import mybir

F32 = mybir.dt.float32
F32R = mybir.dt.float32r
I32 = mybir.dt.int32
ACT = mybir.ActivationFunctionType
ALU = mybir.AluOpType
AX = mybir.AxisListType

P = 128
D = 1024
T = 512
MEM = 256
EPS = 1e-6
DH = 128
GROUPS, PER_GROUP = 2, 4
HEADS = GROUPS * PER_GROUP
RET_HEADS, RET_QK, RET_V = 4, 64, 128
MEM_HEADS = 4
CMP_BLOCK, CMP_STRIDE, CMP_HIDDEN = 32, 16, 256
N_CMP = (T - CMP_BLOCK) // CMP_STRIDE + 1
CMP_COLS = 32
ROT_DIM = DH // 4
NSA_THETA, RET_THETA = 500000.0, 10000.0
SCALE = DH ** -0.5
NEG = -1e30
KT = D // P
TT = T // P
MT = MEM // P
MIX_TILES = HEADS + RET_HEADS + MEM_HEADS
NSA0, RET0, MEM0 = 0, HEADS, HEADS + RET_HEADS
VP = 4
VC = 256
GC = 3 * HEADS // VP
VW = VC + GC
SLAB = 4 * VW
RING = 3
LEAD = 2
KEYS = CMP_COLS + 2 * T
W1_C = 4
BLK_N = GROUPS * N_CMP
BLK_W = CMP_BLOCK * BLK_N + (P - BLK_N)
OUT_ORDER = [*range(RET0, MIX_TILES), *range(NSA0, RET0)]

C_Q, C_KV, C_G = 0, HEADS * DH, HEADS * DH + 6 * GROUPS * DH
C_RQ = C_G + 3 * HEADS
C_RK = C_RQ + RET_HEADS * RET_QK
C_RV = C_RK + RET_HEADS * RET_QK
C_MQ = C_RV + RET_HEADS * RET_V
C_GATE = C_MQ + MEM_HEADS * DH


def kv_col(branch, kv, group):
    return C_KV + ((branch * 2 + kv) * GROUPS + group) * DH


S_GPRE, S_GMEM, S_GN = 0, KT, 2 * KT
S_FREQ = S_GN + RET_HEADS
S_POS = S_FREQ + 4
S_W2 = S_POS + 2 * CMP_BLOCK
S_COLS = S_W2 + 2 * 2 * DH


def schedule():
    s = [("norm", "mem", 0)]
    s += [("slab", "memk", h) for h in range(MEM_HEADS)]
    s += [("slab", "memv", v) for v in range(4)]
    s += [("norm", "x", 0)]
    s += [("slab", "v", v) for v in range(2 * VP)]
    s += [("slab", "memq", h) for h in range(MEM_HEADS)]
    for u, (kind, n) in enumerate([("retq", 0), ("retq", 1), ("retk", 0), ("retk", 1)]):
        s += [("mem", "att", 2 * u), ("mem", "att", 2 * u + 1), ("slab", kind, n)]
    s += [("mem", "flush", 0)]
    for h, (kind, n) in enumerate([("kc", 0), ("kc", 1), ("vc", 0), ("vc", 1)]):
        s += [("ret", "scores", h), ("slab", kind, n), ("ret", "values", h)]
        if h:
            s += [("ret", "turn", h - 1)]
    s += [("blocks", "k", 0), ("slab", "ks", 0), ("ret", "turn", RET_HEADS - 1), ("slab", "ks", 1)]
    for n, fill in enumerate([("kw", 0), ("kw", 1), ("gate", MEM0), None]):
        s += [("slab", "w1k", 2 * n), ("slab", "w1k", 2 * n + 1)] + ([("slab", *fill)] if fill else [])
    s += [("blocks", "v", 0), ("slab", "gate", MEM0 + 1), ("mlp", "k", 0)]
    for n, fill in enumerate([("gate", MEM0 + 2), ("gate", MEM0 + 3), ("q", 0), ("q", 1)]):
        s += [("slab", "w1v", 2 * n), ("slab", "w1v", 2 * n + 1), ("slab", *fill)]
    s += [("mlp", "v", 0), ("slab", "q", 2), ("slab", "q", 3), ("slab", "gate", RET0)]
    fill = {p: ("q", PER_GROUP + p) for p in range(4)}
    fill |= {4 + n: ("gate", RET0 + 1 + n) for n in range(3)}
    fill |= {p: ("gate", NSA0 + n) for n, p in enumerate((9, 10, 12, 14))}
    for p in range(GROUPS * TT * 2):
        s += [("pair", "att", p)]
        if p in fill:
            s += [("slab", *fill[p])]
    s += [("pair", "flush", 0)]
    s += [("slab", "gate", NSA0 + h) for h in range(PER_GROUP, HEADS)]
    s += [("slab", "out", n) for n in range(MIX_TILES)]
    return s


SCHEDULE = schedule()
SLABS = [(kind, n) for what, kind, n in SCHEDULE if what == "slab"]
PAIRS = GROUPS * TT * 2


def pair_of(p):
    return p // (2 * TT), p // 2 % TT, 2 * (p % 2)


def parts_of_step(kind, n, hh):
    if kind == "flush":
        return [(PAIRS - 2, 1), (PAIRS - 1, 0), (PAIRS - 1, 1)][hh]
    p, part = (n - 2, 1) if hh == 0 else (n - 1, 0)
    return (p, part) if p >= 0 else None


def blocks_of_part(p, part):
    i = pair_of(p)[1]
    cut = (i + 1) // 2
    return [-1, *range(cut)] if part == 0 else list(range(cut, i + 1))


def count_uses():
    t = o = 0
    t_used, o_used = {}, {}
    for what, kind, n in SCHEDULE:
        if what == "mem":
            if kind == "flush" or n:
                t, o = t + 1, o + 1
        elif what == "ret":
            t += {"scores": TT, "values": 0, "turn": 1}[kind]
            o += kind == "values"
        elif what == "mlp":
            t += 2
        elif what == "slab" and kind in ("w1k", "w1v") and n == 0:
            o += 1
        elif what == "pair":
            for hh in range(3 if kind == "flush" else 2):
                if (pp := parts_of_step(kind, n, hh)):
                    t, o = t + len(blocks_of_part(*pp)), o + pp[1]
        t_used[what, kind, n], o_used[what, kind, n] = t, o
    return t_used, o_used


T_USED, O_USED = count_uses()
PJ_KINDS = ("memk", "memq", "retq", "retk", "kc", "vc", "ks", "kw", "q", "gate")


def slab_words(kind):
    return SLAB if kind == "v" else D


def build(nc, x, mem, positions, small, gpost, w_proj, w_val, w_mem, w_cmp, w_out, out):
    ctx = ExitStack()
    with ctx:
        at = [16512]

        def sb(name, shape, dt=F32, offset=None):
            size = 4 * int(np.prod(shape[1:]))
            if offset is None:
                offset = at[0]
                at[0] += (size + 31) // 32 * 32
            return nc.alloc_sbuf_tensor_at(name, shape, dt, offset=offset)

        def sem(name):
            return ctx.enter_context(nc.semaphore(name))

        h_hi, h_lo = (sb(f"h_{p}", [P, KT, T], F32R) for p in ("hi", "lo"))
        slab_raw = [sb(f"slab_raw{i}", [P, SLAB]) for i in range(RING)]
        slab_hi = [sb(f"slab_hi{i}", [P, SLAB], F32R) for i in range(RING)]
        slab_lo = [sb(f"slab_lo{i}", [P, SLAB], F32R) for i in range(RING)]
        mixed_at = at[0]
        mixed = sb("mixed", [P, MIX_TILES, T])
        keys_at = at[0]
        keys_hi, keys_lo = (sb(f"keys_{p}", [P, GROUPS, KEYS], F32R) for p in ("hi", "lo"))
        v_hi, v_lo = (sb(f"v_{p}", [P, TT, 2 * VC], F32R) for p in ("hi", "lo"))
        vc_hi, vc_lo = (sb(f"vc_{p}", [P, GROUPS, DH], F32R) for p in ("hi", "lo"))
        par = sb("par", [P, S_COLS])
        ident = sb("ident", [P, P])
        masks = sb("masks", [P, TT * CMP_COLS + 2 * P])
        gates = sb("gates", [P, TT, 3 * HEADS])
        gate_t = sb("gate_t", [P, TT, GC])
        nsa_rot = sb("nsa_rot", [P, 2, T])
        sumsq = sb("sumsq", [P, 16])
        meansq = sb("meansq", [P, 16])
        rstd = sb("rstd", [P, 16])
        power = sb("power", [P, 4])
        smax = sb("smax", [P, 2, 4])
        nbias = sb("nbias", [P, 2, 4])
        ssum = sb("ssum", [P, 2, 4])
        coef = sb("coef", [P, 2, 4])
        bn = sb("bn", [P, TT, 6])
        mv = sb("mv", [P, TT, 2])
        swp = sb("swp", [32, T])
        region = at[0]

        q_at = region
        p_at = q_at + 2 * HEADS * T * 4
        pt_at = p_at + 2 * 2 * KEYS * 4
        z_at = pt_at + 4 * T * 4
        assert z_at + 2 * T * 4 <= 229344, z_at + 2 * T * 4
        q_hi = sb("q_hi", [P, HEADS, T], F32R, q_at)
        q_lo = sb("q_lo", [P, HEADS, T], F32R, q_at + HEADS * T * 4)
        prob = [sb(f"prob{i}", [P, 2, KEYS], F32, p_at + i * 2 * KEYS * 4) for i in range(2)]
        pt_hi = [sb(f"pt_hi{i}", [P, T], F32R, pt_at + i * T * 4) for i in range(2)]
        pt_lo = [sb(f"pt_lo{i}", [P, T], F32R, pt_at + (2 + i) * T * 4) for i in range(2)]
        z = [sb(f"z{i}", [P, T], F32, z_at + i * T * 4) for i in range(2)]
        x_nat = sb("x_nat", [P, TT, D], F32, mixed_at)
        mem_nat = sb("mem_nat", [P, MT, D], F32, mixed_at + TT * D * 4)
        square = sb("square", [P, D], F32, mixed_at + (TT + MT) * D * 4)
        posi = sb("posi", [P, T], I32, q_at + 16384)
        posf = sb("posf", [P, T], F32, q_at + 16384 + 2048)
        ang = sb("ang", [P, T], F32, q_at + 16384 + 4096)
        turns = sb("turns", [P, T], F32, q_at + 16384 + 6144)
        m_hi = sb("m_hi", [P, KT, MEM], F32R, q_at)
        m_lo = sb("m_lo", [P, KT, MEM], F32R, q_at + KT * MEM * 4)
        mq_hi = sb("mq_hi", [P, MEM_HEADS, T], F32R, q_at + 16384)
        mq_lo = sb("mq_lo", [P, MEM_HEADS, T], F32R, q_at + 24576)
        mk_hi = sb("mk_hi", [P, MEM_HEADS, MEM], F32R, keys_at)
        mk_lo = sb("mk_lo", [P, MEM_HEADS, MEM], F32R, keys_at + 4096)
        mv_hi = sb("mv_hi", [P, MT, T], F32R, keys_at + 8192)
        mv_lo = sb("mv_lo", [P, MT, T], F32R, keys_at + 12288)
        mprob = [sb(f"mprob{i}", [P, 2, MEM], F32, p_at + i * 2048) for i in range(2)]
        decay = sb("decay", [P, RET_HEADS, T], F32, mixed_at)
        decay_i = sb("decay_i", [P, T], I32, mixed_at + 16384)
        ret_v = sb("ret_v", [P, TT, RET_HEADS * RET_V], F32, mixed_at + 8192)
        ret_q = sb("ret_q", [P, RET_HEADS, T], F32, q_at)
        ret_k = sb("ret_k", [P, 2, T], F32, q_at + 8192)
        ret_rot = sb("ret_rot", [P, 2, T], F32, p_at + 12288)
        ret_z = sb("ret_z", [P, T], F32, q_at + 12288)
        inner = [sb(f"inner{i}", [P, 1280], F32, q_at + 16384 + i * 5120) for i in range(2)]
        ret_n = [sb(f"ret_n{i}", [P, TT, RET_V], F32, q_at + 26624 + i * 2048) for i in range(2)]
        z_cmp = sb("z_cmp", [P, 4, T], F32, p_at + 4096)
        blk = sb("blk", [P, BLK_W], F32, q_at)
        blk_hi = sb("blk_hi", [P, BLK_W], F32R, q_at + 8224)
        blk_lo = sb("blk_lo", [P, BLK_W], F32R, q_at + 16448)
        hid = sb("hid", [P, 4, CMP_HIDDEN], F32, p_at + 12288)
        hid_t = sb("hid_t", [P, 2, BLK_N], F32, q_at + 30720)
        mix_hi = [sb(f"mix_hi{i}", [P, T], F32R, q_at + i * 2048) for i in range(RING)]
        mix_lo = [sb(f"mix_lo{i}", [P, T], F32R, q_at + (RING + i) * 2048) for i in range(RING)]
        gpost_b = sb("gpost_b", [P, D], F32, q_at + 12288)
        x_res = sb("x_res", [P, TT, D], F32, q_at + 16384)
        y_sb = [sb(f"y_sb{i}", [P, D], F32, pt_at + i * D * 4) for i in range(2)]
        y_sq = sb("y_sq", [P, D], F32, z_at)

        ps = ctx.enter_context(nc.psum_tensor("ps", [P, 8, 512], F32))
        S_, O_, PJ_, T_ = 0, 3, 4, 6

        ld_mem, ld_x, ld_par, ld_pos = sem("ld_mem"), sem("ld_x"), sem("ld_par"), sem("ld_pos")
        ld_res, ld_post = sem("ld_res"), sem("ld_post")
        slab_loaded = [sem(f"slab_loaded{i}") for i in range(RING)]
        slab_hi_ready, slab_lo_ready, slab_used = sem("slab_hi_ready"), sem("slab_lo_ready"), sem("slab_used")
        pool_step, act_step, dve_step = sem("pool_step"), sem("act_step"), sem("dve_step")
        consts_ready = sem("consts_ready")
        squares_done = sem("squares_done")
        meansq_ready, rstd_ready = sem("meansq_ready"), sem("rstd_ready")
        normed = sem("normed")
        turned_mem, turned_x = sem("turned_mem"), sem("turned_x")
        mem_hi, x_hi, mem_lo, x_lo = sem("mem_hi"), sem("x_hi"), sem("mem_lo"), sem("x_lo")
        t_full, t_hi = sem("t_full"), sem("t_hi")
        t_drained = [sem("t_drained0"), sem("t_drained1")]
        pj_hi = sem("pj_hi")
        pj_drained = [sem("pj_drained0"), sem("pj_drained1")]
        memv_hi, memv_drained = sem("memv_hi"), sem("memv_drained")
        val_copied, val_tanh, val_drained = sem("val_copied"), sem("val_tanh"), sem("val_drained")
        angles_ready, rot_ready = sem("angles_ready"), sem("rot_ready")
        decay_iota, decay_exp, decay_ready = sem("decay_iota"), sem("decay_exp"), sem("decay_ready")
        s_full, s_drained, bias_ready, prob_ready = sem("s_full"), sem("s_drained"), sem("bias_ready"), sem("prob_ready")
        pv_done = sem("pv_done")
        ret_full, o_drained = sem("ret_full"), sem("o_drained")
        ret_swapped, ret_sin, ret_ready = sem("ret_swapped"), sem("ret_sin"), sem("ret_ready")
        rot_swapped, rot_turned, rot_hi = sem("rot_swapped"), sem("rot_turned"), sem("rot_hi")
        z_done = sem("z_done")
        ret_var, ret_rstd, ret_normed = sem("ret_var"), sem("ret_rstd"), sem("ret_normed")
        blk_sum, blk_hi_ready, blk_ready = sem("blk_sum"), sem("blk_hi_ready"), sem("blk_ready")
        hid_sq, hid_poly, hid_tanh, hid_ready = sem("hid_sq"), sem("hid_poly"), sem("hid_tanh"), sem("hid_ready")
        gate_tanh = sem("gate_tanh")
        mix_hi_ready, mix_ready = sem("mix_hi_ready"), sem("mix_ready")
        y_full, y_squared, y_meansq, y_rstd, y_ready, y_stored = (
            sem("y_full"), sem("y_squared"), sem("y_meansq"), sem("y_rstd"), sem("y_ready"),
            [sem(f"y_stored{t}") for t in range(TT)])

        block = ctx.enter_context(nc.Block())

        def turn_bank(kind, k):
            if kind == "mem":
                return ps[:, 4 + k // 2, k % 2 * MEM:(k % 2 + 1) * MEM]
            return ps[:, k, :]

        def wait_slab_used(e, kind, n):
            e.wait_ge(slab_used, SLABS.index((kind, n)) + 1)

        def wait_t_drained(e, uses):
            e.wait_ge(t_drained[0], (uses + 1) // 2)
            if uses >= 2:
                e.wait_ge(t_drained[1], uses // 2)

        def wait_pj_all_drained(e, uses):
            e.wait_ge(pj_drained[0], (uses + 1) // 2)
            e.wait_ge(pj_drained[1], uses // 2)

        def gated_by(t):
            return [s for s in SLABS if s[0] == "gate"].index(("gate", t)) + 1

        def wait_head_out(e, t):
            if t >= MEM0:
                step = ("mem", "flush", 0) if t == MIX_TILES - 1 else ("mem", "att", 2 * (t - MEM0) + 2)
                e.wait_ge(o_drained, O_USED[step])
            elif t >= RET0:
                k = T_USED["ret", "turn", t - RET0] - 1
                e.wait_ge(t_drained[k % 2], k // 2 + 1)
            else:
                p = (t // PER_GROUP * TT + TT - 1) * 2 + t % PER_GROUP // 2
                e.wait_ge(o_drained, O_USED[("pair", "att", p + 2) if p + 2 < PAIRS else ("pair", "flush", 0)])

        RET_PROJ = [("retq", 0), ("retq", 1), ("retk", 0), ("retk", 1)]
        Z_ORDER = [s for s in SLABS if s[0] in ("retq", "retk", "ks", "kw", "q", "gate")]
        ROT_ORDER = [s for s in SLABS if s[0] in ("kc", "ks", "kw", "q")]
        HI_ORDER = [s for s in SLABS if s[0] in ("ks", "kw", "q")]
        PJ_ORDER = [s for s in SLABS if s[0] in PJ_KINDS]
        Z_INDEX = {s: i for i, s in enumerate(Z_ORDER)}
        ROT_INDEX = {s: i for i, s in enumerate(ROT_ORDER)}
        HI_INDEX = {s: i for i, s in enumerate(HI_ORDER)}
        SPLIT_ORDER = [s for s in PJ_ORDER if s[0] in ("memk", "memq")]

        def wait_pj_drained(e, kind, n):
            j = PJ_ORDER.index((kind, n))
            e.wait_ge(pj_drained[j % 2], j // 2 + 1)

        def pj_bank(kind, n):
            return PJ_ + PJ_ORDER.index((kind, n)) % 2

        def z_key_dst(t_hi_or_lo, kind, n):
            if kind == "q":
                return (q_hi if t_hi_or_lo == "hi" else q_lo)[:, n, :]
            keys = keys_hi if t_hi_or_lo == "hi" else keys_lo
            v = keys[:, n, CMP_COLS:].rearrange("p (j b k) -> p b j k", b=2, k=P)
            return v[:, 0 if kind == "ks" else 1, :, :]

        def blocks_of(t):
            return t.rearrange("p (j k) -> p j k", k=P)

        @block.sync
        def _(sp):
            src = {}
            for i, s in enumerate([s for s in SLABS if s[0] in ("memq", "retq", "retk", "kc", "vc", "ks", "kw", "q", "gate")]):
                src[s] = w_proj[i]
            for v in range(2 * VP):
                src["v", v] = w_val[v]
            for h in range(MEM_HEADS):
                src["memk", h] = w_mem[h]
                src["memv", h] = w_mem[MEM_HEADS + h]
            for n in range(8):
                src["w1k", n] = w_cmp[n]
                src["w1v", n] = w_cmp[8 + n]
            for n in range(MIX_TILES):
                src["out", n] = w_out[n]
            for n, s in enumerate(SLABS):
                if s == ("out", 0):
                    sp.wait_ge(s_full, 2 * MEM_HEADS + 2 * PAIRS)
                    sp.dma_start(x_res[:, :, :], x.rearrange("(t p) d -> p t d", p=P)).then_inc(ld_res, 16)
                    sp.dma_start(gpost_b[:, :], gpost.partition_broadcast(P)).then_inc(ld_post, 16)
                if n >= RING:
                    sp.wait_ge(slab_lo_ready, n - RING + 1)
                w = slab_words(s[0])
                sp.dma_start(slab_raw[n % RING][:, 0:w], src[s]).then_inc(slab_loaded[n % RING], 16)
            for t in range(TT):
                sp.wait_ge(y_ready, t + 1)
                sp.dma_start(out[t * P:(t + 1) * P, :], y_sb[t % 2][:, :]).then_inc(y_stored[t], 16)
            for t in range(TT):
                sp.wait_ge(y_stored[t], 16)

        @block.gpsimd
        def _(pool):
            count = [0]

            def link(ins):
                count[0] += 1
                ins.then_inc(pool_step, 1)
                pool.wait_ge(pool_step, count[0])

            link(pool.memset(ident[:, :], 0.0))
            pool.affine_select(out=ident[:, :], in_=ident[:, :], compare_op=ALU.not_equal, fill=1.0, base=0,
                               pattern=[[-1, P]], channel_multiplier=1).then_inc(consts_ready, 1)
            pool.memset(power[:, :], -0.5).then_inc(consts_ready, 1)
            
            def power_of(dst, src, ready, n, signal):
                pool.wait_ge(ready, n)
                pool.wait_ge(consts_ready, 2)
                w = src.shape[-1]
                pool.tensor_tensor(dst, src, power[:, 0:w], ALU.pow).then_inc(signal, 1)

            power_of(rstd[:, 0:MT], meansq[:, 0:MT], meansq_ready, 1, rstd_ready)
            power_of(rstd[:, 2:2 + TT], meansq[:, 2:2 + TT], meansq_ready, 2, rstd_ready)
            link(pool.memset(masks[:, :], 0.0))
            cw = TT * CMP_COLS
            for i in range(TT):
                m = masks[:, (TT - 1 - i) * CMP_COLS:(TT - i) * CMP_COLS]
                pool.affine_select(out=m, in_=m, compare_op=ALU.is_ge, fill=NEG, base=i * P - (CMP_BLOCK - 1),
                                   pattern=[[-CMP_STRIDE, CMP_COLS]], channel_multiplier=1).then_inc(consts_ready, 1)
            m = masks[:, cw:]
            pool.affine_select(out=m, in_=m, compare_op=ALU.is_ge, fill=NEG, base=0,
                               pattern=[[0, 2], [-1, P]], channel_multiplier=1).then_inc(consts_ready, 1)
            pool.memset(vc_hi[:, :, :].bitcast(F32), 0.0).then_inc(consts_ready, 1)
            pool.memset(vc_lo[:, :, :].bitcast(F32), 0.0).then_inc(consts_ready, 1)
            pool.wait_ge(turned_x, KT)
            pool.iota(decay_i[:, :], [[1, T]], base=0, channel_multiplier=-1).then_inc(decay_iota, 1)
            wait_slab_used(pool, "memv", 3)
            pool.memset(ret_q[:, :, :], 0.0).then_inc(decay_ready, 1)
            pool.wait_ge(decay_exp, RET_HEADS)
            for h in range(RET_HEADS):
                pool.affine_select(out=decay[:, h, :], in_=decay[:, h, :], compare_op=ALU.is_ge, fill=0.0, base=0,
                                   pattern=[[1, T]], channel_multiplier=-1).then_inc(decay_ready, 1)
            for what, kind, n in SCHEDULE:
                if what == "slab" and kind in ("retq", "retk"):
                    i = RET_PROJ.index((kind, n))
                    t = z[Z_INDEX[kind, n] % 2]
                    pool.wait_ge(ret_swapped, 4 * (i + 1))
                    pool.wait_ge(rot_ready, 10)
                    pool.tensor_tensor(t[:, :], t[:, :], ret_rot[:, 1, :], ALU.mult).then_inc(ret_sin, 1)
                elif what == "slab" and kind in ("kc", "ks", "kw", "q"):
                    r = ROT_INDEX[kind, n]
                    t = z_cmp[0:32, n, :] if kind == "kc" else z[Z_INDEX[kind, n] % 2][0:32, :]
                    w = swp[:, :]
                    pool.wait_ge(rot_swapped, r + 1)
                    link(pool.tensor_tensor(w, w, nsa_rot[0:32, 1, :], ALU.mult))
                    link(pool.tensor_tensor(t, t, nsa_rot[0:32, 0, :], ALU.mult))
                    pool.tensor_tensor(t, t, w, ALU.add).then_inc(rot_turned, 1)
                elif (what, kind) == ("ret", "values"):
                    power_of(rstd[:, 6:6 + TT], meansq[:, 6:6 + TT], ret_var, n + 1, ret_rstd)
            for t in range(TT):
                power_of(rstd[:, 10 + t:11 + t], meansq[:, 10 + t:11 + t], y_meansq, t + 1, y_rstd)

        @block.scalar
        def _(act):
            count = [0]

            def link(ins):
                count[0] += 1
                ins.then_inc(act_step, 1)
                act.wait_ge(act_step, count[0])

            act.dma_start(mem_nat[:, :, :], mem.rearrange("(t p) d -> p t d", p=P)).then_inc(ld_mem, 16)
            act.dma_start(par[:, :], small).then_inc(ld_par, 16)
            act.dma_start(posi[:, :], positions.partition_broadcast(P)).then_inc(ld_pos, 16)
            act.dma_start(x_nat[:, :, :], x.rearrange("(t p) d -> p t d", p=P)).then_inc(ld_x, 16)
            n_split = [0]

            def split():
                n = n_split[0]
                if n == len(SLABS):
                    return
                n_split[0] += 1
                act.wait_ge(slab_loaded[n % RING], 16 * (n // RING + 1))
                if n >= RING:
                    act.wait_ge(slab_used, n - RING + 1)
                w = slab_words(SLABS[n][0])
                act.activation(slab_hi[n % RING][:, 0:w], slab_raw[n % RING][:, 0:w], ACT.Copy).then_inc(slab_hi_ready, 1)

            t_uses, s_uses, o_uses, z_uses, pvs = [0], [0], [0], [0], [0]
            t_marks = []

            def take_t():
                k = t_uses[0]
                t_uses[0] += 1
                act.wait_ge(t_full, k + 1)
                return k

            def turned_block(w):
                k = take_t()
                if pvs[0] >= 2:
                    act.wait_ge(pv_done, pvs[0] - 1)
                pvs[0] += 1
                act.activation(pt_hi[k % 2][:, 0:w], ps[:, T_ + k % 2, 0:w], ACT.Copy).then_inc(t_hi, 1)

            def head_out(dst, src):
                o_uses[0] += 1
                act.wait_ge(pv_done, pvs[0])
                act.activation(dst, src, ACT.Copy).then_inc(o_drained, 1)

            def mem_exps(u):
                s_uses[0] += 1
                act.wait_ge(bias_ready, s_uses[0])
                if u >= 2:
                    act.wait_ge(t_full, t_marks[u - 2])
                for qt in range(2):
                    ins = act.activation(mprob[u % 2][:, qt, :], ps[:, S_, qt * MEM:(qt + 1) * MEM], ACT.Exp,
                                         bias=nbias[:, u % 2, qt:qt + 1], scale=SCALE, accum_out=ssum[:, u % 2, qt:qt + 1])
                ins.then_inc(s_drained, 1)

            def mem_turned(u):
                turned_block(T)
                t_marks.append(t_uses[0])

            def mem_out(u):
                h, half = u // 2, u % 2
                head_out(mixed[:, MEM0 + h, half * 2 * P:(half + 1) * 2 * P], ps[:, O_, 0:2 * P])

            def head_exps(p, hh):
                _, i, _ = pair_of(p)
                u = s_uses[0]
                s_uses[0] += 1
                act.wait_ge(bias_ready, u + 1)
                if p == 0 and hh == 0:
                    act.wait_ge(t_full, t_uses[0])
                    act.wait_ge(pv_done, pvs[0])
                if hh == 0 and p >= 2:
                    act.wait_ge(t_full, t_marks[p - 2])
                o = prob[p % 2][:, hh, :]
                ob = o[:, CMP_COLS:CMP_COLS + 2 * P * (i + 1)].rearrange("p (j b k) -> p b j k", b=2, k=P)
                flat = ps[:, 0:3, :].rearrange("p s c -> p (s c)")
                sbk = flat[:, 256:256 + 2 * P * (i + 1)].rearrange("p (j b k) -> p b j k", b=2, k=P)
                act.activation(o[:, 0:CMP_COLS], flat[:, 224:256], ACT.Exp, bias=nbias[:, u % 2, 0:1], scale=SCALE,
                               accum_out=ssum[:, u % 2, 0:1])
                for b in range(2):
                    ins = act.activation(ob[:, b, :, :], sbk[:, b, :, :], ACT.Exp, bias=nbias[:, u % 2, 1 + b:2 + b],
                                         scale=SCALE, accum_out=ssum[:, u % 2, 1 + b:2 + b])
                ins.then_inc(s_drained, 1)

            def pair_turned(p, part):
                for j in blocks_of_part(p, part):
                    turned_block(2 * P if j < 0 else T)
                if part == 1:
                    t_marks.append(t_uses[0])

            def pair_out(p):
                g, i, h0 = pair_of(p)
                m0 = NSA0 + PER_GROUP * g + h0
                head_out(mixed[:, m0:m0 + 2, i * P:(i + 1) * P], ps[:, O_, 0:2 * P].rearrange("p (h q) -> p h q", h=2))

            pending = []

            def finish_rot():
                if not pending:
                    return
                kind, n = pending.pop()
                if kind == "kc":
                    return
                act.wait_ge(rot_turned, ROT_INDEX[kind, n] + 1)
                src = z[Z_INDEX[kind, n] % 2][:, :]
                dst = z_key_dst("hi", kind, n)
                act.activation(dst, src if kind == "q" else blocks_of(src), ACT.Copy).then_inc(rot_hi, 1)

            def take_z():
                k = z_uses[0]
                z_uses[0] += 1
                if k >= 2:
                    act.wait_ge(z_done, k - 1)
                return z[k % 2]

            def project(kind, n):
                if kind in ("memk", "memq"):
                    wait_slab_used(act, kind, n)
                    src, dst = ps[:, pj_bank(kind, n), :], mq_hi[:, n, :]
                    if kind == "memk":
                        src, dst = src[:, 0:MEM], mk_hi[:, n, :]
                    act.activation(dst, src, ACT.Copy).then_inc(pj_hi, 1)
                elif kind == "memv" and n == 3:
                    wait_slab_used(act, "memv", 3)
                    act.activation(mv_hi[:, :, :], ps[:, S_:S_ + 2, :], ACT.Copy).then_inc(memv_hi, 1)
                elif kind == "v" and n % 2:
                    piece = n // 2
                    bank = 4 * (piece % 2)
                    wait_slab_used(act, "v", n)
                    src = ps[:, bank:bank + 4, :]
                    if piece < 2:
                        act.activation(v_hi[:, :, piece * VC:(piece + 1) * VC], src[:, :, 0:VC], ACT.Copy).then_inc(val_copied, 1)
                    else:
                        act.activation(ret_v[:, :, (piece - 2) * VC:(piece - 1) * VC], src[:, :, 0:VC], ACT.Copy).then_inc(val_copied, 1)
                    if piece:
                        act.wait_ge(val_drained, piece)
                    act.activation(gate_t[:, :, :], src[:, :, VC:VW], ACT.Tanh, scale=0.5).then_inc(val_tanh, 1)
                elif kind in ("retq", "retk"):
                    wait_slab_used(act, kind, n)
                    t = take_z()
                    for b in range(4):
                        act.activation(t[32 * b:32 * b + 32, :], ps[32 * (b ^ 1):32 * (b ^ 1) + 32, pj_bank(kind, n), :],
                                       ACT.Copy).then_inc(ret_swapped, 1)
                elif kind in ("kc", "vc", "ks", "kw", "q"):
                    wait_slab_used(act, kind, n)
                    if kind in ("kc", "vc"):
                        dst = z_cmp[:, (2 if kind == "vc" else 0) + n, :]
                    else:
                        dst = take_z()[:, :]
                    j = PJ_ORDER.index((kind, n))
                    act.activation(dst, ps[:, PJ_ + j % 2, :], ACT.Copy).then_inc(pj_drained[j % 2], 1)
                    finish_rot()
                    if kind != "vc":
                        pending.append((kind, n))
                elif kind == "gate":
                    finish_rot()
                    wait_slab_used(act, kind, n)
                    t = take_z()
                    act.activation(t[:, :], ps[:, pj_bank(kind, n), :], ACT.Tanh, scale=0.5).then_inc(gate_tanh, 1)

            def mixed_hi(n):
                if n >= RING:
                    act.wait_ge(slab_used, SLABS.index(("out", 0)) + n - RING + 1)
                t = OUT_ORDER[n]
                act.wait_ge(z_done, Z_INDEX["gate", t] + 1)
                act.activation(mix_hi[n % RING][:, :], mixed[:, t, :], ACT.Copy).then_inc(mix_hi_ready, 1)

            act.wait_ge(angles_ready, 1)
            for b in range(4):
                act.activation(ret_rot[32 * b:32 * b + 32, 0, :], ang[0:32, :], ACT.Sin).then_inc(rot_ready, 1)
                act.activation(ret_rot[32 * b:32 * b + 32, 1, :], ang[32:64, :], ACT.Sin,
                               scale=1.0 if b % 2 else -1.0).then_inc(rot_ready, 1)
            for v in range(2):
                act.activation(nsa_rot[0:32, v, :], ang[64 + 32 * v:96 + 32 * v, :], ACT.Sin).then_inc(rot_ready, 1)
            for _ in range(LEAD):
                split()
            for what, kind, n in SCHEDULE:
                if what == "norm":
                    gain = S_GMEM if kind == "mem" else S_GPRE
                    hi = m_hi if kind == "mem" else h_hi
                    if kind == "mem":
                        act.wait_ge(ld_mem, 16)
                        for r in range(MT):
                            if r:
                                act.wait_ge(squares_done, r)
                            act.activation(square[:, :], mem_nat[:, r, :], ACT.Square,
                                           accum_out=sumsq[:, r:r + 1]).then_inc(squares_done, 1)
                        act.wait_ge(ld_par, 16)
                    for k in range(KT):
                        src = turn_bank(kind, k)
                        if kind == "mem":
                            act.wait_ge(turned_mem, k // 2 + 1)
                            if k % 2:
                                act.wait_ge(mem_lo, k)
                        else:
                            act.wait_ge(turned_x, k + 1)
                        act.activation(hi[:, k, :], src, ACT.Copy,
                                       scale=par[:, gain + k:gain + k + 1]).then_inc(mem_hi if kind == "mem" else x_hi, 1)
                    if kind == "x":
                        act.wait_ge(decay_iota, 1)
                        for h in range(RET_HEADS):
                            act.activation(decay[:, h, :], decay_i[:, :], ACT.Exp,
                                           scale=math.log1p(-(2.0 ** (-5 - h)))).then_inc(decay_exp, 1)
                elif what == "slab":
                    split()
                    if kind != "out":
                        project(kind, n)
                    elif n + LEAD < MIX_TILES:
                        mixed_hi(n + LEAD)
                elif what == "mem" and kind == "att":
                    if n:
                        mem_turned(n - 1)
                    mem_exps(n)
                    if n:
                        mem_out(n - 1)
                elif what == "mem":
                    mem_turned(2 * MEM_HEADS - 1)
                    mem_out(2 * MEM_HEADS - 1)
                    t_marks.clear()
                elif what == "rot":
                    finish_rot()
                elif (what, kind) == ("ret", "scores"):
                    t_uses[0] += TT
                elif (what, kind) == ("ret", "values"):
                    o_uses[0] += 1
                elif (what, kind) == ("ret", "turn"):
                    k = take_t()
                    act.activation(mixed[:, RET0 + n, :], ps[:, T_ + k % 2, :], ACT.Copy,
                                   scale=par[:, S_GN + n:S_GN + n + 1]).then_inc(t_drained[k % 2], 1)
                elif what == "blocks":
                    i = 0 if kind == "k" else 1
                    act.wait_ge(blk_sum, i + 1)
                    if i:
                        wait_slab_used(act, "w1k", 7)
                    act.activation(blk_hi[:, :], blk[:, :], ACT.Copy).then_inc(blk_hi_ready, 1)
                elif what == "mlp":
                    i = 0 if kind == "k" else 1
                    o_uses[0] += 1
                    wait_slab_used(act, "w1" + kind, 7)
                    if i:
                        act.wait_ge(t_full, t_uses[0])
                    act.activation(hid[0:BLK_N, 0, :], ps[0:BLK_N, O_, 0:CMP_HIDDEN], ACT.Copy).then_inc(o_drained, 1)
                    act.wait_ge(o_drained, o_uses[0])
                    act.activation(hid[0:BLK_N, 1, :], hid[0:BLK_N, 0, :], ACT.Square).then_inc(hid_sq, 1)
                    act.wait_ge(hid_poly, i + 1)
                    act.activation(hid[0:BLK_N, 3, :], hid[0:BLK_N, 2, :], ACT.Tanh,
                                   scale=math.sqrt(2.0 / math.pi)).then_inc(hid_tanh, 1)
                    k = take_t()
                    act.activation(hid_t[:, :, :], ps[:, T_ + k % 2, 0:2 * P].rearrange("p (c r) -> p c r", c=2)[:, :, 0:BLK_N],
                                   ACT.Copy, scale=0.5).then_inc(t_drained[k % 2], 1)
                    k = take_t()
                    if kind == "k":
                        act.activation(keys_hi[:, :, 0:N_CMP], ps[:, T_ + k % 2, 0:BLK_N].rearrange("p (g n) -> p g n", g=2),
                                       ACT.Copy).then_inc(t_hi, 1)
                    else:
                        act.activation(vc_hi[0:N_CMP, :, :], ps[0:N_CMP, T_ + k % 2, 0:2 * P].rearrange("p (g n) -> p g n", g=2),
                                       ACT.Copy).then_inc(t_hi, 1)
                elif what == "pair" and kind == "att":
                    for hh in range(2):
                        pp = parts_of_step(kind, n, hh)
                        if pp:
                            pair_turned(*pp)
                        head_exps(n, hh)
                        if pp and pp[1]:
                            pair_out(pp[0])
                elif what == "pair":
                    for hh in range(3):
                        pp = parts_of_step(kind, n, hh)
                        pair_turned(*pp)
                        if pp[1]:
                            pair_out(pp[0])
                    for m in range(LEAD):
                        mixed_hi(m)
            for t in range(TT):
                act.wait_ge(y_full, t + 1)
                if t:
                    act.wait_ge(y_squared, t)
                act.activation(y_sq[:, :], ps[:, 2 * t:2 * t + 2, :].rearrange("p h c -> p (h c)"), ACT.Square,
                               accum_out=sumsq[:, 10 + t:11 + t]).then_inc(y_squared, 1)

        @block.vector
        def _(dve):
            count = [0]

            def link(ins):
                count[0] += 1
                ins.then_inc(dve_step, 1)
                dve.wait_ge(dve_step, count[0])

            n_split = [0]

            def split():
                n = n_split[0]
                if n == len(SLABS):
                    return
                n_split[0] += 1
                dve.wait_ge(slab_hi_ready, n + 1)
                w = slab_words(SLABS[n][0])
                dve.tensor_tensor(slab_lo[n % RING][:, 0:w], slab_raw[n % RING][:, 0:w],
                                  slab_hi[n % RING][:, 0:w].bitcast(F32), ALU.subtract).then_inc(slab_lo_ready, 1)

            t_uses, t_his, s_uses, z_uses = [0], [0], [0], [0]

            def take_t_hi():
                k = t_uses[0]
                t_uses[0] += 1
                t_his[0] += 1
                dve.wait_ge(t_hi, t_his[0])
                return k

            def turned_block(w):
                k = take_t_hi()
                dve.tensor_tensor(pt_lo[k % 2][:, 0:w], ps[:, T_ + k % 2, 0:w], pt_hi[k % 2][:, 0:w].bitcast(F32),
                                  ALU.subtract).then_inc(t_drained[k % 2], 1)

            def norm_rows(nat, r0, nr, part):
                dve.wait_ge(squares_done, MT)
                dve.tensor_scalar(meansq[:, r0:r0 + nr], sumsq[:, r0:r0 + nr], 1.0 / D, EPS, ALU.mult,
                                  ALU.add).then_inc(meansq_ready, 1)
                dve.wait_ge(rstd_ready, part)
                for r in range(nr):
                    dve.tensor_scalar(nat[:, r, :], nat[:, r, :], rstd[:, r0 + r:r0 + r + 1], None,
                                      ALU.mult).then_inc(normed, 1)

            def mem_front(u):
                s_uses[0] += 1
                dve.wait_ge(s_full, s_uses[0])
                link(dve.tensor_reduce(smax[:, u % 2, 0:2], ps[:, S_, :].rearrange("p (q k) -> p q k", q=2), AX.X, ALU.max))
                dve.tensor_scalar(nbias[:, u % 2, 0:2], smax[:, u % 2, 0:2], -SCALE, None, ALU.mult).then_inc(bias_ready, 1)

            def mem_back(u):
                dve.wait_ge(s_drained, s_uses[0])
                link(dve.reciprocal(coef[:, u % 2, 0:2], ssum[:, u % 2, 0:2]))
                for qt in range(2):
                    ins = dve.tensor_scalar(mprob[u % 2][:, qt, :], mprob[u % 2][:, qt, :], coef[:, u % 2, qt:qt + 1],
                                            None, ALU.mult)
                ins.then_inc(prob_ready, 1)

            def head_front(p, hh):
                g, i, h0 = pair_of(p)
                u = s_uses[0]
                s_uses[0] += 1
                if p == 0 and hh == 0:
                    dve.wait_ge(consts_ready, 2 + TT + 1)
                dve.wait_ge(s_full, u + 1)
                flat = ps[:, 0:3, :].rearrange("p s c -> p (s c)")
                cw = TT * CMP_COLS
                if i == 0:
                    link(dve.tensor_tensor(flat[:, 224:512], flat[:, 224:512], masks[:, cw - CMP_COLS:cw + 2 * P], ALU.add))
                else:
                    m = masks[:, (TT - 1 - i) * CMP_COLS:(TT - i) * CMP_COLS]
                    dve.tensor_tensor(flat[:, 224:256], flat[:, 224:256], m, ALU.add)
                    d = flat[:, 256 + 2 * P * i:256 + 2 * P * (i + 1)]
                    link(dve.tensor_tensor(d, d, masks[:, cw:], ALU.add))
                dve.tensor_reduce(smax[:, u % 2, 0:1], flat[:, 224:256], AX.X, ALU.max)
                view = flat[:, 256:256 + 2 * P * (i + 1)].rearrange("p (j b k) -> p b j k", b=2, k=P)
                link(dve.tensor_reduce(smax[:, u % 2, 1:3], view, AX.XY, ALU.max))
                dve.tensor_scalar(nbias[:, u % 2, 0:3], smax[:, u % 2, 0:3], 0.1 * NEG, -SCALE, ALU.max,
                                  ALU.mult).then_inc(bias_ready, 1)

            def head_back(p, hh):
                g, i, h0 = pair_of(p)
                u = s_uses[0] - 1
                dve.wait_ge(s_drained, u + 1)
                head = PER_GROUP * g + h0 + hh
                c = coef[:, u % 2, 0:3]
                link(dve.tensor_scalar(c, ssum[:, u % 2, 0:3], 1e-30, None, ALU.max))
                link(dve.reciprocal(c, c))
                link(dve.tensor_tensor(c, c, gates[:, i, head:3 * HEADS:HEADS], ALU.mult))
                o = prob[p % 2][:, hh, :]
                ob = o[:, CMP_COLS:CMP_COLS + 2 * P * (i + 1)].rearrange("p (j b k) -> p b j k", b=2, k=P)
                dve.tensor_scalar(o[:, 0:CMP_COLS], o[:, 0:CMP_COLS], coef[:, u % 2, 0:1], None, ALU.mult)
                for b in range(2):
                    ins = dve.tensor_scalar(ob[:, b, :, :], ob[:, b, :, :], coef[:, u % 2, 1 + b:2 + b], None, ALU.mult)
                ins.then_inc(prob_ready, 1)

            pending = []

            def finish_rot():
                if not pending:
                    return
                kind, n = pending.pop()
                if kind == "kc":
                    return
                dve.wait_ge(rot_hi, HI_INDEX[kind, n] + 1)
                src = z[Z_INDEX[kind, n] % 2][:, :]
                hi, lo = z_key_dst("hi", kind, n), z_key_dst("lo", kind, n)
                dve.tensor_tensor(lo, src if kind == "q" else blocks_of(src), hi.bitcast(F32),
                                  ALU.subtract).then_inc(z_done, 1)

            def project(kind, n):
                if kind in ("memk", "memq"):
                    j = PJ_ORDER.index((kind, n))
                    dve.wait_ge(pj_hi, SPLIT_ORDER.index((kind, n)) + 1)
                    src, hi, lo = ps[:, PJ_ + j % 2, :], mq_hi[:, n, :], mq_lo[:, n, :]
                    if kind == "memk":
                        src, hi, lo = src[:, 0:MEM], mk_hi[:, n, :], mk_lo[:, n, :]
                    dve.tensor_tensor(lo, src, hi.bitcast(F32), ALU.subtract).then_inc(pj_drained[j % 2], 1)
                elif kind == "memv" and n == 3:
                    dve.wait_ge(memv_hi, 1)
                    dve.tensor_tensor(mv_lo[:, :, :], ps[:, S_:S_ + 2, :], mv_hi[:, :, :].bitcast(F32),
                                      ALU.subtract).then_inc(memv_drained, 1)
                elif kind == "v" and n % 2:
                    piece = n // 2
                    bank = 4 * (piece % 2)
                    if piece < 2:
                        c = slice(piece * VC, (piece + 1) * VC)
                        dve.wait_ge(val_tanh, piece + 1)
                        dve.tensor_tensor(v_lo[:, :, c], ps[:, bank:bank + 4, 0:VC], v_hi[:, :, c].bitcast(F32), ALU.subtract)
                    dve.wait_ge(val_tanh, piece + 1)
                    dve.tensor_scalar(gates[:, :, piece * GC:(piece + 1) * GC], gate_t[:, :, :], 1.0, 0.5, ALU.add,
                                      ALU.mult).then_inc(val_drained, 1)
                elif kind in ("retq", "retk"):
                    i = RET_PROJ.index((kind, n))
                    j = PJ_ORDER.index((kind, n))
                    dve.wait_ge(ret_swapped, 4 * (i + 1))
                    dve.wait_ge(rot_ready, 8)
                    if i == 0:
                        dve.wait_ge(decay_ready, 1)
                    else:
                        dve.wait_ge(z_done, z_uses[0])
                    dve.tensor_tensor(ret_z[:, :], ps[:, PJ_ + j % 2, :], ret_rot[:, 0, :], ALU.mult).then_inc(pj_drained[j % 2], 1)
                    dve.wait_ge(pj_drained[j % 2], j // 2 + 1)
                    dve.wait_ge(ret_sin, i + 1)
                    t = z[z_uses[0] % 2]
                    z_uses[0] += 1
                    if kind == "retk":
                        dve.tensor_tensor(ret_k[:, n, :], ret_z[:, :], t[:, :], ALU.add).then_inc(z_done, 1)
                    else:
                        for hh in range(2):
                            r = slice(64 * hh, 64 * hh + 64)
                            ins = dve.tensor_tensor(ret_q[r, 2 * n + hh, :], ret_z[r, :], t[r, :], ALU.add)
                        ins.then_inc(z_done, 1)
                elif kind in ("kc", "vc", "ks", "kw", "q"):
                    if kind != "vc":
                        wait_pj_drained(dve, kind, n)
                        r = ROT_INDEX[kind, n]
                        if r:
                            dve.wait_ge(rot_turned, r)
                        if kind == "kc":
                            src = z_cmp[0:32, n, :]
                        else:
                            src = z[z_uses[0] % 2][0:32, :]
                            z_uses[0] += 1
                        dve.stream_shuffle(swp[:, :], src, [(i + 16) % 32 for i in range(32)]).then_inc(rot_swapped, 1)
                    finish_rot()
                    if kind != "vc":
                        pending.append((kind, n))
                elif kind == "gate":
                    finish_rot()
                    t = z[z_uses[0] % 2]
                    z_uses[0] += 1
                    j = PJ_ORDER.index((kind, n))
                    dve.wait_ge(gate_tanh, gated_by(n))
                    dve.scalar_tensor_tensor(t[:, :], t[:, :], 1.0, ps[:, PJ_ + j % 2, :], ALU.add, ALU.mult).then_inc(pj_drained[j % 2], 1)
                    dve.wait_ge(pj_drained[j % 2], j // 2 + 1)
                    wait_head_out(dve, n)
                    dve.scalar_tensor_tensor(mixed[:, n, :], t[:, :], 0.5, mixed[:, n, :], ALU.mult, ALU.mult).then_inc(z_done, 1)

            def mixed_lo(n):
                t = OUT_ORDER[n]
                dve.wait_ge(mix_hi_ready, n + 1)
                dve.tensor_tensor(mix_lo[n % RING][:, :], mixed[:, t, :], mix_hi[n % RING][:, :].bitcast(F32),
                                  ALU.subtract).then_inc(mix_ready, 1)

            dve.wait_ge(ld_pos, 16)
            link(dve.tensor_copy(posf[:, :], posi[:, :]))
            dve.wait_ge(ld_par, 16)
            link(dve.tensor_scalar(ang[:, :], posf[:, :], par[:, S_FREQ:S_FREQ + 1], None, ALU.mult))
            magic = 12582912.0
            link(dve.tensor_scalar(turns[:, :], ang[:, :], 1.0 / (2 * math.pi), par[:, S_FREQ + 1:S_FREQ + 2],
                                   ALU.mult, ALU.add))
            link(dve.tensor_scalar(turns[:, :], turns[:, :], magic, None, ALU.add))
            link(dve.tensor_scalar(turns[:, :], turns[:, :], magic, None, ALU.subtract))
            c1 = 6.28125
            c2 = float(np.float32(round((2 * math.pi - c1) * 2 ** 19) / 2 ** 19))
            for c in (c1, c2, 2 * math.pi - c1 - c2):
                link(dve.scalar_tensor_tensor(ang[:, :], turns[:, :], -c, ang[:, :], ALU.mult, ALU.add))
            link(dve.tensor_scalar(ang[:, :], ang[:, :], par[:, S_FREQ + 2:S_FREQ + 3], None, ALU.add))
            dve.tensor_scalar(ang[:, :], ang[:, :], 3.1415925, -3.1415925, ALU.min, ALU.max).then_inc(angles_ready, 1)
            for _ in range(LEAD):
                split()
            for what, kind, n in SCHEDULE:
                if what == "norm":
                    gain = S_GMEM if kind == "mem" else S_GPRE
                    hi, lo = (m_hi, m_lo) if kind == "mem" else (h_hi, h_lo)
                    if kind == "mem":
                        norm_rows(mem_nat, 0, MT, 1)
                    for k in range(KT):
                        dve.wait_ge(mem_hi if kind == "mem" else x_hi, k + 1)
                        dve.scalar_tensor_tensor(lo[:, k, :], turn_bank(kind, k), par[:, gain + k:gain + k + 1],
                                                 hi[:, k, :].bitcast(F32), ALU.mult,
                                                 ALU.subtract).then_inc(mem_lo if kind == "mem" else x_lo, 1)
                    if kind == "mem":
                        dve.wait_ge(ld_x, 16)
                        dve.wait_ge(squares_done, MT)
                        for r in range(TT):
                            link(dve.scalar_tensor_tensor(square[:, :], x_nat[:, r, :], 1.0, x_nat[:, r, :], ALU.mult,
                                                          ALU.mult, accum_out=sumsq[:, 2 + r:3 + r]))
                        norm_rows(x_nat, 2, TT, 2)
                elif what == "slab":
                    split()
                    if kind != "out":
                        project(kind, n)
                    elif n + LEAD < MIX_TILES:
                        mixed_lo(n + LEAD)
                elif what == "mem" and kind == "att":
                    if n:
                        turned_block(T)
                    mem_front(n)
                    mem_back(n)
                elif what == "mem":
                    turned_block(T)
                elif what == "rot":
                    finish_rot()
                elif (what, kind) == ("ret", "scores"):
                    if n == 0:
                        dve.wait_ge(decay_ready, 1 + RET_HEADS)
                    off = 0
                    if n >= 2:
                        dve.wait_ge(ret_full, n - 1)
                    for j in range(TT):
                        k = t_uses[0]
                        t_uses[0] += 1
                        w = T - P * j
                        dve.wait_ge(t_full, k + 1)
                        dve.scalar_tensor_tensor(inner[n % 2][:, off:off + w], ps[:, T_ + k % 2, 0:w], RET_QK ** -0.5,
                                                 decay[:, n, 0:w], ALU.mult, ALU.mult).then_inc(t_drained[k % 2], 1)
                        off += w
                elif (what, kind) == ("ret", "values"):
                    dve.wait_ge(ret_full, n + 1)
                    for i in range(TT):
                        ins = dve.bn_stats(bn[:, i, :], ps[:, O_, i * P:(i + 1) * P])
                    link(ins)
                    for i in range(TT):
                        ins = dve.bn_aggr(mv[:, i, :], bn[:, i, :])
                    link(ins)
                    dve.tensor_scalar(meansq[:, 6:6 + TT], mv[:, :, 1], EPS, None, ALU.add).then_inc(ret_var, 1)
                    dve.wait_ge(ret_rstd, n + 1)
                    if n >= 2:
                        dve.wait_ge(t_full, T_USED["ret", "turn", n - 2])
                    for i in range(TT):
                        ins = dve.tensor_scalar(ret_n[n % 2][:, i, :], ps[:, O_, i * P:(i + 1) * P], mv[:, i, 0:1],
                                                rstd[:, 6 + i:7 + i], ALU.subtract, ALU.mult)
                    ins.then_inc(o_drained, 1)
                elif (what, kind) == ("ret", "turn"):
                    t_uses[0] += 1
                elif what == "blocks":
                    i = 0 if kind == "k" else 1
                    if i == 0:
                        dve.wait_ge(rot_turned, 2)
                        for g in range(GROUPS):
                            wait_pj_drained(dve, "vc", g)
                        dve.wait_ge(ret_full, RET_HEADS)
                        link(dve.memset(blk[:, CMP_BLOCK * BLK_N:], 0.0))
                    else:
                        dve.wait_ge(blk_ready, 1)
                    pos = par[:, S_POS + CMP_BLOCK * i:S_POS + CMP_BLOCK * (i + 1)]
                    bv = blk[:, 0:CMP_BLOCK * BLK_N].rearrange("p (c g n) -> p c g n", g=GROUPS, n=N_CMP)
                    for g in range(GROUPS):
                        zc = z_cmp[:, 2 * i + g, :].rearrange("p (n s) -> p s n", s=CMP_STRIDE)
                        for half in range(2):
                            c = slice(half * CMP_STRIDE, (half + 1) * CMP_STRIDE)
                            ins = dve.tensor_tensor(bv[:, c, g, :], zc[:, :, half:half + N_CMP],
                                                    pos[:, c].unsqueeze(2).to_broadcast([P, CMP_STRIDE, N_CMP]), ALU.add)
                    ins.then_inc(blk_sum, 1)
                    dve.wait_ge(blk_hi_ready, i + 1)
                    dve.tensor_tensor(blk_lo[:, :], blk[:, :], blk_hi[:, :].bitcast(F32), ALU.subtract).then_inc(blk_ready, 1)
                elif what == "mlp":
                    i = 0 if kind == "k" else 1
                    dve.wait_ge(hid_sq, i + 1)
                    a = hid[0:BLK_N, 2, :]
                    link(dve.tensor_scalar(a, hid[0:BLK_N, 1, :], 0.044715, 1.0, ALU.mult, ALU.add))
                    dve.tensor_tensor(a, a, hid[0:BLK_N, 0, :], ALU.mult).then_inc(hid_poly, 1)
                    dve.wait_ge(hid_tanh, i + 1)
                    dve.scalar_tensor_tensor(hid[0:BLK_N, 3, :], hid[0:BLK_N, 3, :], 1.0, hid[0:BLK_N, 0, :], ALU.add,
                                             ALU.mult).then_inc(hid_ready, 1)
                    t_uses[0] += 1
                    k = take_t_hi()
                    if kind == "k":
                        dve.memset(keys_hi[:, :, N_CMP:CMP_COLS].bitcast(F32), 0.0)
                        dve.memset(keys_lo[:, :, N_CMP:CMP_COLS].bitcast(F32), 0.0)
                        dve.tensor_tensor(keys_lo[:, :, 0:N_CMP], ps[:, T_ + k % 2, 0:BLK_N].rearrange("p (g n) -> p g n", g=2),
                                          keys_hi[:, :, 0:N_CMP].bitcast(F32), ALU.subtract).then_inc(t_drained[k % 2], 1)
                    else:
                        dve.tensor_tensor(vc_lo[0:N_CMP, :, :], ps[0:N_CMP, T_ + k % 2, 0:2 * P].rearrange("p (g n) -> p g n", g=2),
                                          vc_hi[0:N_CMP, :, :].bitcast(F32), ALU.subtract).then_inc(t_drained[k % 2], 1)
                elif what == "pair" and kind == "att":
                    for hh in range(2):
                        pp = parts_of_step(kind, n, hh)
                        widths = [2 * P if j < 0 else T for j in blocks_of_part(*pp)] if pp else []
                        for w in widths[:2]:
                            turned_block(w)
                        head_front(n, hh)
                        for w in widths[2:]:
                            turned_block(w)
                        head_back(n, hh)
                elif what == "pair":
                    for hh in range(3):
                        for j in blocks_of_part(*parts_of_step(kind, n, hh)):
                            turned_block(2 * P if j < 0 else T)
                    for m in range(LEAD):
                        mixed_lo(m)
            dve.wait_ge(ld_res, 16)
            dve.wait_ge(ld_post, 16)
            for t in range(TT):
                y = ps[:, 2 * t:2 * t + 2, :].rearrange("p h c -> p (h c)")
                dve.wait_ge(y_squared, t + 1)
                dve.tensor_scalar(meansq[:, 10 + t:11 + t], sumsq[:, 10 + t:11 + t], 1.0 / D, EPS, ALU.mult,
                                  ALU.add).then_inc(y_meansq, 1)
                dve.wait_ge(y_rstd, t + 1)
                if t >= 2:
                    dve.wait_ge(y_stored[t - 2], 16)
                link(dve.scalar_tensor_tensor(y_sb[t % 2][:, :], y, rstd[:, 10 + t:11 + t], gpost_b[:, :], ALU.mult, ALU.mult))
                dve.tensor_tensor(y_sb[t % 2][:, :], y_sb[t % 2][:, :], x_res[:, t, :], ALU.add).then_inc(y_ready, 1)

        @block.tensor
        def _(pe):
            t_uses, s_uses, o_uses, slabs, pts = [0], [0], [0], [0], [0]

            def take_t():
                k = t_uses[0]
                t_uses[0] += 1
                if k >= 2:
                    pe.wait_ge(t_drained[k % 2], k // 2)
                return k

            def product(dst, w, m, first=True, last=True):
                pe.matmul(dst, w[0], m[0], start=first, stop=False)
                pe.matmul(dst, w[0], m[1], start=False, stop=False)
                return pe.matmul(dst, w[1], m[0], start=False, stop=last)

            def turn_blocks(blocks):
                k = take_t()
                for c, src in enumerate(blocks):
                    ins = pe.transpose(ps[:, T_ + k % 2, c * P:(c + 1) * P], src, ident[:, :])
                ins.then_inc(t_full, 1)
                return k

            def o_bank():
                if o_uses[0]:
                    pe.wait_ge(o_drained, o_uses[0])
                o_uses[0] += 1

            def wait_turned(k):
                pe.wait_ge(t_drained[k % 2], k // 2 + 1)

            def mem_scores(u):
                h, half = u // 2, u % 2
                if s_uses[0]:
                    pe.wait_ge(s_drained, s_uses[0])
                s_uses[0] += 1
                for qt in range(2):
                    c = slice((2 * half + qt) * P, (2 * half + qt + 1) * P)
                    ins = product(ps[:, S_, qt * MEM:(qt + 1) * MEM], (mq_hi[:, h, c], mq_lo[:, h, c]),
                                  (mk_hi[:, h, :], mk_lo[:, h, :]))
                ins.then_inc(s_full, 1)

            def mem_turn(u):
                pe.wait_ge(prob_ready, u + 1)
                return turn_blocks([mprob[u % 2][:, qt, kt * P:(kt + 1) * P] for kt in range(MT) for qt in range(2)])

            def mem_values(u, k):
                h = u // 2
                o_bank()
                wait_turned(k)
                c = slice(h * DH, (h + 1) * DH)
                for kt in range(MT):
                    m = slice(kt * 2 * P, (kt + 1) * 2 * P)
                    ins = product(ps[:, O_, 0:2 * P], (mv_hi[:, kt, c], mv_lo[:, kt, c]),
                                  (pt_hi[k % 2][:, m], pt_lo[k % 2][:, m]), kt == 0, kt == MT - 1)
                ins.then_inc(pv_done, 1)

            def head_scores(p, hh):
                g, i, h0 = pair_of(p)
                h = PER_GROUP * g + h0 + hh
                if s_uses[0]:
                    pe.wait_ge(s_drained, s_uses[0])
                s_uses[0] += 1
                c = slice(i * P, (i + 1) * P)
                q = (q_hi[:, h, c], q_lo[:, h, c])
                cuts = [(0, CMP_COLS + 2 * P, S_, 224)]
                if i:
                    cuts.append((CMP_COLS + 2 * P, 2 * P * min(i, 2), S_ + 1, 0))
                if i == 3:
                    cuts.append((CMP_COLS + 6 * P, 2 * P, S_ + 2, 0))
                for k0, w, bank, col in cuts:
                    ins = product(ps[:, bank, col:col + w], q, (keys_hi[:, g, k0:k0 + w], keys_lo[:, g, k0:k0 + w]))
                ins.then_inc(s_full, 1)

            def turn_pair_block(p, j):
                pr = prob[p % 2]
                if j < 0:
                    return turn_blocks([pr[:, hh, 0:P] for hh in range(2)])
                c = CMP_COLS + 2 * P * j
                return turn_blocks([pr[:, hh, c + b * P:c + (b + 1) * P] for b in range(2) for hh in range(2)])

            def block_values(p, j, k):
                g, i, _ = pair_of(p)
                if j < 0:
                    o_bank()
                wait_turned(k)
                if j < 0:
                    ins = product(ps[:, O_, 0:2 * P], (vc_hi[:, g, :], vc_lo[:, g, :]),
                                  (pt_hi[k % 2][:, 0:2 * P], pt_lo[k % 2][:, 0:2 * P]), True, False)
                else:
                    for b in range(2):
                        c = slice(b * VC + g * DH, b * VC + (g + 1) * DH)
                        m = slice(b * 2 * P, (b + 1) * 2 * P)
                        ins = product(ps[:, O_, 0:2 * P], (v_hi[:, j, c], v_lo[:, j, c]),
                                      (pt_hi[k % 2][:, m], pt_lo[k % 2][:, m]), False, j == i and b == 1)
                ins.then_inc(pv_done, 1)

            def pair_half(pp, scores):
                todo = blocks_of_part(*pp) if pp else []
                turned = []
                if pp and pp[1] == 0:
                    pe.wait_ge(prob_ready, 2 * MEM_HEADS + 2 * (pp[0] + 1))
                while todo and len(turned) < 2:
                    turned.append((todo[0], turn_pair_block(pp[0], todo.pop(0))))
                if scores:
                    head_scores(*scores)
                fill(1)
                while turned:
                    block_values(pp[0], *turned.pop(0))
                    if todo:
                        turned.append((todo[0], turn_pair_block(pp[0], todo.pop(0))))
                    fill(1)
                fill(1)

            running = []

            def fill(chunks):
                if not running:
                    if SLABS[slabs[0]][0] not in PJ_KINDS:
                        return
                    running.append(project(*SLABS[slabs[0]]))
                for _ in range(chunks):
                    if next(running[0], None) is None:
                        return

            def finish_slab():
                for _ in (running.pop() if running else project(*SLABS[slabs[0]])):
                    pass
                slabs[0] += 1

            def project(kind, n):
                s = slabs[0]
                pe.wait_ge(slab_lo_ready, s + 1)
                hi, lo = slab_hi[s % RING], slab_lo[s % RING]
                if kind in PJ_KINDS:
                    j = PJ_ORDER.index((kind, n))
                    if j >= 2:
                        pe.wait_ge(pj_drained[j % 2], j // 2)
                    if j in (4, 5):
                        pe.wait_ge(val_drained, VP)
                    mh, ml, w = (m_hi, m_lo, MEM) if kind == "memk" else (h_hi, h_lo, T)
                    for k in range(KT):
                        c = slice(k * P, (k + 1) * P)
                        ins = product(ps[:, PJ_ + j % 2, 0:w], (hi[:, c], lo[:, c]), (mh[:, k, :], ml[:, k, :]),
                                      k == 0, k == KT - 1)
                        if k < KT - 1:
                            yield True
                elif kind == "memv":
                    for kk in range(2):
                        c = slice(kk * T, (kk + 1) * T)
                        for t in range(MT):
                            r = slice(t * P, (t + 1) * P)
                            k = 2 * n + kk
                            ins = product(ps[:, S_ + t, :], (m_hi[:, k, r], m_lo[:, k, r]), (hi[:, c], lo[:, c]),
                                          k == 0, k == KT - 1)
                elif kind == "v":
                    piece, half = n // 2, n % 2
                    if half == 0:
                        if piece == 0:
                            pe.wait_ge(x_lo, TT)
                        elif piece >= 2:
                            pe.wait_ge(val_drained, piece - 1)
                    elif piece == 0:
                        pe.wait_ge(x_lo, KT)
                    bank = 4 * (piece % 2)
                    for t in range(TT):
                        r = slice(t * P, (t + 1) * P)
                        for kk in range(4):
                            k = 4 * half + kk
                            c = slice(kk * VW, (kk + 1) * VW)
                            ins = product(ps[:, bank + t, 0:VW], (h_hi[:, k, r], h_lo[:, k, r]), (hi[:, c], lo[:, c]),
                                          k == 0, k == KT - 1)
                elif kind in ("w1k", "w1v"):
                    if n == 0:
                        o_bank()
                        pe.wait_ge(blk_ready, 1 if kind == "w1k" else 2)
                    for cc in range(W1_C):
                        c = W1_C * n + cc
                        b = slice(c * BLK_N, c * BLK_N + P)
                        m = slice(cc * CMP_HIDDEN, (cc + 1) * CMP_HIDDEN)
                        ins = product(ps[:, O_, 0:CMP_HIDDEN], (blk_hi[:, b], blk_lo[:, b]), (hi[:, m], lo[:, m]),
                                      c == 0, c == CMP_BLOCK - 1)
                ins.then_inc(slab_used, 1)

            def out_products(n, t, s):
                hi, lo = slab_hi[s % RING], slab_lo[s % RING]
                r = slice(t * P, (t + 1) * P)
                for half in range(2):
                    c = slice(half * T, (half + 1) * T)
                    ins = product(ps[:, 2 * t + half, :], (mix_hi[n % RING][:, r], mix_lo[n % RING][:, r]),
                                  (hi[:, c], lo[:, c]), n == 0, n == MIX_TILES - 1)
                return ins

            for what, kind, n in SCHEDULE:
                if what == "norm":
                    if kind == "mem":
                        pe.wait_ge(consts_ready, 1)
                    pe.wait_ge(normed, MT if kind == "mem" else MT + TT)
                    nat, rows = (mem_nat, MT) if kind == "mem" else (x_nat, TT)
                    for k in range(KT):
                        if kind == "x" and k == 0:
                            pe.wait_ge(memv_drained, 1)
                        if kind == "x" and k == 4:
                            wait_pj_all_drained(pe, MEM_HEADS)
                        dst = turn_bank(kind, k)
                        for r in range(rows):
                            ins = pe.transpose(dst[:, r * P:(r + 1) * P], nat[:, r, k * P:(k + 1) * P], ident[:, :])
                        if kind == "x":
                            ins.then_inc(turned_x, 1)
                        elif k % 2:
                            ins.then_inc(turned_mem, 1)
                    if kind == "mem":
                        pe.wait_ge(mem_lo, KT)
                elif what == "slab" and kind != "out":
                    finish_slab()
                elif what == "mem" and kind == "att":
                    if n == 0:
                        pe.wait_ge(val_drained, VP)
                        pe.wait_ge(pj_drained[0], 4)
                        pe.wait_ge(pj_drained[1], 4)
                    if n:
                        k = mem_turn(n - 1)
                    mem_scores(n)
                    fill(2)
                    if n:
                        mem_values(n - 1, k)
                    fill(2)
                elif what == "mem":
                    k = mem_turn(2 * MEM_HEADS - 1)
                    fill(4)
                    mem_values(2 * MEM_HEADS - 1, k)
                elif (what, kind) == ("ret", "scores"):
                    if n == 0:
                        pe.wait_ge(z_done, len(RET_PROJ))
                    for j in range(TT):
                        k = take_t()
                        pe.matmul(ps[:, T_ + k % 2, 0:T - P * j], ret_k[:, n // 2, j * P:(j + 1) * P],
                                  ret_q[:, n, j * P:], start=True, stop=True).then_inc(t_full, 1)
                        fill(1)
                elif (what, kind) == ("ret", "values"):
                    o_bank()
                    wait_t_drained(pe, T_USED["ret", "scores", n])
                    offs = [0, 512, 896, 1152]
                    for i in range(TT):
                        for j in range(i + 1):
                            c = offs[j] + (i - j) * P
                            ins = pe.matmul(ps[:, O_, i * P:(i + 1) * P], inner[n % 2][:, c:c + P],
                                            ret_v[:, j, n * RET_V:(n + 1) * RET_V], start=j == 0, stop=j == i)
                    ins.then_inc(ret_full, 1)
                elif (what, kind) == ("ret", "turn"):
                    pe.wait_ge(o_drained, O_USED["ret", "values", n])
                    turn_blocks([ret_n[n % 2][:, i, :] for i in range(TT)])
                elif what == "mlp":
                    pe.wait_ge(hid_ready, 1 if kind == "k" else 2)
                    k = take_t()
                    for c in range(2):
                        ins = pe.transpose(ps[:, T_ + k % 2, c * P:c * P + BLK_N], hid[0:BLK_N, 3, c * P:(c + 1) * P],
                                           ident[0:BLK_N, 0:BLK_N])
                    ins.then_inc(t_full, 1)
                    wait_turned(k)
                    k = take_t()
                    w2 = par[:, S_W2:].rearrange("p (a c d) -> p a c d", a=2, c=2)
                    if kind == "k":
                        for c in range(2):
                            ins = pe.matmul(ps[:, T_ + k % 2, 0:BLK_N], w2[:, 0, c, :], hid_t[:, c, :], start=c == 0, stop=c == 1)
                    else:
                        for g in range(GROUPS):
                            for c in range(2):
                                ins = pe.matmul(ps[0:N_CMP, T_ + k % 2, g * P:(g + 1) * P], hid_t[:, c, g * N_CMP:(g + 1) * N_CMP],
                                                w2[:, 1, c, :], start=c == 0, stop=c == 1)
                    ins.then_inc(t_full, 1)
                elif what == "pair" and kind == "att":
                    if n == 0:
                        wait_t_drained(pe, t_uses[0])
                        pe.wait_ge(consts_ready, 2 + TT + 1 + 2)
                        pe.wait_ge(z_done, Z_INDEX["q", PER_GROUP - 1] + 1)
                    if n == 2 * TT:
                        pe.wait_ge(z_done, Z_INDEX["q", HEADS - 1] + 1)
                    for hh in range(2):
                        pair_half(parts_of_step(kind, n, hh), (n, hh))
                elif what == "pair":
                    for hh in range(3):
                        pair_half(parts_of_step(kind, n, hh), None)
            s0 = slabs[0]
            last3 = MIX_TILES - RING
            pe.wait_ge(s_drained, s_uses[0])
            pe.wait_ge(o_drained, o_uses[0])
            for n in range(last3):
                pe.wait_ge(slab_lo_ready, s0 + n + 1)
                pe.wait_ge(mix_ready, n + 1)
                for t in range(TT):
                    if n == 0 and t == 2:
                        wait_pj_all_drained(pe, len(PJ_ORDER))
                    if n == 0 and t == 3:
                        wait_t_drained(pe, t_uses[0])
                    ins = out_products(n, t, s0 + n)
                ins.then_inc(slab_used, 1)
            pe.wait_ge(slab_lo_ready, s0 + MIX_TILES)
            pe.wait_ge(mix_ready, MIX_TILES)
            for t in range(TT):
                for n in range(last3, MIX_TILES):
                    ins = out_products(n, t, s0 + n)
                ins.then_inc(y_full, 1)


def frequencies():
    f = np.zeros((P, 4), np.float32)
    row = np.arange(32)
    ret = RET_THETA ** (-(row % (RET_QK // 2)) / (RET_QK // 2))
    nsa = NSA_THETA ** (-(row % (ROT_DIM // 2)) / (ROT_DIM // 2))
    f[:, 0] = np.concatenate([ret, ret, nsa, nsa * np.where(row < ROT_DIM // 2, -1.0, 1.0)])
    f[:32, 1:3] = f[64:96, 1:3] = [0.25, math.pi / 2]
    return f


def column_slabs(w, starts):
    v = w.reshape(KT, P, -1)
    return np.stack([v[:, :, c:c + P].transpose(1, 0, 2).reshape(P, D) for c in starts])


def kernel(x, mem, positions, norm_pre, w_in, cmp_pos_k, cmp_w1_k, cmp_w2_k, cmp_pos_v, cmp_w1_v, cmp_w2_v,
           ret_gn, mem_norm, w_mem_kv, w_out, norm_post):
    import concourse.bacc as bacc
    from concourse.bass_utils import run_bass_kernel_spmd

    w_in, w_mem_kv, w_out = (np.asarray(a)[0] for a in (w_in, w_mem_kv, w_out))
    start = {"memq": lambda n: C_MQ + n * P, "retq": lambda n: C_RQ + n * P, "retk": lambda n: C_RK + n * P,
             "kc": lambda n: kv_col(0, 0, n), "vc": lambda n: kv_col(0, 1, n), "ks": lambda n: kv_col(1, 0, n),
             "kw": lambda n: kv_col(2, 0, n), "q": lambda n: C_Q + n * P, "gate": lambda n: C_GATE + n * P}
    w_proj = column_slabs(w_in, [start[k](n) for k, n in SLABS if k in start])
    pieces = []
    for v, c0 in enumerate((kv_col(1, 1, 0), kv_col(2, 1, 0), C_RV, C_RV + VC)):
        cols = np.r_[c0:c0 + VC, C_G + v * GC:C_G + (v + 1) * GC]
        w = w_in[:, cols].reshape(2, 4, P, VW)
        pieces += [w[f].transpose(1, 0, 2).reshape(P, SLAB) for f in range(2)]
    w_val = np.stack(pieces)
    half = MEM_HEADS * DH
    w_mem = np.concatenate([
        column_slabs(w_mem_kv, [h * DH for h in range(MEM_HEADS)]),
        w_mem_kv[:, half:].reshape(4, 2, P, half).transpose(0, 2, 1, 3).reshape(4, P, D)])
    w_cmp = np.concatenate([np.asarray(w)[0].reshape(8, W1_C, P, CMP_HIDDEN).transpose(0, 2, 1, 3).reshape(8, P, D)
                            for w in (cmp_w1_k, cmp_w1_v)])
    w_o = np.stack([w_out[t * P:(t + 1) * P] for t in OUT_ORDER])
    small = np.concatenate(
        [np.asarray(a)[0].reshape(-1, P).T for a in (norm_pre, mem_norm, ret_gn)] + [frequencies()]
        + [np.asarray(a)[0].T for a in (cmp_pos_k, cmp_pos_v)]
        + [np.asarray(a)[0].reshape(2, P, DH).transpose(1, 0, 2).reshape(P, 2 * DH) for a in (cmp_w2_k, cmp_w2_v)], axis=1)
    arrays = {"x_in": np.asarray(x)[0], "mem_in": np.asarray(mem)[0], "positions_in": np.asarray(positions)[0],
              "small_in": small, "gpost_in": np.asarray(norm_post)[0], "w_proj_in": w_proj, "w_val_in": w_val,
              "w_mem_in": w_mem, "w_cmp_in": w_cmp, "w_out_in": w_o}
    arrays = {k: np.ascontiguousarray(a) for k, a in arrays.items()}
    nc = bacc.Bacc("TRN2", target_bir_lowering=False, num_devices=1)
    args = [nc.dram_tensor(k, a.shape, mybir.dt.from_np(a.dtype), kind="ExternalInput").ap() for k, a in arrays.items()]
    out = nc.dram_tensor("y_out", (T, D), F32, kind="ExternalOutput").ap()
    build(nc, *args, out)
    r = run_bass_kernel_spmd(nc, [arrays], core_ids=[0])
    return r.results[0]["y_out"].reshape(1, T, D)
```

```python
import math
from contextlib import ExitStack

import numpy as np
import concourse.bass as bass
from concourse import mybir

F32 = mybir.dt.float32
F32R = mybir.dt.float32r
I32 = mybir.dt.int32
ACT = mybir.ActivationFunctionType
ALU = mybir.AluOpType
AX = mybir.AxisListType

P = 128
D = 1024
T = 512
MEM = 256
EPS = 1e-6
DH = 128
GROUPS, PER_GROUP = 2, 4
HEADS = GROUPS * PER_GROUP
RET_HEADS, RET_QK, RET_V = 4, 64, 128
MEM_HEADS = 4
CMP_BLOCK, CMP_STRIDE, CMP_HIDDEN = 32, 16, 256
N_CMP = (T - CMP_BLOCK) // CMP_STRIDE + 1
CMP_COLS = 32
ROT_DIM = DH // 4
NSA_THETA, RET_THETA = 500000.0, 10000.0
SCALE = DH ** -0.5
NEG = -2.0 ** 100
KT = D // P
TT = T // P
MT = MEM // P
MIX_TILES = HEADS + RET_HEADS + MEM_HEADS
NSA0, RET0, MEM0 = 0, HEADS, HEADS + RET_HEADS
VP = 4
VC = 256
GC = 3 * HEADS // VP
VW = VC + GC
SLAB = 4 * VW
RING = 4
MIX_RING = 3
LEAD = 2
KEYS = CMP_COLS + 2 * T
W1_C = 4
BLK_N = GROUPS * N_CMP
BLK_W = CMP_BLOCK * BLK_N + (P - BLK_N)
OUT_ORDER = [*range(RET0, MIX_TILES), *range(NSA0, RET0)]

C_Q, C_KV, C_G = 0, HEADS * DH, HEADS * DH + 6 * GROUPS * DH
C_RQ = C_G + 3 * HEADS
C_RK = C_RQ + RET_HEADS * RET_QK
C_RV = C_RK + RET_HEADS * RET_QK
C_MQ = C_RV + RET_HEADS * RET_V
C_GATE = C_MQ + MEM_HEADS * DH


def kv_col(branch, kv, group):
    return C_KV + ((branch * 2 + kv) * GROUPS + group) * DH


S_GPRE, S_GMEM, S_GN = 0, KT, 2 * KT
S_FREQ = S_GN + RET_HEADS
S_POS = S_FREQ + 4
S_W2 = S_POS + 2 * CMP_BLOCK
S_COLS = S_W2 + 2 * 2 * DH


def schedule():
    s = [("norm", "mem", 0)]
    for h in range(MEM_HEADS):
        s += [("slab", "memk", h), ("square", "x", h)]
    for v in range(4):
        s += [("slab", "memv", v), ("scale", "x", v)]
    s += [("norm", "x", 0)]
    s += [("slab", "v", 0), ("angles", "rot", 0), ("slab", "v", 1), ("tables", "rot", 0)]
    s += [("slab", "v", v) for v in range(2, 2 * VP)]
    s += [("slab", "memq", h) for h in range(MEM_HEADS)]
    for u, (kind, n) in enumerate([("retq", 0), ("retq", 1), ("retk", 0), ("retk", 1)]):
        s += [("mem", "att", 2 * u), ("mem", "att", 2 * u + 1), ("late", kind, n)]
    s += [("mem", "flush", 0), ("slab", "kc", 0)]
    for h, (kind, n) in enumerate([("kc", 1), ("vc", 0), ("vc", 1), ("ks", 0)]):
        s += [("ret", "scores", h)]
        if h:
            s += [("ret", "values", h - 1)]
        if h > 1:
            s += [("ret", "turn", h - 2)]
        s += [("slab", kind, n)]
    s += [("ret", "values", RET_HEADS - 1), ("ret", "turn", RET_HEADS - 2)]
    s += [("blocks", "k", 0), ("slab", "ks", 1), ("ret", "turn", RET_HEADS - 1), ("slab", "kw", 0)]
    for n, fill in enumerate([("kw", 1), ("gate", MEM0), None, None]):
        s += [("slab", "w1k", 2 * n), ("slab", "w1k", 2 * n + 1)] + ([("slab", *fill)] if fill else [])
    s += [("hidden", "k", 0), ("slab", "gate", MEM0 + 1), ("mlp", "k", 0), ("blocks", "v", 0), ("slab", "gate", MEM0 + 2)]
    for n, fill in enumerate([("gate", MEM0 + 3), ("gate", RET0), ("q", 0), None]):
        s += [("slab", "w1v", 2 * n), ("slab", "w1v", 2 * n + 1)] + ([("slab", *fill)] if fill else [])
    s += [("hidden", "v", 0), ("slab", "q", 1), ("mlp", "v", 0), ("slab", "gate", RET0 + 1)]
    fill = [("q", h) for h in range(2, HEADS)] + [("gate", NSA0), ("gate", NSA0 + 1), ("gate", RET0 + 2)]
    fill += [("gate", NSA0 + 2), ("gate", NSA0 + 3), None, ("gate", RET0 + 3), ("gate", NSA0 + 4), ("gate", NSA0 + 5), None]
    for p in range(GROUPS * TT * 2):
        s += [("pair", "att", p)]
        if fill[p]:
            s += [("late", *fill[p])]
    s += [("pair", "flush", 0)]
    s += [("slab", "gate", NSA0 + h) for h in range(HEADS - 2, HEADS)]
    s += [("slab", "out", n) for n in range(MIX_TILES)]
    return s


SCHEDULE = schedule()
SLABS = [(kind, n) for what, kind, n in SCHEDULE if what in ("slab", "late")]
LATE = {after: slab[1:] for slab, after in zip(SCHEDULE, SCHEDULE[1:]) if slab[0] == "late"}
PAIRS = GROUPS * 2 * TT


def pair_of(p):
    return p // (2 * TT), p % TT, 2 * (p // TT % 2)


def parts_of_step(kind, n, hh):
    if kind == "flush":
        return [(PAIRS - 2, 1), (PAIRS - 1, 0), (PAIRS - 1, 1)][hh]
    p, part = (n - 2, 1) if hh == 0 else (n - 1, 0)
    return (p, part) if p >= 0 else None


def blocks_of_part(p, part):
    i = pair_of(p)[1]
    cut = (i + 1) // 2
    return [-1, *range(cut)] if part == 0 else list(range(cut, i + 1))


def count_uses():
    t = o = 0
    t_used, o_used = {}, {}
    for what, kind, n in SCHEDULE:
        if what == "mem":
            if kind == "flush" or n:
                t, o = t + 1, o + 1
        elif what == "ret":
            t += {"scores": TT, "values": 0, "turn": 1}[kind]
            o += kind == "values"
        elif what == "mlp":
            t += 2
        elif what == "slab" and kind in ("w1k", "w1v") and n == 0:
            o += 1
        elif what == "pair":
            for hh in range(3 if kind == "flush" else 2):
                if (pp := parts_of_step(kind, n, hh)):
                    t, o = t + len(blocks_of_part(*pp)), o + pp[1]
        t_used[what, kind, n], o_used[what, kind, n] = t, o
    return t_used, o_used


T_USED, O_USED = count_uses()
PJ_KINDS = ("memk", "memq", "retq", "retk", "kc", "vc", "ks", "kw", "q", "gate")


def slab_words(kind):
    return SLAB if kind == "v" else D


def build(nc, x, mem, positions, small, gpost, w_proj, w_val, w_mem, w_cmp, w_out, out):
    ctx = ExitStack()
    with ctx:
        at = [16512]

        def sb(name, shape, dt=F32, offset=None):
            size = 4 * int(np.prod(shape[1:]))
            if offset is None:
                offset = at[0]
                at[0] += (size + 31) // 32 * 32
            return nc.alloc_sbuf_tensor_at(name, shape, dt, offset=offset)

        def sem(name):
            return ctx.enter_context(nc.semaphore(name))

        h_hi, h_lo = (sb(f"h_{p}", [P, KT, T], F32R) for p in ("hi", "lo"))
        slab_hi = [sb(f"slab_hi{i}", [P, SLAB], F32R) for i in range(RING)]
        slab_raw_at = at[0]
        slab_raw = [sb(f"slab_raw{i}", [P, SLAB]) for i in range(RING)]
        slab_size = (slab_raw_at - at[0]) // -RING
        slab_lo = [sb(f"slab_lo{i}", [P, SLAB], F32R, slab_raw_at + i * slab_size) for i in range(RING)]
        mixed_at = at[0]
        mixed = sb("mixed", [P, MIX_TILES, T])
        keys_at = at[0]
        keys_hi, keys_lo = (sb(f"keys_{p}", [P, GROUPS, KEYS], F32R) for p in ("hi", "lo"))
        v_hi, v_lo = (sb(f"v_{p}", [P, TT, 2 * VC], F32R) for p in ("hi", "lo"))
        vc_hi, vc_lo = (sb(f"vc_{p}", [P, GROUPS, DH], F32R) for p in ("hi", "lo"))
        par = sb("par", [P, S_COLS])
        ident = sb("ident", [P, P])
        ident_r = sb("ident_r", [P, P], F32R)
        masks = sb("masks", [P, TT * CMP_COLS + 2 * P], F32R)
        gates = sb("gates", [P, TT, 3 * HEADS])
        gate_t = sb("gate_t", [P, TT, GC])
        nsa_rot = sb("nsa_rot", [P, 2, T])
        sumsq = sb("sumsq", [P, 16])
        meansq = sb("meansq", [P, 16])
        rstd = sb("rstd", [P, 16])
        power = sb("power", [P, 4])
        smax = sb("smax", [P, 2, 4])
        nbias = sb("nbias", [P, 2, 4])
        ssum = sb("ssum", [P, 2, 4])
        coef = sb("coef", [P, 2, 4])
        bn = sb("bn", [P, TT, 6])
        mv = sb("mv", [P, TT, 2])
        swp = sb("swp", [32, T])
        region = at[0]

        q_at = region
        p_at = q_at + 2 * HEADS * T * 4
        pt_at = p_at + 2 * 2 * KEYS * 4
        z_at = pt_at + 4 * T * 4
        assert z_at + 2 * T * 4 <= 229344, z_at + 2 * T * 4
        q_hi = sb("q_hi", [P, HEADS, T], F32R, q_at)
        q_lo = sb("q_lo", [P, HEADS, T], F32R, q_at + HEADS * T * 4)
        prob = [sb(f"prob{i}", [P, 2, KEYS], F32, p_at + i * 2 * KEYS * 4) for i in range(2)]
        pt_hi = [sb(f"pt_hi{i}", [P, T], F32R, pt_at + i * T * 4) for i in range(2)]
        pt_lo = [sb(f"pt_lo{i}", [P, T], F32R, pt_at + (2 + i) * T * 4) for i in range(2)]
        z = [sb(f"z{i}", [P, T], F32, z_at + i * T * 4) for i in range(2)]
        x_nat = sb("x_nat", [P, TT, D], F32, mixed_at)
        mem_nat = sb("mem_nat", [P, MT, D], F32, mixed_at + TT * D * 4)
        square = sb("square", [P, D], F32, mixed_at + (TT + MT) * D * 4)
        square_v = sb("square_v", [P, D], F32, mixed_at + (TT + MT + 1) * D * 4)
        posi = sb("posi", [P, T], I32, q_at + 16384)
        posf = sb("posf", [P, T], F32, q_at + 16384 + 2048)
        ang = sb("ang", [P, T], F32, q_at + 16384 + 4096)
        turns = sb("turns", [P, T], F32, q_at + 16384 + 6144)
        m_hi = sb("m_hi", [P, KT, MEM], F32R, q_at)
        m_lo = sb("m_lo", [P, KT, MEM], F32R, q_at + KT * MEM * 4)
        mq_hi = sb("mq_hi", [P, MEM_HEADS, T], F32R, q_at + 16384)
        mq_lo = sb("mq_lo", [P, MEM_HEADS, T], F32R, q_at + 24576)
        mk_hi = sb("mk_hi", [P, MEM_HEADS, MEM], F32R, keys_at)
        mk_lo = sb("mk_lo", [P, MEM_HEADS, MEM], F32R, keys_at + 4096)
        mv_hi = sb("mv_hi", [P, MT, T], F32R, keys_at + 8192)
        mv_lo = sb("mv_lo", [P, MT, T], F32R, keys_at + 12288)
        mprob = [sb(f"mprob{i}", [P, 2, MEM], F32, p_at + i * 2048) for i in range(2)]
        decay = sb("decay", [P, RET_HEADS, T], F32, mixed_at)
        decay_i = sb("decay_i", [P, T], I32, mixed_at + 16384)
        ret_v = sb("ret_v", [P, TT, RET_HEADS * RET_V], F32, mixed_at + 8192)
        ret_q = sb("ret_q", [P, RET_HEADS, T], F32, q_at)
        ret_k = sb("ret_k", [P, 2, T], F32, q_at + 8192)
        ret_rot = sb("ret_rot", [P, 2, T], F32, p_at + 12288)
        ret_z = sb("ret_z", [P, T], F32, q_at + 12288)
        inner = [sb(f"inner{i}", [P, 1280], F32, q_at + 16384 + i * 5120) for i in range(2)]
        ret_n = [sb(f"ret_n{i}", [P, TT, RET_V], F32, q_at + 26624 + i * 2048) for i in range(2)]
        masks_f = sb("masks_f", [P, TT * CMP_COLS + 2 * P], F32, p_at + 4096)
        z_cmp = sb("z_cmp", [P, 4, T], F32, p_at + 4096)
        blk = sb("blk", [P, BLK_W], F32, q_at)
        blk_hi = sb("blk_hi", [P, BLK_W], F32R, q_at + 8224)
        blk_lo = sb("blk_lo", [P, BLK_W], F32R, q_at + 16448)
        hid = sb("hid", [P, 4, CMP_HIDDEN], F32, p_at + 12288)
        hid_t = sb("hid_t", [P, 2, BLK_N], F32, q_at + 30720)
        mix_hi = [sb(f"mix_hi{i}", [P, T], F32R, q_at + i * 2048) for i in range(MIX_RING)]
        mix_lo = [sb(f"mix_lo{i}", [P, T], F32R, q_at + (MIX_RING + i) * 2048) for i in range(MIX_RING)]
        gpost_b = sb("gpost_b", [P, D], F32, q_at + 12288)
        x_res = sb("x_res", [P, TT, D], F32, q_at + 16384)
        y_sb = [sb(f"y_sb{i}", [P, D], F32, pt_at + i * D * 4) for i in range(2)]
        y_sq = sb("y_sq", [P, T], F32, z_at)

        S_Y = MT + TT

        ps = ctx.enter_context(nc.psum_tensor("ps", [P, 8, 512], F32))
        S_, O_, PJ_, T_ = 0, 3, 4, 6

        ld_mem, ld_x, ld_par, ld_pos = sem("ld_mem"), sem("ld_x"), sem("ld_par"), sem("ld_pos")
        ld_res, ld_post = sem("ld_res"), sem("ld_post")
        slab_loaded = [sem(f"slab_loaded{i}") for i in range(RING)]
        slab_hi_ready, slab_lo_ready, slab_used = sem("slab_hi_ready"), sem("slab_lo_ready"), sem("slab_used")
        pool_step, act_step, dve_step = sem("pool_step"), sem("act_step"), sem("dve_step")
        consts_ready = sem("consts_ready")
        squares_done = sem("squares_done")
        meansq_ready, rstd_ready = sem("meansq_ready"), sem("rstd_ready")
        normed = sem("normed")
        rounded_ready = sem("rounded_ready")
        turned_mem, turned_x = sem("turned_mem"), sem("turned_x")
        mem_hi, x_hi, mem_lo, x_lo = sem("mem_hi"), sem("x_hi"), sem("mem_lo"), sem("x_lo")
        t_full, t_hi = sem("t_full"), sem("t_hi")
        t_drained = [sem("t_drained0"), sem("t_drained1")]
        pj_hi = sem("pj_hi")
        pj_drained = [sem("pj_drained0"), sem("pj_drained1")]
        memv_hi, memv_drained = sem("memv_hi"), sem("memv_drained")
        val_copied, val_tanh, val_drained = sem("val_copied"), sem("val_tanh"), sem("val_drained")
        angles_ready, rot_ready = sem("angles_ready"), sem("rot_ready")
        decay_iota, decay_exp, decay_ready = sem("decay_iota"), sem("decay_exp"), sem("decay_ready")
        s_full, s_drained, bias_ready, prob_ready = sem("s_full"), sem("s_drained"), sem("bias_ready"), sem("prob_ready")
        pv_done = sem("pv_done")
        ret_full, o_drained = sem("ret_full"), sem("o_drained")
        ret_swapped, ret_sin, ret_ready = sem("ret_swapped"), sem("ret_sin"), sem("ret_ready")
        rot_swapped, rot_turned, rot_hi = sem("rot_swapped"), sem("rot_turned"), sem("rot_hi")
        z_done = sem("z_done")
        ret_var, ret_rstd, ret_normed = sem("ret_var"), sem("ret_rstd"), sem("ret_normed")
        blk_sum, blk_hi_ready, blk_ready = sem("blk_sum"), sem("blk_hi_ready"), sem("blk_ready")
        hid_sq, hid_poly, hid_tanh, hid_ready = sem("hid_sq"), sem("hid_poly"), sem("hid_tanh"), sem("hid_ready")
        gate_tanh = sem("gate_tanh")
        mix_hi_ready, mix_ready = sem("mix_hi_ready"), sem("mix_ready")
        y_full, y_squared, y_meansq, y_rstd, y_ready, y_stored = (
            sem("y_full"), sem("y_squared"), sem("y_meansq"), sem("y_rstd"), sem("y_ready"),
            [sem(f"y_stored{u}") for u in range(2 * TT)])

        block = ctx.enter_context(nc.Block())

        def turn_bank(kind, k):
            return ps[:, (PJ_ + k) % KT, 0:MEM] if kind == "mem" else ps[:, (2 + k) % KT, :]

        def val_bank(piece):
            return PJ_ if piece % 2 == 0 else 0

        def wait_slab_used(e, kind, n):
            e.wait_ge(slab_used, SLABS.index((kind, n)) + 1)

        def wait_t_drained(e, uses):
            e.wait_ge(t_drained[0], (uses + 1) // 2)
            if uses >= 2:
                e.wait_ge(t_drained[1], uses // 2)

        def wait_pj_all_drained(e, uses):
            e.wait_ge(pj_drained[0], (uses + 1) // 2)
            e.wait_ge(pj_drained[1], uses // 2)

        def gated_by(t):
            return [s for s in SLABS if s[0] == "gate"].index(("gate", t)) + 1

        def wait_head_out(e, t):
            if t >= MEM0:
                step = ("mem", "flush", 0) if t == MIX_TILES - 1 else ("mem", "att", 2 * (t - MEM0) + 2)
                e.wait_ge(o_drained, O_USED[step])
            elif t >= RET0:
                k = T_USED["ret", "turn", t - RET0] - 1
                e.wait_ge(t_drained[k % 2], k // 2 + 1)
            else:
                p = t // 2 * TT + TT - 1
                e.wait_ge(o_drained, O_USED[("pair", "att", p + 2) if p + 2 < PAIRS else ("pair", "flush", 0)])

        RET_PROJ = [("retq", 0), ("retq", 1), ("retk", 0), ("retk", 1)]
        Z_ORDER = [s for s in SLABS if s[0] in ("retq", "retk", "ks", "kw", "q", "gate")]
        ROT_ORDER = [s for s in SLABS if s[0] in ("kc", "ks", "kw", "q")]
        HI_ORDER = [s for s in SLABS if s[0] in ("ks", "kw", "q")]
        PJ_ORDER = [s for s in SLABS if s[0] in PJ_KINDS]
        Z_INDEX = {s: i for i, s in enumerate(Z_ORDER)}
        ROT_INDEX = {s: i for i, s in enumerate(ROT_ORDER)}
        HI_INDEX = {s: i for i, s in enumerate(HI_ORDER)}
        SPLIT_ORDER = [s for s in PJ_ORDER if s[0] in ("memk", "memq")]

        def wait_pj_drained(e, kind, n):
            j = PJ_ORDER.index((kind, n))
            e.wait_ge(pj_drained[j % 2], j // 2 + 1)

        def pj_bank(kind, n):
            return PJ_ + PJ_ORDER.index((kind, n)) % 2

        def z_key_dst(t_hi_or_lo, kind, n):
            if kind == "q":
                return (q_hi if t_hi_or_lo == "hi" else q_lo)[:, n, :]
            keys = keys_hi if t_hi_or_lo == "hi" else keys_lo
            v = keys[:, n, CMP_COLS:].rearrange("p (j b k) -> p b j k", b=2, k=P)
            return v[:, 0 if kind == "ks" else 1, :, :]

        def blocks_of(t):
            return t.rearrange("p (j k) -> p j k", k=P)

        @block.sync
        def _(sp):
            sp.dma_start(mem_nat[:, :, :], mem.rearrange("(t p) d -> p t d", p=P)).then_inc(ld_mem, 16)
            sp.dma_start(par[:, :], small).then_inc(ld_par, 16)
            src = {}
            for i, s in enumerate([s for s in SLABS if s[0] in ("memq", "retq", "retk", "kc", "vc", "ks", "kw", "q", "gate")]):
                src[s] = w_proj[i]
            for v in range(2 * VP):
                src["v", v] = w_val[v]
            for h in range(MEM_HEADS):
                src["memk", h] = w_mem[h]
                src["memv", h] = w_mem[MEM_HEADS + h]
            for n in range(8):
                src["w1k", n] = w_cmp[n]
                src["w1v", n] = w_cmp[8 + n]
            for n in range(MIX_TILES):
                src["out", n] = w_out[n]
            for n, s in enumerate(SLABS):
                if s == ("out", 0):
                    sp.wait_ge(s_full, 2 * MEM_HEADS + 2 * PAIRS)
                    sp.dma_start(x_res[:, :, :], x.rearrange("(t p) d -> p t d", p=P)).then_inc(ld_res, 16)
                    sp.dma_start(gpost_b[:, :], gpost.partition_broadcast(P)).then_inc(ld_post, 16)
                if n >= RING:
                    sp.wait_ge(slab_used, n - RING + 1)
                w = slab_words(s[0])
                sp.dma_start(slab_raw[n % RING][:, 0:w], src[s]).then_inc(slab_loaded[n % RING], 16)
                if n == RING - 1:
                    sp.dma_start(x_nat[:, :, :], x.rearrange("(t p) d -> p t d", p=P)).then_inc(ld_x, 16)
            for u in range(2 * TT):
                t, c = u // 2, slice(u % 2 * T, (u % 2 + 1) * T)
                sp.wait_ge(y_ready, u + 1)
                sp.dma_start(out[t * P:(t + 1) * P, c], y_sb[t % 2][:, c]).then_inc(y_stored[u], 16)
            for u in range(2 * TT):
                sp.wait_ge(y_stored[u], 16)

        @block.gpsimd
        def _(pool):
            count = [0]

            def link(ins):
                count[0] += 1
                ins.then_inc(pool_step, 1)
                pool.wait_ge(pool_step, count[0])

            link(pool.memset(ident[:, :], 0.0))
            pool.affine_select(out=ident[:, :], in_=ident[:, :], compare_op=ALU.not_equal, fill=1.0, base=0,
                               pattern=[[-1, P]], channel_multiplier=1).then_inc(consts_ready, 1)
            pool.memset(power[:, :], -0.5).then_inc(consts_ready, 1)
            
            def power_of(dst, src, ready, n, signal):
                pool.wait_ge(ready, n)
                pool.wait_ge(consts_ready, 2)
                w = src.shape[-1]
                pool.tensor_tensor(dst, src, power[:, 0:w], ALU.pow).then_inc(signal, 1)

            power_of(rstd[:, 0:MT], meansq[:, 0:MT], meansq_ready, 1, rstd_ready)
            power_of(rstd[:, 2:2 + TT], meansq[:, 2:2 + TT], meansq_ready, 2, rstd_ready)
            link(pool.memset(masks_f[:, :], 0.0))
            cw = TT * CMP_COLS
            for i in range(TT):
                m = masks_f[:, (TT - 1 - i) * CMP_COLS:(TT - i) * CMP_COLS]
                pool.affine_select(out=m, in_=m, compare_op=ALU.is_ge, fill=NEG, base=i * P - (CMP_BLOCK - 1),
                                   pattern=[[-CMP_STRIDE, CMP_COLS]], channel_multiplier=1).then_inc(consts_ready, 1)
            m = masks_f[:, cw:]
            pool.affine_select(out=m, in_=m, compare_op=ALU.is_ge, fill=NEG, base=0,
                               pattern=[[0, 2], [-1, P]], channel_multiplier=1).then_inc(consts_ready, 1)
            pool.memset(vc_hi[:, :, :].bitcast(F32), 0.0).then_inc(consts_ready, 1)
            pool.memset(vc_lo[:, :, :].bitcast(F32), 0.0).then_inc(consts_ready, 1)
            pool.wait_ge(turned_x, KT)
            pool.iota(decay_i[:, :], [[1, T]], base=0, channel_multiplier=-1).then_inc(decay_iota, 1)
            wait_slab_used(pool, "memv", 3)
            pool.memset(ret_q[:, :, :], 0.0).then_inc(decay_ready, 1)
            pool.wait_ge(decay_exp, RET_HEADS)
            for h in range(RET_HEADS):
                pool.affine_select(out=decay[:, h, :], in_=decay[:, h, :], compare_op=ALU.is_ge, fill=0.0, base=0,
                                   pattern=[[1, T]], channel_multiplier=-1).then_inc(decay_ready, 1)
            for what, kind, n in SCHEDULE:
                if what in ("slab", "late") and kind in ("retq", "retk"):
                    i = RET_PROJ.index((kind, n))
                    t = z[Z_INDEX[kind, n] % 2]
                    pool.wait_ge(ret_swapped, 4 * (i + 1))
                    pool.wait_ge(rot_ready, 10)
                    pool.tensor_tensor(t[:, :], t[:, :], ret_rot[:, 1, :], ALU.mult).then_inc(ret_sin, 1)
                elif what in ("slab", "late") and kind in ("kc", "ks", "kw", "q"):
                    r = ROT_INDEX[kind, n]
                    t = z_cmp[0:32, n, :] if kind == "kc" else z[Z_INDEX[kind, n] % 2][0:32, :]
                    w = swp[:, :]
                    pool.wait_ge(rot_swapped, r + 1)
                    link(pool.tensor_tensor(w, w, nsa_rot[0:32, 1, :], ALU.mult))
                    link(pool.tensor_tensor(t, t, nsa_rot[0:32, 0, :], ALU.mult))
                    pool.tensor_tensor(t, t, w, ALU.add).then_inc(rot_turned, 1)
                elif (what, kind) == ("ret", "values"):
                    power_of(rstd[:, 6:6 + TT], meansq[:, 6:6 + TT], ret_var, n + 1, ret_rstd)
            for t in range(TT):
                power_of(rstd[:, 10 + t:11 + t], meansq[:, 10 + t:11 + t], y_meansq, t + 1, y_rstd)

        @block.scalar
        def _(act):
            count = [0]

            def link(ins):
                count[0] += 1
                ins.then_inc(act_step, 1)
                act.wait_ge(act_step, count[0])

            act.dma_start(posi[:, :], positions.partition_broadcast(P)).then_inc(ld_pos, 16)
            n_split = [0]

            def split():
                n = n_split[0]
                if n == len(SLABS):
                    return
                n_split[0] += 1
                act.wait_ge(slab_loaded[n % RING], 16 * (n // RING + 1))
                w = slab_words(SLABS[n][0])
                act.activation(slab_hi[n % RING][:, 0:w], slab_raw[n % RING][:, 0:w], ACT.Copy).then_inc(slab_hi_ready, 1)

            t_uses, s_uses, o_uses, z_uses, pvs = [0], [0], [0], [0], [0]
            t_marks = []

            def take_t():
                k = t_uses[0]
                t_uses[0] += 1
                act.wait_ge(t_full, k + 1)
                return k

            def turned_block(w):
                k = take_t()
                if pvs[0] >= 2:
                    act.wait_ge(pv_done, pvs[0] - 1)
                pvs[0] += 1
                act.activation(pt_hi[k % 2][:, 0:w], ps[:, T_ + k % 2, 0:w], ACT.Copy).then_inc(t_hi, 1)

            def head_out(dst, src):
                o_uses[0] += 1
                act.wait_ge(pv_done, pvs[0])
                act.activation(dst, src, ACT.Copy).then_inc(o_drained, 1)

            def mem_exps(u):
                s_uses[0] += 1
                act.wait_ge(bias_ready, s_uses[0])
                if u >= 2:
                    act.wait_ge(t_full, t_marks[u - 2])
                for qt in range(2):
                    ins = act.activation(mprob[u % 2][:, qt, :], ps[:, S_, qt * MEM:(qt + 1) * MEM], ACT.Exp,
                                         bias=nbias[:, u % 2, qt:qt + 1], scale=SCALE, accum_out=ssum[:, u % 2, qt:qt + 1])
                ins.then_inc(s_drained, 1)

            def mem_turned(u):
                turned_block(T)
                t_marks.append(t_uses[0])

            def mem_out(u):
                h, half = u // 2, u % 2
                head_out(mixed[:, MEM0 + h, half * 2 * P:(half + 1) * 2 * P], ps[:, O_, 0:2 * P])

            def head_exps(p, hh):
                _, i, _ = pair_of(p)
                u = s_uses[0]
                s_uses[0] += 1
                act.wait_ge(bias_ready, u + 1)
                if p == 0 and hh == 0:
                    act.wait_ge(t_full, t_uses[0])
                    act.wait_ge(pv_done, pvs[0])
                if hh == 0 and p >= 2:
                    act.wait_ge(t_full, t_marks[p - 2])
                o = prob[p % 2][:, hh, :]
                ob = o[:, CMP_COLS:CMP_COLS + 2 * P * (i + 1)].rearrange("p (j b k) -> p b j k", b=2, k=P)
                flat = ps[:, 0:3, :].rearrange("p s c -> p (s c)")
                sbk = flat[:, 256:256 + 2 * P * (i + 1)].rearrange("p (j b k) -> p b j k", b=2, k=P)
                act.activation(o[:, 0:CMP_COLS], flat[:, 224:256], ACT.Exp, bias=nbias[:, u % 2, 0:1], scale=SCALE,
                               accum_out=ssum[:, u % 2, 0:1])
                for b in range(2):
                    ins = act.activation(ob[:, b, :, :], sbk[:, b, :, :], ACT.Exp, bias=nbias[:, u % 2, 1 + b:2 + b],
                                         scale=SCALE, accum_out=ssum[:, u % 2, 1 + b:2 + b])
                ins.then_inc(s_drained, 1)

            def pair_turned(p, part):
                for j in blocks_of_part(p, part):
                    turned_block(2 * P if j < 0 else T)
                if part == 1:
                    t_marks.append(t_uses[0])

            def pair_out(p):
                g, i, h0 = pair_of(p)
                m0 = NSA0 + PER_GROUP * g + h0
                head_out(mixed[:, m0:m0 + 2, i * P:(i + 1) * P], ps[:, O_, 0:2 * P].rearrange("p (h q) -> p h q", h=2))

            pending = []

            def finish_rot():
                if not pending:
                    return
                kind, n = pending.pop()
                if kind == "kc":
                    return
                act.wait_ge(rot_turned, ROT_INDEX[kind, n] + 1)
                src = z[Z_INDEX[kind, n] % 2][:, :]
                dst = z_key_dst("hi", kind, n)
                act.activation(dst, src if kind == "q" else blocks_of(src), ACT.Copy).then_inc(rot_hi, 1)

            def take_z():
                k = z_uses[0]
                z_uses[0] += 1
                if k >= 2:
                    act.wait_ge(z_done, k - 1)
                return z[k % 2]

            def project(kind, n):
                if kind in ("memk", "memq"):
                    wait_slab_used(act, kind, n)
                    src, dst = ps[:, pj_bank(kind, n), :], mq_hi[:, n, :]
                    if kind == "memk":
                        src, dst = src[:, 0:MEM], mk_hi[:, n, :]
                    act.activation(dst, src, ACT.Copy).then_inc(pj_hi, 1)
                elif kind == "memv" and n == 3:
                    wait_slab_used(act, "memv", 3)
                    act.activation(mv_hi[:, :, :], ps[:, S_:S_ + 2, :], ACT.Copy).then_inc(memv_hi, 1)
                elif kind == "v" and n % 2:
                    piece = n // 2
                    bank = val_bank(piece)
                    wait_slab_used(act, "v", n)
                    src = ps[:, bank:bank + 4, :]
                    if piece < 2:
                        act.activation(v_hi[:, :, piece * VC:(piece + 1) * VC], src[:, :, 0:VC], ACT.Copy).then_inc(val_copied, 1)
                    else:
                        act.activation(ret_v[:, :, (piece - 2) * VC:(piece - 1) * VC], src[:, :, 0:VC], ACT.Copy).then_inc(val_copied, 1)
                    if piece:
                        act.wait_ge(val_drained, piece)
                    act.activation(gate_t[:, :, :], src[:, :, VC:VW], ACT.Tanh, scale=0.5).then_inc(val_tanh, 1)
                elif kind in ("retq", "retk"):
                    wait_slab_used(act, kind, n)
                    t = take_z()
                    for b in range(4):
                        act.activation(t[32 * b:32 * b + 32, :], ps[32 * (b ^ 1):32 * (b ^ 1) + 32, pj_bank(kind, n), :],
                                       ACT.Copy).then_inc(ret_swapped, 1)
                elif kind in ("kc", "vc", "ks", "kw", "q"):
                    wait_slab_used(act, kind, n)
                    if kind in ("kc", "vc"):
                        dst = z_cmp[:, (2 if kind == "vc" else 0) + n, :]
                    else:
                        dst = take_z()[:, :]
                    j = PJ_ORDER.index((kind, n))
                    act.activation(dst, ps[:, PJ_ + j % 2, :], ACT.Copy).then_inc(pj_drained[j % 2], 1)
                    finish_rot()
                    if kind != "vc":
                        pending.append((kind, n))
                elif kind == "gate":
                    finish_rot()
                    wait_slab_used(act, kind, n)
                    t = take_z()
                    act.activation(t[:, :], ps[:, pj_bank(kind, n), :], ACT.Tanh, scale=0.5).then_inc(gate_tanh, 1)

            def late_split(*step):
                if step in LATE:
                    split()

            def late_project(*step):
                if step in LATE:
                    project(*LATE[step])

            def mixed_hi(n):
                if n >= MIX_RING:
                    act.wait_ge(slab_used, SLABS.index(("out", 0)) + n - MIX_RING + 1)
                t = OUT_ORDER[n]
                act.wait_ge(z_done, Z_INDEX["gate", t] + 1)
                act.activation(mix_hi[n % MIX_RING][:, :], mixed[:, t, :], ACT.Copy).then_inc(mix_hi_ready, 1)

            for what, kind, n in SCHEDULE:
                if what == "norm":
                    gain = S_GMEM if kind == "mem" else S_GPRE
                    hi = m_hi if kind == "mem" else h_hi
                    if kind == "mem":
                        act.wait_ge(ld_mem, 16)
                        act.activation(square[:, :], mem_nat[:, 0, :], ACT.Square,
                                       accum_out=sumsq[:, 0:1]).then_inc(squares_done, 1)
                        for _ in range(LEAD):
                            split()
                        act.wait_ge(ld_par, 16)
                    for k in range(KT):
                        src = turn_bank(kind, k)
                        act.wait_ge(turned_mem if kind == "mem" else turned_x, k + 1)
                        act.activation(hi[:, k, :], src, ACT.Copy,
                                       scale=par[:, gain + k:gain + k + 1]).then_inc(mem_hi if kind == "mem" else x_hi, 1)
                    if kind == "x":
                        act.wait_ge(decay_iota, 1)
                        for h in range(RET_HEADS):
                            act.activation(decay[:, h, :], decay_i[:, :], ACT.Exp,
                                           scale=math.log1p(-(2.0 ** (-5 - h)))).then_inc(decay_exp, 1)
                elif what == "square":
                    if n % 2 == 0:
                        act.wait_ge(ld_x, 16)
                        act.wait_ge(squares_done, 1 + n // 2)
                        act.activation(square[:, :], x_nat[:, n, :], ACT.Square,
                                       accum_out=sumsq[:, 2 + n:3 + n]).then_inc(squares_done, 1)
                elif what == "tables":
                    act.wait_ge(consts_ready, 2 + TT + 1)
                    act.activation(ident_r[:, :], ident[:, :], ACT.Copy).then_inc(rounded_ready, 1)
                    act.activation(masks[:, :], masks_f[:, :], ACT.Copy).then_inc(rounded_ready, 1)
                    act.wait_ge(angles_ready, 1)
                    for b in range(4):
                        act.activation(ret_rot[32 * b:32 * b + 32, 0, :], ang[0:32, :], ACT.Sin).then_inc(rot_ready, 1)
                        act.activation(ret_rot[32 * b:32 * b + 32, 1, :], ang[32:64, :], ACT.Sin,
                                       scale=1.0 if b % 2 else -1.0).then_inc(rot_ready, 1)
                    for v in range(2):
                        act.activation(nsa_rot[0:32, v, :], ang[64 + 32 * v:96 + 32 * v, :], ACT.Sin).then_inc(rot_ready, 1)
                elif what == "slab":
                    split()
                    if kind != "out":
                        project(kind, n)
                    elif n + LEAD < MIX_TILES:
                        mixed_hi(n + LEAD)
                elif what == "mem" and kind == "att":
                    if n:
                        mem_turned(n - 1)
                    late_split(what, kind, n)
                    mem_exps(n)
                    late_project(what, kind, n)
                    if n:
                        mem_out(n - 1)
                elif what == "mem":
                    mem_turned(2 * MEM_HEADS - 1)
                    late_split(what, kind, n)
                    late_project(what, kind, n)
                    mem_out(2 * MEM_HEADS - 1)
                    t_marks.clear()
                elif what == "rot":
                    finish_rot()
                elif (what, kind) == ("ret", "scores"):
                    t_uses[0] += TT
                elif (what, kind) == ("ret", "values"):
                    o_uses[0] += 1
                elif (what, kind) == ("ret", "turn"):
                    k = take_t()
                    act.activation(mixed[:, RET0 + n, :], ps[:, T_ + k % 2, :], ACT.Copy,
                                   scale=par[:, S_GN + n:S_GN + n + 1]).then_inc(t_drained[k % 2], 1)
                elif what == "blocks":
                    i = 0 if kind == "k" else 1
                    act.wait_ge(blk_sum, i + 1)
                    if i:
                        wait_slab_used(act, "w1k", 7)
                    act.activation(blk_hi[:, :], blk[:, :], ACT.Copy).then_inc(blk_hi_ready, 1)
                elif what == "hidden":
                    i = 0 if kind == "k" else 1
                    o_uses[0] += 1
                    wait_slab_used(act, "w1" + kind, 7)
                    if i:
                        act.wait_ge(t_full, t_uses[0])
                    act.activation(hid[0:BLK_N, 0, :], ps[0:BLK_N, O_, 0:CMP_HIDDEN], ACT.Copy).then_inc(o_drained, 1)
                    act.wait_ge(o_drained, o_uses[0])
                    act.activation(hid[0:BLK_N, 1, :], hid[0:BLK_N, 0, :], ACT.Square).then_inc(hid_sq, 1)
                    act.wait_ge(hid_poly, i + 1)
                    act.activation(hid[0:BLK_N, 3, :], hid[0:BLK_N, 2, :], ACT.Tanh,
                                   scale=math.sqrt(2.0 / math.pi)).then_inc(hid_tanh, 1)
                elif what == "mlp":
                    k = take_t()
                    act.activation(hid_t[:, :, :], ps[:, T_ + k % 2, 0:2 * P].rearrange("p (c r) -> p c r", c=2)[:, :, 0:BLK_N],
                                   ACT.Copy, scale=0.5).then_inc(t_drained[k % 2], 1)
                    k = take_t()
                    if kind == "k":
                        act.activation(keys_hi[:, :, 0:N_CMP], ps[:, T_ + k % 2, 0:BLK_N].rearrange("p (g n) -> p g n", g=2),
                                       ACT.Copy).then_inc(t_hi, 1)
                    else:
                        act.activation(vc_hi[0:N_CMP, :, :], ps[0:N_CMP, T_ + k % 2, 0:2 * P].rearrange("p (g n) -> p g n", g=2),
                                       ACT.Copy).then_inc(t_hi, 1)
                elif what == "pair" and kind == "att":
                    for hh in range(2):
                        pp = parts_of_step(kind, n, hh)
                        if pp:
                            pair_turned(*pp)
                        if hh == 0:
                            late_split(what, kind, n)
                            late_project(what, kind, n)
                        head_exps(n, hh)
                        if pp and pp[1]:
                            pair_out(pp[0])
                elif what == "pair":
                    for hh in range(3):
                        pp = parts_of_step(kind, n, hh)
                        pair_turned(*pp)
                        if pp[1]:
                            pair_out(pp[0])
                    for m in range(LEAD):
                        mixed_hi(m)
            for u in range(2 * TT):
                act.wait_ge(y_full, u + 1)
                if u:
                    act.wait_ge(y_squared, u)
                act.activation(y_sq[:, :], ps[:, u, :], ACT.Square,
                               accum_out=sumsq[:, S_Y + u:S_Y + u + 1]).then_inc(y_squared, 1)

        @block.vector
        def _(dve):
            count = [0]

            def link(ins):
                count[0] += 1
                ins.then_inc(dve_step, 1)
                dve.wait_ge(dve_step, count[0])

            n_split = [0]

            def split():
                n = n_split[0]
                if n == len(SLABS):
                    return
                n_split[0] += 1
                dve.wait_ge(slab_hi_ready, n + 1)
                w = slab_words(SLABS[n][0])
                dve.tensor_tensor(slab_lo[n % RING][:, 0:w], slab_raw[n % RING][:, 0:w],
                                  slab_hi[n % RING][:, 0:w].bitcast(F32), ALU.subtract).then_inc(slab_lo_ready, 1)

            t_uses, t_his, s_uses, z_uses = [0], [0], [0], [0]

            def take_t_hi():
                k = t_uses[0]
                t_uses[0] += 1
                t_his[0] += 1
                dve.wait_ge(t_hi, t_his[0])
                return k

            def turned_block(w):
                k = take_t_hi()
                dve.tensor_tensor(pt_lo[k % 2][:, 0:w], ps[:, T_ + k % 2, 0:w], pt_hi[k % 2][:, 0:w].bitcast(F32),
                                  ALU.subtract).then_inc(t_drained[k % 2], 1)

            def row_norms(r0, nr, part, squares):
                dve.wait_ge(squares_done, squares)
                dve.tensor_scalar(meansq[:, r0:r0 + nr], sumsq[:, r0:r0 + nr], 1.0 / D, EPS, ALU.mult,
                                  ALU.add).then_inc(meansq_ready, 1)
                dve.wait_ge(rstd_ready, part)

            def scale_row(nat, r0, r):
                dve.tensor_scalar(nat[:, r, :], nat[:, r, :], rstd[:, r0 + r:r0 + r + 1], None, ALU.mult).then_inc(normed, 1)

            def mem_front(u):
                s_uses[0] += 1
                dve.wait_ge(s_full, s_uses[0])
                link(dve.tensor_reduce(smax[:, u % 2, 0:2], ps[:, S_, :].rearrange("p (q k) -> p q k", q=2), AX.X, ALU.max))
                dve.tensor_scalar(nbias[:, u % 2, 0:2], smax[:, u % 2, 0:2], -SCALE, None, ALU.mult).then_inc(bias_ready, 1)

            def mem_back(u):
                dve.wait_ge(s_drained, s_uses[0])
                link(dve.reciprocal(coef[:, u % 2, 0:2], ssum[:, u % 2, 0:2]))
                for qt in range(2):
                    ins = dve.tensor_scalar(mprob[u % 2][:, qt, :], mprob[u % 2][:, qt, :], coef[:, u % 2, qt:qt + 1],
                                            None, ALU.mult)
                ins.then_inc(prob_ready, 1)

            def head_front(p, hh):
                g, i, h0 = pair_of(p)
                u = s_uses[0]
                s_uses[0] += 1
                dve.wait_ge(s_full, u + 1)
                flat = ps[:, 0:3, :].rearrange("p s c -> p (s c)")
                dve.tensor_reduce(smax[:, u % 2, 0:1], flat[:, 224:256], AX.X, ALU.max)
                view = flat[:, 256:256 + 2 * P * (i + 1)].rearrange("p (j b k) -> p b j k", b=2, k=P)
                link(dve.tensor_reduce(smax[:, u % 2, 1:3], view, AX.XY, ALU.max))
                dve.tensor_scalar(nbias[:, u % 2, 0:3], smax[:, u % 2, 0:3], 0.1 * NEG, -SCALE, ALU.max,
                                  ALU.mult).then_inc(bias_ready, 1)

            def head_back(p, hh):
                g, i, h0 = pair_of(p)
                u = s_uses[0] - 1
                dve.wait_ge(s_drained, u + 1)
                head = PER_GROUP * g + h0 + hh
                c = coef[:, u % 2, 0:3]
                link(dve.tensor_scalar(c, ssum[:, u % 2, 0:3], 1e-30, None, ALU.max))
                link(dve.reciprocal(c, c))
                link(dve.tensor_tensor(c, c, gates[:, i, head:3 * HEADS:HEADS], ALU.mult))
                o = prob[p % 2][:, hh, :]
                ob = o[:, CMP_COLS:CMP_COLS + 2 * P * (i + 1)].rearrange("p (j b k) -> p b j k", b=2, k=P)
                dve.tensor_scalar(o[:, 0:CMP_COLS], o[:, 0:CMP_COLS], coef[:, u % 2, 0:1], None, ALU.mult)
                for b in range(2):
                    ins = dve.tensor_scalar(ob[:, b, :, :], ob[:, b, :, :], coef[:, u % 2, 1 + b:2 + b], None, ALU.mult)
                ins.then_inc(prob_ready, 1)

            pending = []

            def finish_rot():
                if not pending:
                    return
                kind, n = pending.pop()
                if kind == "kc":
                    return
                dve.wait_ge(rot_hi, HI_INDEX[kind, n] + 1)
                src = z[Z_INDEX[kind, n] % 2][:, :]
                hi, lo = z_key_dst("hi", kind, n), z_key_dst("lo", kind, n)
                dve.tensor_tensor(lo, src if kind == "q" else blocks_of(src), hi.bitcast(F32),
                                  ALU.subtract).then_inc(z_done, 1)

            def project(kind, n):
                if kind in ("memk", "memq"):
                    j = PJ_ORDER.index((kind, n))
                    dve.wait_ge(pj_hi, SPLIT_ORDER.index((kind, n)) + 1)
                    src, hi, lo = ps[:, PJ_ + j % 2, :], mq_hi[:, n, :], mq_lo[:, n, :]
                    if kind == "memk":
                        src, hi, lo = src[:, 0:MEM], mk_hi[:, n, :], mk_lo[:, n, :]
                    dve.tensor_tensor(lo, src, hi.bitcast(F32), ALU.subtract).then_inc(pj_drained[j % 2], 1)
                elif kind == "memv" and n == 3:
                    dve.wait_ge(memv_hi, 1)
                    dve.tensor_tensor(mv_lo[:, :, :], ps[:, S_:S_ + 2, :], mv_hi[:, :, :].bitcast(F32),
                                      ALU.subtract).then_inc(memv_drained, 1)
                elif kind == "v" and n % 2:
                    piece = n // 2
                    bank = val_bank(piece)
                    if piece < 2:
                        c = slice(piece * VC, (piece + 1) * VC)
                        dve.wait_ge(val_tanh, piece + 1)
                        dve.tensor_tensor(v_lo[:, :, c], ps[:, bank:bank + 4, 0:VC], v_hi[:, :, c].bitcast(F32), ALU.subtract)
                    dve.wait_ge(val_tanh, piece + 1)
                    dve.tensor_scalar(gates[:, :, piece * GC:(piece + 1) * GC], gate_t[:, :, :], 1.0, 0.5, ALU.add,
                                      ALU.mult).then_inc(val_drained, 1)
                elif kind in ("retq", "retk"):
                    i = RET_PROJ.index((kind, n))
                    j = PJ_ORDER.index((kind, n))
                    dve.wait_ge(ret_swapped, 4 * (i + 1))
                    dve.wait_ge(rot_ready, 8)
                    if i == 0:
                        dve.wait_ge(decay_ready, 1)
                    else:
                        dve.wait_ge(z_done, z_uses[0])
                    dve.tensor_tensor(ret_z[:, :], ps[:, PJ_ + j % 2, :], ret_rot[:, 0, :], ALU.mult).then_inc(pj_drained[j % 2], 1)
                    dve.wait_ge(pj_drained[j % 2], j // 2 + 1)
                    dve.wait_ge(ret_sin, i + 1)
                    t = z[z_uses[0] % 2]
                    z_uses[0] += 1
                    if kind == "retk":
                        dve.tensor_tensor(ret_k[:, n, :], ret_z[:, :], t[:, :], ALU.add).then_inc(z_done, 1)
                    else:
                        for hh in range(2):
                            r = slice(64 * hh, 64 * hh + 64)
                            ins = dve.tensor_tensor(ret_q[r, 2 * n + hh, :], ret_z[r, :], t[r, :], ALU.add)
                        ins.then_inc(z_done, 1)
                elif kind in ("kc", "vc", "ks", "kw", "q"):
                    if kind != "vc":
                        wait_pj_drained(dve, kind, n)
                        r = ROT_INDEX[kind, n]
                        if r:
                            dve.wait_ge(rot_turned, r)
                        if kind == "kc":
                            src = z_cmp[0:32, n, :]
                        else:
                            src = z[z_uses[0] % 2][0:32, :]
                            z_uses[0] += 1
                        dve.stream_shuffle(swp[:, :], src, [(i + 16) % 32 for i in range(32)]).then_inc(rot_swapped, 1)
                    finish_rot()
                    if kind != "vc":
                        pending.append((kind, n))
                elif kind == "gate":
                    finish_rot()
                    t = z[z_uses[0] % 2]
                    z_uses[0] += 1
                    j = PJ_ORDER.index((kind, n))
                    dve.wait_ge(gate_tanh, gated_by(n))
                    dve.scalar_tensor_tensor(t[:, :], t[:, :], 1.0, ps[:, PJ_ + j % 2, :], ALU.add, ALU.mult).then_inc(pj_drained[j % 2], 1)
                    dve.wait_ge(pj_drained[j % 2], j // 2 + 1)
                    wait_head_out(dve, n)
                    dve.scalar_tensor_tensor(mixed[:, n, :], t[:, :], 0.5, mixed[:, n, :], ALU.mult, ALU.mult).then_inc(z_done, 1)

            def late_split(*step):
                if step in LATE:
                    split()

            def late_project(*step):
                if step in LATE:
                    project(*LATE[step])

            def mixed_lo(n):
                t = OUT_ORDER[n]
                dve.wait_ge(mix_hi_ready, n + 1)
                dve.tensor_tensor(mix_lo[n % MIX_RING][:, :], mixed[:, t, :], mix_hi[n % MIX_RING][:, :].bitcast(F32),
                                  ALU.subtract).then_inc(mix_ready, 1)

            for what, kind, n in SCHEDULE:
                if what == "norm":
                    gain = S_GMEM if kind == "mem" else S_GPRE
                    hi, lo = (m_hi, m_lo) if kind == "mem" else (h_hi, h_lo)
                    if kind == "mem":
                        dve.wait_ge(ld_mem, 16)
                        link(dve.scalar_tensor_tensor(square_v[:, :], mem_nat[:, 1, :], 1.0, mem_nat[:, 1, :], ALU.mult,
                                                      ALU.mult, accum_out=sumsq[:, 1:2]))
                        row_norms(0, MT, 1, 1)
                        for r in range(MT):
                            scale_row(mem_nat, 0, r)
                        split()
                        dve.wait_ge(ld_par, 16)
                    for k in range(KT):
                        dve.wait_ge(mem_hi if kind == "mem" else x_hi, k + 1)
                        dve.scalar_tensor_tensor(lo[:, k, :], turn_bank(kind, k), par[:, gain + k:gain + k + 1],
                                                 hi[:, k, :].bitcast(F32), ALU.mult,
                                                 ALU.subtract).then_inc(mem_lo if kind == "mem" else x_lo, 1)
                    if kind == "mem":
                        split()
                elif what == "square":
                    if n % 2:
                        dve.wait_ge(ld_x, 16)
                        link(dve.scalar_tensor_tensor(square_v[:, :], x_nat[:, n, :], 1.0, x_nat[:, n, :], ALU.mult,
                                                      ALU.mult, accum_out=sumsq[:, 2 + n:3 + n]))
                elif what == "scale":
                    if n == 0:
                        row_norms(2, TT, 2, 1 + TT // 2)
                    scale_row(x_nat, 2, n)
                elif what == "angles":
                    dve.wait_ge(ld_pos, 16)
                    link(dve.tensor_copy(posf[:, :], posi[:, :]))
                    dve.wait_ge(ld_par, 16)
                    link(dve.tensor_scalar(ang[:, :], posf[:, :], par[:, S_FREQ:S_FREQ + 1], None, ALU.mult))
                    magic = 12582912.0
                    link(dve.tensor_scalar(turns[:, :], ang[:, :], 1.0 / (2 * math.pi), par[:, S_FREQ + 1:S_FREQ + 2],
                                           ALU.mult, ALU.add))
                    link(dve.tensor_scalar(turns[:, :], turns[:, :], magic, None, ALU.add))
                    link(dve.tensor_scalar(turns[:, :], turns[:, :], magic, None, ALU.subtract))
                    c1 = 6.28125
                    c2 = float(np.float32(round((2 * math.pi - c1) * 2 ** 19) / 2 ** 19))
                    for c in (c1, c2, 2 * math.pi - c1 - c2):
                        link(dve.scalar_tensor_tensor(ang[:, :], turns[:, :], -c, ang[:, :], ALU.mult, ALU.add))
                    link(dve.tensor_scalar(ang[:, :], ang[:, :], par[:, S_FREQ + 2:S_FREQ + 3], None, ALU.add))
                    dve.tensor_scalar(ang[:, :], ang[:, :], 3.1415925, -3.1415925, ALU.min, ALU.max).then_inc(angles_ready, 1)
                elif what == "slab":
                    split()
                    if kind != "out":
                        project(kind, n)
                    elif n + LEAD < MIX_TILES:
                        mixed_lo(n + LEAD)
                elif what == "mem" and kind == "att":
                    if n:
                        turned_block(T)
                    mem_front(n)
                    late_split(what, kind, n)
                    mem_back(n)
                    late_project(what, kind, n)
                elif what == "mem":
                    turned_block(T)
                    late_split(what, kind, n)
                    late_project(what, kind, n)
                elif what == "rot":
                    finish_rot()
                elif (what, kind) == ("ret", "scores"):
                    if n == 0:
                        dve.wait_ge(decay_ready, 1 + RET_HEADS)
                    off = 0
                    if n >= 2:
                        dve.wait_ge(ret_full, n - 1)
                    for j in range(TT):
                        k = t_uses[0]
                        t_uses[0] += 1
                        w = T - P * j
                        dve.wait_ge(t_full, k + 1)
                        dve.scalar_tensor_tensor(inner[n % 2][:, off:off + w], ps[:, T_ + k % 2, 0:w], RET_QK ** -0.5,
                                                 decay[:, n, 0:w], ALU.mult, ALU.mult).then_inc(t_drained[k % 2], 1)
                        off += w
                elif (what, kind) == ("ret", "values"):
                    dve.wait_ge(ret_full, n + 1)
                    for i in range(TT):
                        ins = dve.bn_stats(bn[:, i, :], ps[:, O_, i * P:(i + 1) * P])
                    link(ins)
                    for i in range(TT):
                        ins = dve.bn_aggr(mv[:, i, :], bn[:, i, :])
                    link(ins)
                    dve.tensor_scalar(meansq[:, 6:6 + TT], mv[:, :, 1], EPS, None, ALU.add).then_inc(ret_var, 1)
                    dve.wait_ge(ret_rstd, n + 1)
                    if n >= 2:
                        dve.wait_ge(t_full, T_USED["ret", "turn", n - 2])
                    for i in range(TT):
                        ins = dve.tensor_scalar(ret_n[n % 2][:, i, :], ps[:, O_, i * P:(i + 1) * P], mv[:, i, 0:1],
                                                rstd[:, 6 + i:7 + i], ALU.subtract, ALU.mult)
                    ins.then_inc(o_drained, 1)
                elif (what, kind) == ("ret", "turn"):
                    t_uses[0] += 1
                elif what == "blocks":
                    i = 0 if kind == "k" else 1
                    if i == 0:
                        dve.wait_ge(rot_turned, 2)
                        for g in range(GROUPS):
                            wait_pj_drained(dve, "vc", g)
                        dve.wait_ge(ret_full, RET_HEADS)
                        link(dve.memset(blk[:, CMP_BLOCK * BLK_N:], 0.0))
                    else:
                        dve.wait_ge(blk_ready, 1)
                    pos = par[:, S_POS + CMP_BLOCK * i:S_POS + CMP_BLOCK * (i + 1)]
                    bv = blk[:, 0:CMP_BLOCK * BLK_N].rearrange("p (c g n) -> p c g n", g=GROUPS, n=N_CMP)
                    for g in range(GROUPS):
                        zc = z_cmp[:, 2 * i + g, :].rearrange("p (n s) -> p s n", s=CMP_STRIDE)
                        for half in range(2):
                            c = slice(half * CMP_STRIDE, (half + 1) * CMP_STRIDE)
                            ins = dve.tensor_tensor(bv[:, c, g, :], zc[:, :, half:half + N_CMP],
                                                    pos[:, c].unsqueeze(2).to_broadcast([P, CMP_STRIDE, N_CMP]), ALU.add)
                    ins.then_inc(blk_sum, 1)
                    dve.wait_ge(blk_hi_ready, i + 1)
                    dve.tensor_tensor(blk_lo[:, :], blk[:, :], blk_hi[:, :].bitcast(F32), ALU.subtract).then_inc(blk_ready, 1)
                elif what == "hidden":
                    i = 0 if kind == "k" else 1
                    dve.wait_ge(hid_sq, i + 1)
                    a = hid[0:BLK_N, 2, :]
                    link(dve.tensor_scalar(a, hid[0:BLK_N, 1, :], 0.044715, 1.0, ALU.mult, ALU.add))
                    dve.tensor_tensor(a, a, hid[0:BLK_N, 0, :], ALU.mult).then_inc(hid_poly, 1)
                    dve.wait_ge(hid_tanh, i + 1)
                    dve.scalar_tensor_tensor(hid[0:BLK_N, 3, :], hid[0:BLK_N, 3, :], 1.0, hid[0:BLK_N, 0, :], ALU.add,
                                             ALU.mult).then_inc(hid_ready, 1)
                elif what == "mlp":
                    t_uses[0] += 1
                    k = take_t_hi()
                    if kind == "k":
                        dve.memset(keys_hi[:, :, N_CMP:CMP_COLS].bitcast(F32), 0.0)
                        dve.memset(keys_lo[:, :, N_CMP:CMP_COLS].bitcast(F32), 0.0)
                        dve.tensor_tensor(keys_lo[:, :, 0:N_CMP], ps[:, T_ + k % 2, 0:BLK_N].rearrange("p (g n) -> p g n", g=2),
                                          keys_hi[:, :, 0:N_CMP].bitcast(F32), ALU.subtract).then_inc(t_drained[k % 2], 1)
                    else:
                        dve.tensor_tensor(vc_lo[0:N_CMP, :, :], ps[0:N_CMP, T_ + k % 2, 0:2 * P].rearrange("p (g n) -> p g n", g=2),
                                          vc_hi[0:N_CMP, :, :].bitcast(F32), ALU.subtract).then_inc(t_drained[k % 2], 1)
                elif what == "pair" and kind == "att":
                    for hh in range(2):
                        pp = parts_of_step(kind, n, hh)
                        widths = [2 * P if j < 0 else T for j in blocks_of_part(*pp)] if pp else []
                        for w in widths[:2]:
                            turned_block(w)
                        head_front(n, hh)
                        for w in widths[2:]:
                            turned_block(w)
                        if hh == 0:
                            late_split(what, kind, n)
                            late_project(what, kind, n)
                        head_back(n, hh)
                elif what == "pair":
                    for hh in range(3):
                        for j in blocks_of_part(*parts_of_step(kind, n, hh)):
                            turned_block(2 * P if j < 0 else T)
                    for m in range(LEAD):
                        mixed_lo(m)
            dve.wait_ge(ld_res, 16)
            dve.wait_ge(ld_post, 16)
            for t in range(TT):
                m = meansq[:, 10 + t:11 + t]
                dve.wait_ge(y_squared, 2 * t + 2)
                link(dve.tensor_tensor(m, sumsq[:, S_Y + 2 * t:S_Y + 2 * t + 1], sumsq[:, S_Y + 2 * t + 1:S_Y + 2 * t + 2], ALU.add))
                dve.tensor_scalar(m, m, 1.0 / D, EPS, ALU.mult, ALU.add).then_inc(y_meansq, 1)
                dve.wait_ge(y_rstd, t + 1)
                for half in range(2):
                    c = slice(half * T, (half + 1) * T)
                    y = y_sb[t % 2][:, c]
                    if t >= 2:
                        dve.wait_ge(y_stored[2 * (t - 2) + half], 16)
                    link(dve.scalar_tensor_tensor(y, ps[:, 2 * t + half, :], rstd[:, 10 + t:11 + t], gpost_b[:, c], ALU.mult, ALU.mult))
                    dve.tensor_tensor(y, y, x_res[:, t, c], ALU.add).then_inc(y_ready, 1)

        @block.tensor
        def _(pe):
            t_uses, s_uses, o_uses, slabs, pts = [0], [0], [0], [0], [0]

            def take_t():
                k = t_uses[0]
                t_uses[0] += 1
                if k >= 2:
                    pe.wait_ge(t_drained[k % 2], k // 2)
                return k

            def product(dst, w, m, first=True, last=True):
                pe.matmul(dst, w[0], m[0], start=first, stop=False)
                pe.matmul(dst, w[0], m[1], start=False, stop=False)
                return pe.matmul(dst, w[1], m[0], start=False, stop=last)

            def turn_blocks(blocks):
                k = take_t()
                for c, src in enumerate(blocks):
                    ins = pe.transpose(ps[:, T_ + k % 2, c * P:(c + 1) * P], src, ident[:, :])
                ins.then_inc(t_full, 1)
                return k

            def o_bank():
                if o_uses[0]:
                    pe.wait_ge(o_drained, o_uses[0])
                o_uses[0] += 1

            def wait_turned(k):
                pe.wait_ge(t_drained[k % 2], k // 2 + 1)

            def mem_scores(u):
                h, half = u // 2, u % 2
                if s_uses[0]:
                    pe.wait_ge(s_drained, s_uses[0])
                s_uses[0] += 1
                for qt in range(2):
                    c = slice((2 * half + qt) * P, (2 * half + qt + 1) * P)
                    ins = product(ps[:, S_, qt * MEM:(qt + 1) * MEM], (mq_hi[:, h, c], mq_lo[:, h, c]),
                                  (mk_hi[:, h, :], mk_lo[:, h, :]))
                ins.then_inc(s_full, 1)

            def mem_turn(u):
                pe.wait_ge(prob_ready, u + 1)
                return turn_blocks([mprob[u % 2][:, qt, kt * P:(kt + 1) * P] for kt in range(MT) for qt in range(2)])

            def mem_values(u, k):
                h = u // 2
                o_bank()
                wait_turned(k)
                c = slice(h * DH, (h + 1) * DH)
                for kt in range(MT):
                    m = slice(kt * 2 * P, (kt + 1) * 2 * P)
                    ins = product(ps[:, O_, 0:2 * P], (mv_hi[:, kt, c], mv_lo[:, kt, c]),
                                  (pt_hi[k % 2][:, m], pt_lo[k % 2][:, m]), kt == 0, kt == MT - 1)
                ins.then_inc(pv_done, 1)

            def head_scores(p, hh):
                g, i, h0 = pair_of(p)
                h = PER_GROUP * g + h0 + hh
                if s_uses[0]:
                    pe.wait_ge(s_drained, s_uses[0])
                s_uses[0] += 1
                c = slice(i * P, (i + 1) * P)
                q = (q_hi[:, h, c], q_lo[:, h, c])
                cw = TT * CMP_COLS
                cuts = [(0, CMP_COLS + 2 * P, S_, 224, [(CMP_COLS, 224, (TT - 1 - i) * CMP_COLS)])]
                if i == 0:
                    cuts[0][4][0] = (CMP_COLS + 2 * P, 224, cw - CMP_COLS)
                else:
                    cuts.append((CMP_COLS + 2 * P, 2 * P * min(i, 2), S_ + 1, 0, [(2 * P, 2 * P * (i - 1), cw)]))
                if i == 3:
                    cuts[1][4].clear()
                    cuts.append((CMP_COLS + 6 * P, 2 * P, S_ + 2, 0, [(2 * P, 0, cw)]))
                for k0, w, bank, col, spans in cuts:
                    dst, k_hi, k_lo = ps[:, bank, col:col + w], keys_hi[:, g, k0:k0 + w], keys_lo[:, g, k0:k0 + w]
                    pe.matmul(dst, q[0], k_hi, start=True, stop=False)
                    for mw, mc, m0 in spans:
                        pe.matmul(ps[:, bank, mc:mc + mw], ident_r[:, :], masks[:, m0:m0 + mw], start=False, stop=False)
                    pe.matmul(dst, q[0], k_lo, start=False, stop=False)
                    ins = pe.matmul(dst, q[1], k_hi, start=False, stop=True)
                ins.then_inc(s_full, 1)

            def turn_pair_block(p, j):
                pr = prob[p % 2]
                if j < 0:
                    return turn_blocks([pr[:, hh, 0:P] for hh in range(2)])
                c = CMP_COLS + 2 * P * j
                return turn_blocks([pr[:, hh, c + b * P:c + (b + 1) * P] for b in range(2) for hh in range(2)])

            def block_values(p, j, k):
                g, i, _ = pair_of(p)
                if j < 0:
                    o_bank()
                wait_turned(k)
                if j < 0:
                    ins = product(ps[:, O_, 0:2 * P], (vc_hi[:, g, :], vc_lo[:, g, :]),
                                  (pt_hi[k % 2][:, 0:2 * P], pt_lo[k % 2][:, 0:2 * P]), True, False)
                else:
                    for b in range(2):
                        c = slice(b * VC + g * DH, b * VC + (g + 1) * DH)
                        m = slice(b * 2 * P, (b + 1) * 2 * P)
                        ins = product(ps[:, O_, 0:2 * P], (v_hi[:, j, c], v_lo[:, j, c]),
                                      (pt_hi[k % 2][:, m], pt_lo[k % 2][:, m]), False, j == i and b == 1)
                ins.then_inc(pv_done, 1)

            def pair_half(pp, scores):
                todo = blocks_of_part(*pp) if pp else []
                turned = []
                if pp and pp[1] == 0:
                    pe.wait_ge(prob_ready, 2 * MEM_HEADS + 2 * (pp[0] + 1))
                while todo and len(turned) < 2:
                    turned.append((todo[0], turn_pair_block(pp[0], todo.pop(0))))
                if scores:
                    head_scores(*scores)
                fill(1)
                while turned:
                    block_values(pp[0], *turned.pop(0))
                    if todo:
                        turned.append((todo[0], turn_pair_block(pp[0], todo.pop(0))))
                    fill(1)
                fill(1)

            running = []

            def fill(chunks):
                if not running:
                    if SLABS[slabs[0]][0] not in PJ_KINDS:
                        return
                    running.append(project(*SLABS[slabs[0]]))
                for _ in range(chunks):
                    if next(running[0], None) is None:
                        return

            def finish_slab():
                for _ in (running.pop() if running else project(*SLABS[slabs[0]])):
                    pass
                slabs[0] += 1

            def project(kind, n):
                s = slabs[0]
                pe.wait_ge(slab_lo_ready, s + 1)
                hi, lo = slab_hi[s % RING], slab_lo[s % RING]
                if kind in PJ_KINDS:
                    j = PJ_ORDER.index((kind, n))
                    if j >= 2:
                        pe.wait_ge(pj_drained[j % 2], j // 2)
                    if j in (4, 5):
                        pe.wait_ge(val_drained, VP - 1)
                    mh, ml, w = (m_hi, m_lo, MEM) if kind == "memk" else (h_hi, h_lo, T)
                    for k in range(KT):
                        c = slice(k * P, (k + 1) * P)
                        if kind == "memk" and n < 2:
                            pe.wait_ge(mem_lo, max(k, n) + 1)
                        ins = product(ps[:, PJ_ + j % 2, 0:w], (hi[:, c], lo[:, c]), (mh[:, k, :], ml[:, k, :]),
                                      k == 0, k == KT - 1)
                        if k < KT - 1:
                            yield True
                elif kind == "memv":
                    if n == 0:
                        pe.wait_ge(mem_lo, KT)
                    for kk in range(2):
                        c = slice(kk * T, (kk + 1) * T)
                        for t in range(MT):
                            r = slice(t * P, (t + 1) * P)
                            k = 2 * n + kk
                            ins = product(ps[:, S_ + t, :], (m_hi[:, k, r], m_lo[:, k, r]), (hi[:, c], lo[:, c]),
                                          k == 0, k == KT - 1)
                elif kind == "v":
                    piece, half = n // 2, n % 2
                    if half == 0:
                        if piece == 0:
                            pe.wait_ge(x_lo, 6)
                        elif piece >= 2:
                            pe.wait_ge(val_drained, piece - 1)
                    elif piece == 0:
                        pe.wait_ge(x_lo, KT)
                    bank = val_bank(piece)
                    for t in range(TT):
                        r = slice(t * P, (t + 1) * P)
                        for kk in range(4):
                            k = 4 * half + kk
                            c = slice(kk * VW, (kk + 1) * VW)
                            ins = product(ps[:, bank + t, 0:VW], (h_hi[:, k, r], h_lo[:, k, r]), (hi[:, c], lo[:, c]),
                                          k == 0, k == KT - 1)
                elif kind in ("w1k", "w1v"):
                    if n == 0:
                        o_bank()
                        pe.wait_ge(blk_ready, 1 if kind == "w1k" else 2)
                    for cc in range(W1_C):
                        c = W1_C * n + cc
                        b = slice(c * BLK_N, c * BLK_N + P)
                        m = slice(cc * CMP_HIDDEN, (cc + 1) * CMP_HIDDEN)
                        ins = product(ps[:, O_, 0:CMP_HIDDEN], (blk_hi[:, b], blk_lo[:, b]), (hi[:, m], lo[:, m]),
                                      c == 0, c == CMP_BLOCK - 1)
                ins.then_inc(slab_used, 1)

            def out_products(n, t, half, s):
                hi, lo = slab_hi[s % RING], slab_lo[s % RING]
                r = slice(t * P, (t + 1) * P)
                c = slice(half * T, (half + 1) * T)
                return product(ps[:, 2 * t + half, :], (mix_hi[n % MIX_RING][:, r], mix_lo[n % MIX_RING][:, r]),
                               (hi[:, c], lo[:, c]), n == 0, n == MIX_TILES - 1)

            for what, kind, n in SCHEDULE:
                if what == "norm":
                    if kind == "mem":
                        pe.wait_ge(consts_ready, 1)
                    pe.wait_ge(normed, MT if kind == "mem" else MT + TT)
                    nat, rows = (mem_nat, MT) if kind == "mem" else (x_nat, TT)
                    for k in range(KT):
                        if kind == "x" and k == 6:
                            pe.wait_ge(memv_drained, 1)
                        if kind == "x" and k == 2:
                            wait_pj_all_drained(pe, MEM_HEADS)
                        dst = turn_bank(kind, k)
                        for r in range(rows):
                            ins = pe.transpose(dst[:, r * P:(r + 1) * P], nat[:, r, k * P:(k + 1) * P], ident[:, :])
                        ins.then_inc(turned_x if kind == "x" else turned_mem, 1)
                elif what in ("slab", "late") and kind != "out":
                    finish_slab()
                elif what == "mem" and kind == "att":
                    if n == 0:
                        pe.wait_ge(val_drained, VP)
                        pe.wait_ge(pj_drained[0], 4)
                        pe.wait_ge(pj_drained[1], 4)
                    if n:
                        k = mem_turn(n - 1)
                    mem_scores(n)
                    fill(2)
                    if n:
                        mem_values(n - 1, k)
                    fill(2)
                elif what == "mem":
                    k = mem_turn(2 * MEM_HEADS - 1)
                    fill(4)
                    mem_values(2 * MEM_HEADS - 1, k)
                elif (what, kind) == ("ret", "scores"):
                    if n == 0:
                        pe.wait_ge(z_done, len(RET_PROJ))
                    for j in range(TT):
                        k = take_t()
                        pe.matmul(ps[:, T_ + k % 2, 0:T - P * j], ret_k[:, n // 2, j * P:(j + 1) * P],
                                  ret_q[:, n, j * P:], start=True, stop=True).then_inc(t_full, 1)
                        fill(1)
                elif (what, kind) == ("ret", "values"):
                    o_bank()
                    wait_t_drained(pe, T_USED["ret", "scores", n])
                    offs = [0, 512, 896, 1152]
                    for i in range(TT):
                        for j in range(i + 1):
                            c = offs[j] + (i - j) * P
                            ins = pe.matmul(ps[:, O_, i * P:(i + 1) * P], inner[n % 2][:, c:c + P],
                                            ret_v[:, j, n * RET_V:(n + 1) * RET_V], start=j == 0, stop=j == i)
                    ins.then_inc(ret_full, 1)
                elif (what, kind) == ("ret", "turn"):
                    pe.wait_ge(o_drained, O_USED["ret", "values", n])
                    turn_blocks([ret_n[n % 2][:, i, :] for i in range(TT)])
                elif what == "mlp":
                    pe.wait_ge(hid_ready, 1 if kind == "k" else 2)
                    k = take_t()
                    for c in range(2):
                        ins = pe.transpose(ps[:, T_ + k % 2, c * P:c * P + BLK_N], hid[0:BLK_N, 3, c * P:(c + 1) * P],
                                           ident[0:BLK_N, 0:BLK_N])
                    ins.then_inc(t_full, 1)
                    wait_turned(k)
                    k = take_t()
                    w2 = par[:, S_W2:].rearrange("p (a c d) -> p a c d", a=2, c=2)
                    if kind == "k":
                        for c in range(2):
                            ins = pe.matmul(ps[:, T_ + k % 2, 0:BLK_N], w2[:, 0, c, :], hid_t[:, c, :], start=c == 0, stop=c == 1)
                    else:
                        for g in range(GROUPS):
                            for c in range(2):
                                ins = pe.matmul(ps[0:N_CMP, T_ + k % 2, g * P:(g + 1) * P], hid_t[:, c, g * N_CMP:(g + 1) * N_CMP],
                                                w2[:, 1, c, :], start=c == 0, stop=c == 1)
                    ins.then_inc(t_full, 1)
                elif what == "pair" and kind == "att":
                    if n == 0:
                        wait_t_drained(pe, t_uses[0])
                        pe.wait_ge(consts_ready, 2 + TT + 1 + 2)
                        pe.wait_ge(rounded_ready, 2)
                    if pair_of(n)[1] == 0:
                        pe.wait_ge(z_done, Z_INDEX["q", n // (2 * TT) * PER_GROUP + pair_of(n)[2] + 1] + 1)
                    for hh in range(2):
                        pair_half(parts_of_step(kind, n, hh), (n, hh))
                elif what == "pair":
                    for hh in range(3):
                        pair_half(parts_of_step(kind, n, hh), None)
            s0 = slabs[0]
            by_slab = MIX_TILES - LEAD
            pe.wait_ge(s_drained, s_uses[0])
            pe.wait_ge(o_drained, o_uses[0])
            for n in range(by_slab):
                pe.wait_ge(slab_lo_ready, s0 + n + 1)
                pe.wait_ge(mix_ready, n + 1)
                for t in range(TT):
                    if n == 0 and t == 2:
                        wait_pj_all_drained(pe, len(PJ_ORDER))
                    if n == 0 and t == 3:
                        wait_t_drained(pe, t_uses[0])
                    for half in range(2):
                        ins = out_products(n, t, half, s0 + n)
                ins.then_inc(slab_used, 1)
            pe.wait_ge(slab_lo_ready, s0 + MIX_TILES)
            pe.wait_ge(mix_ready, MIX_TILES)
            for t in range(TT):
                for half in range(2):
                    for n in range(by_slab, MIX_TILES):
                        ins = out_products(n, t, half, s0 + n)
                    ins.then_inc(y_full, 1)


def frequencies():
    f = np.zeros((P, 4), np.float32)
    row = np.arange(32)
    ret = RET_THETA ** (-(row % (RET_QK // 2)) / (RET_QK // 2))
    nsa = NSA_THETA ** (-(row % (ROT_DIM // 2)) / (ROT_DIM // 2))
    f[:, 0] = np.concatenate([ret, ret, nsa, nsa * np.where(row < ROT_DIM // 2, -1.0, 1.0)])
    f[:32, 1:3] = f[64:96, 1:3] = [0.25, math.pi / 2]
    return f


def column_slabs(w, starts):
    v = w.reshape(KT, P, -1)
    return np.stack([v[:, :, c:c + P].transpose(1, 0, 2).reshape(P, D) for c in starts])


def kernel(x, mem, positions, norm_pre, w_in, cmp_pos_k, cmp_w1_k, cmp_w2_k, cmp_pos_v, cmp_w1_v, cmp_w2_v,
           ret_gn, mem_norm, w_mem_kv, w_out, norm_post):
    import concourse.bacc as bacc
    from concourse.bass_utils import run_bass_kernel_spmd

    w_in, w_mem_kv, w_out = (np.asarray(a)[0] for a in (w_in, w_mem_kv, w_out))
    start = {"memq": lambda n: C_MQ + n * P, "retq": lambda n: C_RQ + n * P, "retk": lambda n: C_RK + n * P,
             "kc": lambda n: kv_col(0, 0, n), "vc": lambda n: kv_col(0, 1, n), "ks": lambda n: kv_col(1, 0, n),
             "kw": lambda n: kv_col(2, 0, n), "q": lambda n: C_Q + n * P, "gate": lambda n: C_GATE + n * P}
    w_proj = column_slabs(w_in, [start[k](n) for k, n in SLABS if k in start])
    pieces = []
    for v, c0 in enumerate((kv_col(1, 1, 0), kv_col(2, 1, 0), C_RV, C_RV + VC)):
        cols = np.r_[c0:c0 + VC, C_G + v * GC:C_G + (v + 1) * GC]
        w = w_in[:, cols].reshape(2, 4, P, VW)
        pieces += [w[f].transpose(1, 0, 2).reshape(P, SLAB) for f in range(2)]
    w_val = np.stack(pieces)
    half = MEM_HEADS * DH
    w_mem = np.concatenate([
        column_slabs(w_mem_kv, [h * DH for h in range(MEM_HEADS)]),
        w_mem_kv[:, half:].reshape(4, 2, P, half).transpose(0, 2, 1, 3).reshape(4, P, D)])
    w_cmp = np.concatenate([np.asarray(w)[0].reshape(8, W1_C, P, CMP_HIDDEN).transpose(0, 2, 1, 3).reshape(8, P, D)
                            for w in (cmp_w1_k, cmp_w1_v)])
    w_o = np.stack([w_out[t * P:(t + 1) * P] for t in OUT_ORDER])
    small = np.concatenate(
        [np.asarray(a)[0].reshape(-1, P).T for a in (norm_pre, mem_norm, ret_gn)] + [frequencies()]
        + [np.asarray(a)[0].T for a in (cmp_pos_k, cmp_pos_v)]
        + [np.asarray(a)[0].reshape(2, P, DH).transpose(1, 0, 2).reshape(P, 2 * DH) for a in (cmp_w2_k, cmp_w2_v)], axis=1)
    arrays = {"x_in": np.asarray(x)[0], "mem_in": np.asarray(mem)[0], "positions_in": np.asarray(positions)[0],
              "small_in": small, "gpost_in": np.asarray(norm_post)[0], "w_proj_in": w_proj, "w_val_in": w_val,
              "w_mem_in": w_mem, "w_cmp_in": w_cmp, "w_out_in": w_o}
    arrays = {k: np.ascontiguousarray(a) for k, a in arrays.items()}
    nc = bacc.Bacc("TRN2", target_bir_lowering=False, num_devices=1)
    args = [nc.dram_tensor(k, a.shape, mybir.dt.from_np(a.dtype), kind="ExternalInput").ap() for k, a in arrays.items()]
    out = nc.dram_tensor("y_out", (T, D), F32, kind="ExternalOutput").ap()
    build(nc, *args, out)
    r = run_bass_kernel_spmd(nc, [arrays], core_ids=[0])
    return r.results[0]["y_out"].reshape(1, T, D)
```
